# Optimizing a Trainium2 kernel written in Bass

```python
import jax, jax.numpy as jnp
from jax import lax
import numpy as np

D_MODEL = 1024
BATCH = 1
SEQ = 512
DEPTH = 1

CHUNK = 64
EPS = 1e-6
NEG_INF = -1e30

SSD_EXPAND = 2
D_SSD = SSD_EXPAND * D_MODEL
SSD_HEAD_DIM = 64
SSD_HEADS = D_SSD // SSD_HEAD_DIM
SSD_GROUPS = 4
SSD_STATE = 128
CONV_K = 4
CONV_DIM = D_SSD + 2 * SSD_GROUPS * SSD_STATE

ATTN_HEAD_DIM = 64
ATTN_HEADS = D_MODEL // ATTN_HEAD_DIM
ATTN_KV_HEADS = 4
ROPE_DIM = ATTN_HEAD_DIM // 4
ROPE_THETA = 500000.0
IDX_HEADS = 8
IDX_DIM = 64
DSA_MAX_TOPK = 256
QBLOCK = 128

IN_SIZES = (D_SSD, CONV_DIM, SSD_HEADS,
            ATTN_HEADS * ATTN_HEAD_DIM, ATTN_KV_HEADS * ATTN_HEAD_DIM, ATTN_KV_HEADS * ATTN_HEAD_DIM,
            IDX_HEADS * IDX_DIM, IDX_DIM, IDX_HEADS,
            D_MODEL, D_MODEL)
IN_DIM = sum(IN_SIZES)

PEER_HEADS = 8
PEER_TOPK = 16
N_KEYS = 128
N_EXPERTS = N_KEYS * N_KEYS
PEER_DKEY = 128
PEER_BLOCK = 128

kernel_name = "hybrid_ssd_dsa_peer_adaln_block"

def _rms(x):
    xf = x.astype(jnp.float32)
    return xf * lax.rsqrt(jnp.mean(xf * xf, axis=-1, keepdims=True) + EPS)

def rms_norm(x, g):
    return (_rms(x) * g.astype(jnp.float32)).astype(x.dtype)

def split_cols(t, sizes):
    out, start = [], 0
    for n in sizes:
        out.append(t[..., start:start + n])
        start += n
    return out

def rope_tables(positions):
    inv = ROPE_THETA ** (-jnp.arange(0, ROPE_DIM, 2, dtype=jnp.float32) / ROPE_DIM)
    ang = positions.astype(jnp.float32)[..., None] * inv
    return jnp.cos(ang), jnp.sin(ang)

def apply_rope(t, cos, sin):
    half = ROPE_DIM // 2
    tf = t[..., :ROPE_DIM].astype(jnp.float32)
    t1, t2 = tf[..., :half], tf[..., half:]
    cs, sn = cos[:, :, None, :], sin[:, :, None, :]
    rot = jnp.concatenate([t1 * cs - t2 * sn, t2 * cs + t1 * sn], axis=-1).astype(t.dtype)
    return jnp.concatenate([rot, t[..., ROPE_DIM:]], axis=-1)

def causal_dwconv(x, w, b):
    C = x.shape[-1]
    y = lax.conv_general_dilated(x, w[:, None, :], window_strides=(1,), padding=[(CONV_K - 1, 0)],
                                 dimension_numbers=("NWC", "WIO", "NWC"), feature_group_count=C)
    return y + b

def ssd_chunked(x, dt, a, bm, cm):
    Bsz, S, H, P = x.shape
    G, N = bm.shape[2], bm.shape[3]
    Hg = H // G
    nc = S // CHUNK
    xd = (x.astype(jnp.float32) * dt[..., None]).reshape(Bsz, nc, CHUNK, G, Hg, P)
    ad = (dt * a).reshape(Bsz, nc, CHUNK, G, Hg)
    a_cs = jnp.cumsum(ad, axis=2)
    bc = bm.astype(jnp.float32).reshape(Bsz, nc, CHUNK, G, N)
    cc = cm.astype(jnp.float32).reshape(Bsz, nc, CHUNK, G, N)
    seg = a_cs[:, :, :, None] - a_cs[:, :, None]
    causal = jnp.tril(jnp.ones((CHUNK, CHUNK), dtype=bool))
    lmat = jnp.exp(jnp.where(causal[:, :, None, None], seg, -jnp.inf))
    cb = jnp.einsum("bclgn,bcsgn->bclsg", cc, bc)
    y_diag = jnp.einsum("bclsg,bclsgh,bcsghp->bclghp", cb, lmat, xd)
    decay = jnp.exp(a_cs[:, :, -1:] - a_cs)
    states = jnp.einsum("bclgn,bclgh,bclghp->bcghpn", bc, decay, xd)
    chunk_decay = jnp.exp(a_cs[:, :, -1])

    def step(carry, inp):
        st, dec = inp
        return carry * dec[..., None, None] + st, carry

    init = jnp.zeros((Bsz, G, Hg, P, N), jnp.float32)
    _, prev = lax.scan(step, init, (jnp.moveaxis(states, 1, 0), jnp.moveaxis(chunk_decay, 1, 0)))
    prev = jnp.moveaxis(prev, 0, 1)
    y_off = jnp.einsum("bclgn,bcghpn,bclgh->bclghp", cc, prev, jnp.exp(a_cs))
    return (y_diag + y_off).reshape(Bsz, S, H, P).astype(x.dtype)

def dsa_attention(q, k, v, qi, ki, wi, topk):
    Bsz, S, H, dh = q.shape
    Hkv = k.shape[2]
    G = H // Hkv
    nb = S // QBLOCK
    qb = q.reshape(Bsz, nb, QBLOCK, Hkv, G, dh).transpose(1, 0, 2, 3, 4, 5)
    qib = qi.reshape(Bsz, nb, QBLOCK, IDX_HEADS, IDX_DIM).transpose(1, 0, 2, 3, 4)
    wib = wi.reshape(Bsz, nb, QBLOCK, IDX_HEADS).transpose(1, 0, 2, 3)
    kif = ki.astype(jnp.float32)
    key_chunk = jnp.arange(S) // CHUNK
    scale = ATTN_HEAD_DIM ** -0.5
    iscale = IDX_DIM ** -0.5
    wscale = IDX_HEADS ** -0.5

    def block(args):
        qq, qqi, ww, bi = args
        q_chunk = (bi * QBLOCK + jnp.arange(QBLOCK)) // CHUNK
        visible = key_chunk[None, :] <= q_chunk[:, None]
        logits = jnp.einsum("bqhd,bsd->bqhs", qqi.astype(jnp.float32), kif) * iscale
        iscore = jnp.einsum("bqhs,bqh->bqs", jax.nn.relu(logits), ww.astype(jnp.float32) * wscale)
        iscore = jnp.where(visible[None], iscore, NEG_INF)
        _, idx = lax.top_k(iscore, topk)
        valid = (idx // CHUNK) <= q_chunk[None, :, None]
        ks = jax.vmap(lambda kk, ii: kk[ii])(k, idx).astype(jnp.float32)
        vs = jax.vmap(lambda vv, ii: vv[ii])(v, idx).astype(jnp.float32)
        s = jnp.einsum("bqhgd,bqkhd->bqhgk", qq.astype(jnp.float32), ks) * scale
        s = jnp.where(valid[:, :, None, None, :], s, NEG_INF)
        p = jax.nn.softmax(s, axis=-1)
        o = jnp.einsum("bqhgk,bqkhd->bqhgd", p, vs)
        return o.reshape(Bsz, QBLOCK, H * dh).astype(q.dtype)

    out = lax.map(block, (qb, qib, wib, jnp.arange(nb)))
    return out.transpose(1, 0, 2, 3).reshape(Bsz, S, H * dh)

def token_mixer(h, cos, sin, w_in, conv_w, conv_b, dt_bias, a_log, d_skip, g_ssd,
                q_g, k_g, w_ssd_br, w_attn_br, w_out):
    Bsz, S, _ = h.shape
    proj = h @ w_in
    z, xbc, dt_raw, q, k, v, qi, ki, wi, gate_s, gate_a = split_cols(proj, IN_SIZES)
    xbc = jax.nn.silu(causal_dwconv(xbc, conv_w, conv_b))
    xs, bm, cm = split_cols(xbc, (D_SSD, SSD_GROUPS * SSD_STATE, SSD_GROUPS * SSD_STATE))
    xs = xs.reshape(Bsz, S, SSD_HEADS, SSD_HEAD_DIM)
    bm = bm.reshape(Bsz, S, SSD_GROUPS, SSD_STATE)
    cm = cm.reshape(Bsz, S, SSD_GROUPS, SSD_STATE)
    dt = jax.nn.softplus(dt_raw.astype(jnp.float32) + dt_bias.astype(jnp.float32))
    a = -jnp.exp(a_log.astype(jnp.float32))
    y = ssd_chunked(xs, dt, a, bm, cm) + d_skip[:, None] * xs
    y = y.reshape(Bsz, S, D_SSD) * jax.nn.silu(z)
    y = (_rms(y.reshape(Bsz, S, SSD_GROUPS, D_SSD // SSD_GROUPS)).reshape(Bsz, S, D_SSD)
         * g_ssd.astype(jnp.float32)).astype(h.dtype)
    ssd_out = y @ w_ssd_br
    q = apply_rope(rms_norm(q.reshape(Bsz, S, ATTN_HEADS, ATTN_HEAD_DIM), q_g), cos, sin)
    k = apply_rope(rms_norm(k.reshape(Bsz, S, ATTN_KV_HEADS, ATTN_HEAD_DIM), k_g), cos, sin)
    v = v.reshape(Bsz, S, ATTN_KV_HEADS, ATTN_HEAD_DIM)
    qi = apply_rope(qi.reshape(Bsz, S, IDX_HEADS, IDX_DIM), cos, sin)
    ki = apply_rope(ki[:, :, None, :], cos, sin)[:, :, 0, :]
    topk = min(DSA_MAX_TOPK, S // 4)
    attn = dsa_attention(q, k, v, qi, ki, wi, topk)
    attn_out = attn @ w_attn_br
    merged = jax.nn.sigmoid(gate_s) * ssd_out + jax.nn.sigmoid(gate_a) * attn_out
    return merged @ w_out

def peer_ffn(h, w_q, subkeys, u, v):
    Bsz, S, D = h.shape
    T = Bsz * S
    ht = h.reshape(T, D)
    q = (ht @ w_q).astype(jnp.float32).reshape(T, PEER_HEADS, PEER_DKEY)
    half = PEER_DKEY // 2
    sk = subkeys.astype(jnp.float32)
    s1 = jnp.einsum("thd,hnd->thn", q[..., :half], sk[:, 0])
    s2 = jnp.einsum("thd,hnd->thn", q[..., half:], sk[:, 1])
    v1, i1 = lax.top_k(s1, PEER_TOPK)
    v2, i2 = lax.top_k(s2, PEER_TOPK)
    cand = (v1[..., :, None] + v2[..., None, :]).reshape(T, PEER_HEADS, PEER_TOPK * PEER_TOPK)
    sc, ci = lax.top_k(cand, PEER_TOPK)
    e = (jnp.take_along_axis(i1, ci // PEER_TOPK, axis=-1) * N_KEYS
         + jnp.take_along_axis(i2, ci % PEER_TOPK, axis=-1))
    g = jax.nn.softmax(sc, axis=-1).astype(h.dtype)
    nb = T // PEER_BLOCK

    def blk(args):
        hh, ee, gg = args
        act = jax.nn.gelu(jnp.einsum("thkd,td->thk", u[ee], hh), approximate=False)
        return jnp.einsum("thk,thkd->td", gg * act, v[ee])

    out = lax.map(blk, (ht.reshape(nb, PEER_BLOCK, D),
                        e.reshape(nb, PEER_BLOCK, PEER_HEADS, PEER_TOPK),
                        g.reshape(nb, PEER_BLOCK, PEER_HEADS, PEER_TOPK)))
    return out.reshape(Bsz, S, D)

def setup_inputs(seed: int = 0) -> dict:
    key = jax.random.key(seed)
    ks = jax.random.split(key, 26)
    f32 = jnp.float32
    nrm = lambda k, shape, s: jax.random.normal(k, shape, f32) * s
    x = jax.random.normal(ks[0], (BATCH, SEQ, D_MODEL), f32)
    c = jax.random.normal(ks[1], (BATCH, D_MODEL), f32)
    offsets = jax.random.randint(ks[2], (BATCH,), 0, 64, dtype=jnp.int32) * CHUNK
    positions = offsets[:, None] + jnp.arange(SEQ, dtype=jnp.int32)[None, :]
    dt0 = jnp.exp(jax.random.uniform(ks[9], (DEPTH, SSD_HEADS), f32, jnp.log(1e-3), jnp.log(1e-1)))
    return {
        "x": x,
        "c": c,
        "positions": positions,
        "w_ada": nrm(ks[3], (DEPTH, D_MODEL, 6 * D_MODEL), 0.5 * D_MODEL ** -0.5),
        "b_ada": nrm(ks[4], (DEPTH, 6 * D_MODEL), 0.01),
        "g_norm1": 1.0 + nrm(ks[5], (DEPTH, D_MODEL), 0.02),
        "g_norm2": 1.0 + nrm(ks[6], (DEPTH, D_MODEL), 0.02),
        "w_in": nrm(ks[7], (DEPTH, D_MODEL, IN_DIM), D_MODEL ** -0.5),
        "conv_w": nrm(ks[8], (DEPTH, CONV_K, CONV_DIM), CONV_K ** -0.5),
        "conv_b": nrm(ks[10], (DEPTH, CONV_DIM), 0.01),
        "dt_bias": dt0 + jnp.log(-jnp.expm1(-dt0)),
        "a_log": jnp.log(jax.random.uniform(ks[11], (DEPTH, SSD_HEADS), f32, 1.0, 16.0)),
        "d_skip": 1.0 + nrm(ks[12], (DEPTH, SSD_HEADS), 0.1),
        "g_ssd": 1.0 + nrm(ks[13], (DEPTH, D_SSD), 0.02),
        "q_norm_g": 1.0 + nrm(ks[14], (DEPTH, ATTN_HEAD_DIM), 0.02),
        "k_norm_g": 1.0 + nrm(ks[15], (DEPTH, ATTN_HEAD_DIM), 0.02),
        "w_ssd_br": nrm(ks[16], (DEPTH, D_SSD, D_MODEL), D_SSD ** -0.5),
        "w_attn_br": nrm(ks[17], (DEPTH, ATTN_HEADS * ATTN_HEAD_DIM, D_MODEL), (ATTN_HEADS * ATTN_HEAD_DIM) ** -0.5),
        "w_out": nrm(ks[18], (DEPTH, D_MODEL, D_MODEL), D_MODEL ** -0.5),
        "w_peer_q": nrm(ks[19], (DEPTH, D_MODEL, PEER_HEADS * PEER_DKEY), D_MODEL ** -0.5),
        "peer_subkeys": nrm(ks[20], (DEPTH, PEER_HEADS, 2, N_KEYS, PEER_DKEY // 2), (PEER_DKEY // 2) ** -0.5),
        "peer_u": nrm(ks[21], (DEPTH, N_EXPERTS, D_MODEL), D_MODEL ** -0.5),
        "peer_v": nrm(ks[22], (DEPTH, N_EXPERTS, D_MODEL), 0.25),
    }

def reference(x, c, positions, w_ada, b_ada, g_norm1, g_norm2, w_in, conv_w, conv_b, dt_bias,
              a_log, d_skip, g_ssd, q_norm_g, k_norm_g, w_ssd_br, w_attn_br, w_out,
              w_peer_q, peer_subkeys, peer_u, peer_v):
    cos, sin = rope_tables(positions)
    cond = jax.nn.silu(c)
    for l in range(DEPTH):
        mod = cond @ w_ada[l] + b_ada[l]
        sh1, sc1, gt1, sh2, sc2, gt2 = [m[:, None, :] for m in jnp.split(mod, 6, axis=-1)]
        h = rms_norm(x, g_norm1[l]) * (1.0 + sc1) + sh1
        x = x + gt1 * token_mixer(h, cos, sin, w_in[l], conv_w[l], conv_b[l], dt_bias[l], a_log[l],
                                  d_skip[l], g_ssd[l], q_norm_g[l], k_norm_g[l], w_ssd_br[l],
                                  w_attn_br[l], w_out[l])
        h = rms_norm(x, g_norm2[l]) * (1.0 + sc2) + sh2
        x = x + gt2 * peer_ffn(h, w_peer_q[l], peer_subkeys[l], peer_u[l], peer_v[l])
    return x


_drawn_inputs = setup_inputs


def setup_inputs(seed=0):
    import zlib

    import numpy as np

    out = dict(_drawn_inputs(seed))
    spreads = {}
    factors = {'b_ada': 6.078,
     'g_norm1': 8.0,
     'g_norm2': 26.18,
     'conv_b': 39.641,
     'd_skip': 200.0,
     'g_ssd': 21.61,
     'q_norm_g': 8.0,
     'k_norm_g': 8.0}
    for name, (base, spread) in spreads.items():
        noise = np.random.default_rng([zlib.crc32(name.encode()), seed]).standard_normal(out[name].shape)
        drawn = base * np.exp(spread * noise) if base else spread * noise
        out[name] = __import__('jax').numpy.asarray(drawn.astype(out[name].dtype))
    for name, factor in factors.items():
        out[name] = (out[name] * factor).astype(out[name].dtype)
    return out
```

```python
from contextlib import ExitStack

import numpy as np

import concourse.bass as bass
from concourse import mybir

P = 128
T, D = 512, 1024
NT, NK = T // P, D // P
CHUNK = 64
EPS = 1e-6
NEG = -1e30
SSD_H, SSD_P, SSD_G, SSD_N = 32, 64, 4, 128
D_SSD = SSD_H * SSD_P
NY = D_SSD // P
NX = (D_SSD + 2 * SSD_G * SSD_N) // P
CONV_K = 4
AH, KVH, DH = 16, 4, 64
IH = 8
TOPK = 128
ROT = 8
ROPE_THETA = 500000.0
PH, PK, NKEYS = 8, 16, 128
C_Z, C_XBC, C_DT = 0, 2048, 5120
C_Q, C_K, C_QI, C_KI, C_G = 5152, 6176, 6688, 7200, 7272
NSMALL = SSD_H + 64 + IH
CW = 512
GT = 8
NG = NKEYS // GT
TC = 32
NTC = T // TC
TWO_PI = 2 * np.pi
C1 = 6.28125
C2 = float(np.float32(int((TWO_PI - C1) * 2 ** 21) / 2 ** 21))
C3 = float(np.float32(TWO_PI - C1 - C2))
MAGIC = 12582912.0
PI_F = 3.1415925


class Steps:

    def __init__(self, eng, sem):
        self.eng, self.sem, self.n, self.off = eng, sem, 0, 0

    def __call__(self, ins):
        ins.then_inc(self.sem, 1)
        self.n += 1
        return ins

    def wait(self):
        self.eng.wait_ge(self.sem, self.n + self.off)

    def enter(self, i, per):
        self.start, self.per, self.off = self.n, per, i * per

    def leave(self, count):
        assert self.n - self.start == self.per, (self.n - self.start, self.per)
        self.n, self.off = self.start + self.per * count, 0


class Section:

    def __init__(self, before, blocks, units):
        self.blocks, self.units = blocks, units
        self.u0 = before.u1 if before else 0
        self.b0 = before.b1 if before else 0
        self.p0 = before.p1 if before else 0
        self.u1 = self.u0 + blocks * units
        self.b1 = self.b0 + blocks
        self.p1 = self.p0 + blocks * (units - 1)


def sections():
    small = Section(None, 1, 4)
    qi = Section(small, 1, 4)
    kv = Section(qi, 1, 4)
    q = Section(kv, 2, 4)
    xbc = Section(q, 6, 4)
    z = Section(xbc, 4, 4)
    gates = Section(z, 4, 4)
    br_s = Section(gates, 2, 8)
    br_a = Section(br_s, 2, 4)
    out = Section(br_a, 2, 4)
    pq = Section(out, 2, 4)
    return small, qi, kv, q, xbc, z, gates, br_s, br_a, out, pq


def build(nc, A, stop=99):
    F, R, U32, I32 = mybir.dt.float32, mybir.dt.float32r, mybir.dt.uint32, mybir.dt.int32
    ALU, ACT, AX = mybir.AluOpType, mybir.ActivationFunctionType, mybir.AxisListType
    SMALL, QI, KV, Q, XBC, Z, GATES, BR_S, BR_A, OUT, PQ = sections()
    PU0 = PQ.u1
    BASE = 16512
    KB = 1024

    def at(name, shape, dt, kb):
        return nc.alloc_sbuf_tensor_at(name, shape, dt, offset=BASE + int(kb * KB))

    xT = at("xT", [P, NK, T], F, 0)
    hTh = at("hTh", [P, NK, T], R, 16)
    hTl = at("hTl", [P, NK, T], R, 32)
    raw = at("raw", [P, 4, 1024], F, 48)
    whi = at("whi", [P, 2, 1024], R, 64)
    wlo = at("wlo", [P, 2, 1024], R, 72)
    cpos = [80 * KB]

    def const(name, shape, dt=F):
        n = 4 * int(np.prod(shape[1:]))
        t = nc.alloc_sbuf_tensor_at(name, shape, dt, offset=BASE + cpos[0])
        cpos[0] += (n + 31) // 32 * 32
        assert cpos[0] <= 88 * KB, name
        return t

    ident = const("ident", [P, P])
    ones = const("ones", [P, P])
    tri = const("tri", [P, P])
    iota = const("iota", [P, P])
    iota16 = const("iota16", [P, PK])
    mod = const("mod", [P, 48])
    cT = const("cT", [P, NK])
    bada = const("bada", [P, 48])
    g1 = const("g1", [P, NK])
    g2 = const("g2", [P, NK])
    a1 = const("a1", [P, NK])
    a2 = const("a2", [P, NK])
    convw = const("convw", [P, NX, CONV_K])
    convb = const("convb", [P, NX])
    gssd = const("gssd", [P, NY])
    dtb = const("dtb", [P, SSD_H])
    alog = const("alog", [P, SSD_H])
    dskip = const("dskip", [P, SSD_H])
    qg = const("qg", [P, DH])
    kg = const("kg", [P, DH])
    posi = const("posi", [P, NT], I32)
    posf = const("posf", [P, NT])
    cosT = const("cosT", [P, NT, ROT])
    sinT = const("sinT", [P, NT, ROT])
    dt = const("dt", [P, NT, SSD_H])
    acs = const("acs", [P, NT, SSD_H])
    eacs = const("eacs", [P, NT, SSD_H])
    wi = const("wi", [P, NT, IH])

    R0 = 88
    ada = at("ada", [P, 6 * D], F, R0)
    adar = at("adar", [P, 4, 2048], F, R0 + 24)
    sq = at("sq", [P, NK, T], F, R0 + 56)
    hf = at("hf", [P, NK, T], F, R0 + 72)
    rms = at("rms", [P, 2, T], F, R0 + 88)
    adat = at("adat", [P, 2048], F, R0 + 92)
    xbc = at("xbc", [P, NX, T], F, R0)
    qk = at("qk", [P, NT, 1280], F, R0 + 48)
    qit = at("qit", [P, NT, 576], F, R0 + 68)
    vt = at("vt", [P, NT, 256], F, R0 + 77)
    craw = at("craw", [P, 4, T], F, R0 + 81)
    cacc = at("cacc", [P, 4, T], F, R0 + 89)
    stg = at("stg", [P, 2, 4, CW], F, R0 + 97)
    qT = at("qT", [P, 8, T], F, 16)
    kT = at("kT", [P, 4, T], F, 32)
    qiT = at("qiT", [P, 4, T], F, 40)
    kdup = at("kdup", [P, NT, KVH, 2, DH], F, R0 + 81)
    kidup = at("kidup", [P, NT, 2, DH], F, R0 + 89)
    kiT = at("kiT", [P, T], F, R0 + 91)
    prep = at("prep", [P, NT, 1280], F, R0 + 93)
    score = at("score", [P, T], F, R0 + 93)
    work = at("work", [P, T], F, R0 + 95)
    mb = at("mb", [P, 4, T], F, R0 + 97)
    rl = at("rl", [P, 4, T], F, R0 + 105)
    pm = at("pm", [P, 2, T], F, R0 + 113)
    pe_ = at("pexp", [P, 2, T], F, R0 + 81)
    pts = at("pts", [P, 2, T], F, R0 + 85)
    otok = at("otok", [P, AH * DH], F, R0 + 64)
    zer = at("zer", [P, T], F, R0 + 68)
    eqm = at("eqm", [P, T], F, R0 + 70)
    cum = at("cum", [P, T], F, R0 + 72)
    selm = at("selm", [P, T], F, R0 + 74)
    asm = at("asm", [P, 3, AH], F, R0 + 89)
    tk8 = at("tk8", [P, 16], F, R0 + 90)
    attnT = at("attnT", [P, NK, T], F, R0 + 48)
    st = at("st", [P, D_SSD], F, 16)
    seg = at("seg", [P, SSD_H, P], F, 24)
    zc = at("zc", [P, D_SSD], F, 40)
    cbm = at("cbm", [P, SSD_G, P], F, R0 + 64)
    btok = at("btok", [P, SSD_G, P], F, R0 + 66)
    ytmp = at("ytmp", [P, T], F, R0 + 68)
    xd = at("xd", [P, D_SSD], F, R0 + 72)
    xsk = at("xsk", [P, D_SSD], F, R0 + 80)
    xdd = at("xdd", [P, D_SSD], F, R0 + 88)
    yt = at("yt", [P, D_SSD], F, R0 + 96)
    ysq = at("ysq", [P, T], F, R0 + 104)
    ssm = at("ssm", [P, 6, SSD_H], F, R0 + 106)
    acsT = at("acsT", [SSD_H, T], F, R0 + 108)
    yh = at("yh", [P, NY, T], R, 16)
    yl = at("yl", [P, NY, T], R, R0 + 64)
    ah = at("ah", [P, NK, T], R, R0)
    al = at("al", [P, NK, T], R, R0 + 16)
    mg = at("mg", [P, NK, T], F, R0 + 32)
    mh = at("mh", [P, NK, T], R, R0 + 96)
    ml = at("ml", [P, NK, T], R, R0 + 48)
    gring = at("gring", [P, 2, T], F, R0 + 112)
    mtmp = at("mtmp", [P, T], F, R0 + 116)
    sq2 = at("sq2", [P, NK, T], F, R0)
    hf2 = at("hf2", [P, NK, T], F, R0 + 16)
    rms2 = at("rms2", [P, 2, T], F, R0 + 64)
    pqT = at("pqT", [P, PH, T], F, R0 + 32)
    skbd = at("skbd", [P, PH, 2, NKEYS], F, R0)
    sc = at("sc", [P, PH, 2, NKEYS], F, R0 + 8)
    cand = at("cand", [P, PH, PK, PK], F, R0 + 16)
    eqa = at("eqa", [P, PH, PK, PK], F, R0 + 24)
    v8 = at("v8", [P, PH, 2, PK], F, R0 + 48)
    i8 = at("i8", [P, PH, 2, PK], U32, R0 + 49)
    if8 = at("if8", [P, PH, 2, PK], F, R0 + 50)
    sv = at("sv", [P, PH, PK], F, R0 + 51)
    ci = at("ci", [P, PH, PK], U32, R0 + 51.5)
    cab = at("cab", [P, 2, PH, PK], U32, R0 + 52)
    cabf = at("cabf", [P, 2, PH, PK], F, R0 + 53)
    sel = at("sel", [P, 3, PH * PK], F, R0 + 54)
    gsm = at("gsm", [P, 2, PH], F, R0 + 55.5)
    selT = at("selT", [P, 3, T], F, R0 + 56)
    oh1 = at("oh1", [P, 8, P], F, R0 + 62)
    oh2 = at("oh2", [P, 8, P], F, R0 + 66)
    gst = at("gst", [P, 2, NKEYS, TC], F, R0 + 76)
    acc = at("acc", [P, NK, T], F, R0)
    ach = at("ach", [P, GT, T], R, R0 + 16)
    acl = at("acl", [P, GT, T], R, R0 + 32)
    gel = at("gel", [P, 2, T], F, R0 + 48)
    gac = at("gac", [P, 2, T], F, R0 + 52)
    gg = at("gg", [P, NTC, GT, TC], F, R0 + 60)

    z_d = nc.dram_tensor("z_scratch", (NT, P, D_SSD), F, kind="Internal").ap()
    g_d = nc.dram_tensor("gates_scratch", (16, P, T), F, kind="Internal").ap()
    acs_d = nc.dram_tensor("acs_scratch", (SSD_H, T), F, kind="Internal").ap()
    w_d = nc.dram_tensor("expert_gates_scratch", (NTC, P, NKEYS * TC), F, kind="Internal").ap()

    ctx = ExitStack()
    with ctx:
        bank = [ctx.enter_context(nc.psum_tensor(f"bank{i}", [P, 512], F)) for i in range(8)]

        def sem(name):
            return ctx.enter_context(nc.semaphore(name))

        raw_full = [sem(f"raw_full{i}") for i in range(4)]
        consts_in = sem("consts_in")
        x_in = sem("x_in")
        ada_in = [sem(f"ada_in{i}") for i in range(4)]
        hi_done, lo_done, unit_used = sem("hi_done"), sem("lo_done"), sem("unit_used")
        acc_done, acc_free = sem("acc_done"), sem("acc_free")
        act_step, dve_step, pool_step, pe_step = sem("act_step"), sem("dve_step"), sem("pool_step"), sem("pe_step")
        consts_made = sem("consts_made")
        cond_done, ada_v_used, ada_p_used = sem("cond_done"), sem("ada_v_used"), sem("ada_p_used")
        ada_ready, mod_done, mod_out = sem("ada_ready"), sem("mod_done"), sem("mod_out")
        sq_done, ssq_done, ms_done, rt_done = sem("sq_done"), sem("ssq_done"), sem("ms_done"), sem("rt_done")
        h_made, h_hi, h_ready = sem("h_made"), sem("h_hi"), sem("h_ready")
        craw_full, conv_done, silu_done = sem("craw_full"), sem("conv_done"), sem("silu_done")
        stg_full, stg_out = sem("stg_full"), [sem(f"stg_out{k}") for k in range(2)]
        tok_done = sem("tok_done")

        rope_arg, rope_done, qk_ms = sem("rope_arg"), sem("rope_done"), sem("qk_ms")
        qk_rt, prep_done, tp_done = sem("qk_rt"), sem("prep_done"), sem("tp_done")
        tp_free, ix_done, rl_full = sem("tp_free"), sem("ix_done"), sem("rl_full")
        rl_used, s_done, neg_max = sem("rl_used"), sem("s_done"), sem("neg_max")
        exp_done, pt_done, pt_evac = sem("exp_done"), sem("pt_done"), sem("pt_evac")
        pv_done, o_ready, ot_done = sem("pv_done"), sem("o_ready"), sem("ot_done")
        attn_ready, dt_in, sp_exp = sem("attn_ready"), sem("dt_in"), sem("sp_exp")
        sp_ln, sp_relu, ad_done = sem("sp_ln"), sem("sp_relu"), sem("ad_done")
        acs_done, acs_cp, acsT_tp = sem("acs_done"), sem("acs_cp"), sem("acsT_tp")
        acsT_ready, acsd_out, seg_in = sem("acsT_ready"), sem("acsd_out"), sem("seg_in")
        z_in, xp_done, b_done = sem("z_in"), sem("xp_done"), sem("b_done")
        b_copied, cb_done, alast_done = sem("b_copied"), sem("cb_done"), sem("alast_done")
        decay_done, segmin_done, segexp_done = sem("decay_done"), sem("segmin_done"), sem("segexp_done")
        m_ready, yo_done, y_used = sem("m_ready"), sem("yo_done"), sem("y_used")
        st_mm, st_used, ysq_done = sem("st_mm"), sem("st_used"), sem("ysq_done")
        yrt_done, yn_done, yt_done = sem("yrt_done"), sem("yn_done"), sem("yt_done")
        y_done, y_hi, y_split = sem("y_done"), sem("y_hi"), sem("y_split")
        a_split_hi, a_split, gate_used = sem("a_split_hi"), sem("a_split"), sem("gate_used")
        mg_done, m_hi, m_split = sem("mg_done"), sem("m_hi"), sem("m_split")
        x1_done, sk_in, sc_done = sem("x1_done"), sem("sk_in"), sem("sc_done")
        sc_full, pk_done, sub_done = sem("sc_full"), sem("pk_done"), sem("sub_done")
        gexp_done, sel_ready, selT_tp = sem("gexp_done"), sem("sel_ready"), sem("selT_tp")
        selT_done, oh_made, w_done = sem("selT_done"), sem("oh_made"), sem("w_done")
        w_evac, up_done, gelu_done = sem("w_evac"), sem("up_done"), sem("gelu_done")
        gated, act_hi, act_ready = sem("gated"), sem("act_hi"), sem("act_ready")
        down_done, added, gg_in = sem("down_done"), sem("added"), sem("gg_in")
        out_made, out_done = sem("out_made"), sem("out_done")
        gate_in = [sem(f"gate_in{k}") for k in range(2)]
        w_out = [sem(f"w_out{k}") for k in range(2)]
        block = ctx.enter_context(nc.Block())

        def last_unit_waits(eng, s, b, j):
            if j == 1:
                if not (isinstance(b, int) and s.b0 + b == 0):
                    eng.wait_ge(acc_done, 4 * s.b0 + b * 4)
            else:
                n = s.p0 + b * (s.units - 1) + max(j - 1, 0)
                if not (isinstance(n, int) and n == 0):
                    eng.wait_ge(unit_used, n)

        def src_n(src):
            return int(np.prod(src.shape[1:]))

        def first_units(sp):
            sp.dma_start(raw[:, 0, 0:2 * NSMALL].rearrange("p (a c) -> p a c", a=2),
                         A["w_small"][0:256, :].rearrange("(a p) c -> p a c", a=2)).then_inc(raw_full[0], 16)

        def expert_free(eng, g, n):
            if n in (0, 1):
                if isinstance(g, int) and g == 0:
                    if n == 0:
                        eng.wait_ge(unit_used, PQ.p1)
                    else:
                        eng.wait_ge(acc_done, 4 * PQ.b1)
                else:
                    eng.wait_ge(down_done, g * GT + (n - 1))
            elif n < GT + 2:
                eng.wait_ge(up_done, g * GT + (n - 1))
            else:
                eng.wait_ge(down_done, g * GT + (n - GT - 1))

        BR_S_free0 = BR_S.b0 - Z.blocks - GATES.blocks

        h_pair = (hTh, hTl)

        def out_t(pe, i):
            pe.wait_ge(o_ready, 2 * i + 2)
            for b in range(2):
                if i:
                    pe.wait_ge(attn_ready, 2 * i)
                for f in range(4):
                    ins = pe.transpose(bank[1 + b][:, f * P:(f + 1) * P], otok[:, (4 * b + f) * P:(4 * b + f + 1) * P], ident[:])
                ins.then_inc(ot_done, 1)

        def picks_t(pe, i):
            pe.wait_ge(sel_ready, i + 1)
            if i:
                pe.wait_ge(selT_done, i)
            for e in range(3):
                ins = pe.transpose(bank[4][:, e * P:(e + 1) * P], sel[:, e], ident[:])
            ins.then_inc(selT_tp, 1)

        @block.sync
        def _(sp):
            sp.dma_start(cT[:], A["cT"]).then_inc(consts_in, 16)
            for t, n in ((bada, "b_ada"), (g1, "g1"), (g2, "g2"), (convb, "conv_b"), (gssd, "g_ssd"), (posi, "pos")):
                sp.dma_start(t[:], A[n]).then_inc(consts_in, 16)
            sp.dma_start(convw[:], A["conv_w"].rearrange("p (m k) -> p m k", k=CONV_K)).then_inc(consts_in, 16)
            for t, n in ((dtb, "dt_bias"), (alog, "a_log"), (dskip, "d_skip"), (qg, "q_g"), (kg, "k_g")):
                sp.dma_start(t[:], A[n].partition_broadcast(P)).then_inc(consts_in, 16)
            wa = A["w_ada"].rearrange("(k p) n -> k p n", p=P)
            for k in range(NK):
                if k >= 2:
                    sp.wait_ge(ada_v_used, k - 1)
                sp.dma_start(adar[:, k % 2], wa[k, :, 0:2048]).then_inc(ada_in[k % 2], 16)
                if k == 1:
                    sp.dma_start(xT[:], A["xT"].rearrange("(k p) t -> p k t", p=P)).then_inc(x_in, 16)
            for n in range(2 * NK):
                k, c = n // 2, n % 2
                if n >= 2:
                    sp.wait_ge(ada_p_used, n - 1)
                sp.dma_start(adar[:, 2 + c], wa[k, :, 2048 * (c + 1):2048 * (c + 2)]).then_inc(ada_in[2 + c], 16)
                if n == 1:
                    first_units(sp)

            def load(src, s, b, j):
                u = s.u0 + j + b * s.units
                if not (isinstance(u, int) and u < 4):
                    sp.wait_ge(lo_done, u - 3)
                sp.dma_start(raw[:, j % 4, 0:src_n(src)]
                             .rearrange("p (a c) -> p a c", a=2), src).then_inc(raw_full[j % 4], 16)

            def unit_src(w, c0, n, j):
                return w[256 * j:256 * j + 256, c0:c0 + n].rearrange("(a p) c -> p a c", a=2)

            w_in = A["w_in"]
            for j in range(1, 4):
                load(unit_src(A["w_small"], 0, NSMALL, j), SMALL, 0, j)
            for s, c0 in ((QI, C_QI), (KV, C_K)):
                for j in range(4):
                    load(unit_src(w_in, c0, CW, j), s, 0, j)
            for s, c0 in ((Q, C_Q), (XBC, C_XBC), (Z, C_Z), (GATES, C_G)):
                cols = w_in[:, c0:c0 + CW * s.blocks].rearrange("(j a p) (b c) -> j p a b c", a=2, p=P, c=CW)
                with sp.Fori(0, s.blocks) as b:
                    for j in range(4):
                        load(cols[j][:, :, bass.ds(b, 1), :].rearrange("p a o c -> p a (o c)"), s, b, j)
            if stop <= 3:
                return
            for s, n in ((BR_S, "w_ssd_br"), (BR_A, "w_attn_br"), (OUT, "w_out"), (PQ, "w_peer_q")):
                cols = A[n].rearrange("(j a p) (b c) -> j p a b c", a=2, p=P, c=CW)
                with sp.Fori(0, s.blocks) as b:
                    for j in range(s.units):
                        load(cols[j][:, :, bass.ds(b, 1), :].rearrange("p a o c -> p a (o c)"), s, b, j)
            if stop <= 4:
                return
            with sp.Fori(0, NG) as g:
                for n, src in enumerate((A["U"], A["V"])):
                    for j in range(GT):
                        sp.wait_ge(lo_done, PU0 + 2 * GT * g + GT * n + j - 3)
                        sp.dma_start(raw[:, j % 4, :],
                                     src[bass.ds(g * GT + j, 1)].rearrange("o p n -> p (o n)")).then_inc(raw_full[j % 4], 16)
            for m in range(NK):
                sp.wait_ge(out_made, m + 1)
                sp.dma_start(A["out"][m * P:(m + 1) * P, :], xT[:, m, :]).then_inc(out_done, 16)
            sp.wait_ge(out_done, 16 * NK)

        @block.gpsimd
        def _(pool):
            step = Steps(pool, pool_step)
            pool.memset(ident[:], 0.0).then_inc(pool_step, 1)
            step.n += 1
            step(pool.memset(ones[:], 1.0))
            step(pool.memset(tri[:], 1.0))
            step.wait()
            step(pool.affine_select(out=ident[:], in_=ident[:], compare_op=ALU.not_equal, fill=1.0,
                                    base=0, pattern=[[-1, P]], channel_multiplier=1))
            step(pool.affine_select(out=tri[:], in_=tri[:], compare_op=ALU.is_ge, fill=0.0,
                                    base=0, pattern=[[1, P]], channel_multiplier=-1))
            step(pool.iota(iota[:], [[1, P]], base=0, channel_multiplier=0, allow_small_or_imprecise_dtypes=True))
            step(pool.iota(iota16[:], [[1, PK]], base=0, channel_multiplier=0, allow_small_or_imprecise_dtypes=True))
            step.wait()
            pool.sem_inc(consts_made, 1)
            pool.wait_ge(cond_done, 1)
            for n in range(2 * NK):
                k, c = n // 2, n % 2
                dst = ada[:, 2048 * (c + 1):2048 * (c + 2)]
                pool.wait_ge(ada_in[2 + c], 16 * (k + 1))
                if k == 0:
                    step(pool.tensor_scalar(dst, adar[:, 2 + c], cT[:, k:k + 1], 0.0, ALU.mult, ALU.add))
                    step.wait()
                    pool.sem_inc(ada_p_used, 1)
                else:
                    if n > 2:
                        step.wait()
                    step(pool.tensor_scalar(adat[:], adar[:, 2 + c], cT[:, k:k + 1], 0.0, ALU.mult, ALU.add))
                    step.wait()
                    pool.sem_inc(ada_p_used, 1)
                    step(pool.tensor_tensor(dst, dst, adat[:], ALU.add))
            step.wait()
            pool.sem_inc(ada_ready, 1)
            zv = z_d.rearrange("t p (b c) -> p t b c", c=CW)
            gv = g_d.rearrange("(b m) p t -> b p m t", m=4)
            for n in range(8):
                pool.wait_ge(stg_full, 4 * n + 4)
                pool.dma_start(zv[:, :, n, :] if n < 4 else gv[n - 4], stg[:, n % 2]).then_inc(stg_out[n % 2], 16)
            for k in range(2):
                pool.wait_ge(stg_out[k], 16 * 4)
            if stop <= 1:
                return
            pool.wait_ge(acsT_ready, 1)
            pool.dma_start(acs_d, acsT[:]).then_inc(acsd_out, 16)
            pool.wait_ge(acsd_out, 16)
            if stop <= 2:
                return
            pool.wait_ge(attn_ready, 2 * NT)
            for i in range(NT):
                if i:
                    pool.wait_ge(y_done, 8 * i)
                pool.dma_start(seg[:], acs_d[:, i * P:(i + 1) * P].partition_broadcast(P)).then_inc(seg_in, 16)
                pool.dma_start(zc[:], z_d[i]).then_inc(z_in, 16)
            if stop <= 3:
                return
            for n in range(16):
                if n >= 2:
                    pool.wait_ge(gate_used, n - 1)
                else:
                    pool.wait_ge(y_done, 8 * NT)
                pool.dma_start(gring[:, n % 2], g_d[n]).then_inc(gate_in[n % 2], 16)
            if stop <= 4:
                return
            pool.wait_ge(h_ready, 2 * NK)
            step(pool.memset(skbd[:], 0.0))
            step.wait()
            skv = A["subkeys"].rearrange("p (h n) -> p h n", n=NKEYS)
            for half in range(2):
                pool.dma_start(skbd[64 * half:64 * half + 64, :, half, :],
                               skv[64 * half:64 * half + 64]).then_inc(sk_in, 16)
            with pool.Fori(0, NTC // 2) as c:
                for k in range(2):
                    pool.wait_ge(w_evac, 16 * c + 8 * k + 8)
                    pool.dma_start(w_d[bass.ds(c * 2 + k, 1)].rearrange("o p n -> p (o n)"),
                                   gst[:, k].rearrange("p e t -> p (e t)")).then_inc(w_out[k], 16)
            for k in range(2):
                pool.wait_ge(w_out[k], 16 * NTC // 2)
            wv = w_d.rearrange("c p (g n) -> p c g n", n=GT * TC)
            pool.dma_start(gg[:].rearrange("p c e t -> p c (e t)"), wv[:, :, 0, :]).then_inc(gg_in, 16)
            with pool.Fori(1, NG) as g:
                pool.wait_ge(gated, GT * g)
                pool.dma_start(gg[:].rearrange("p c e t -> p c (e t)"),
                               wv[:, :, bass.ds(g, 1), :].rearrange("p c o n -> p c (o n)")).then_inc(gg_in, 16)
            pool.wait_ge(gg_in, 16 * NG)

        @block.scalar
        def _(act):
            step = Steps(act, act_step)

            def hi(s, b, j):
                u = s.u0 + j + b * s.units
                act.wait_ge(raw_full[j % 4], 16 * (s.u0 // 4 + j // 4 + 1) + b * (4 * s.units))
                last_unit_waits(act, s, b, j)
                n = 2 * NSMALL if s is SMALL else 1024
                act.activation(whi[:, j % 2, 0:n], raw[:, j % 4, 0:n], ACT.Copy).then_inc(hi_done, 1)

            def hi_next(s, b, nxt, is_last):
                if is_last:
                    if nxt is not None:
                        hi(nxt, 0, 0)
                else:
                    hi(s, b + 1, 0)

            act.wait_ge(consts_in, 16 * 13)
            step(act.activation(cT[:], cT[:], ACT.Silu))
            step.wait()
            act.sem_inc(cond_done, 1)
            act.wait_ge(x_in, 16)
            for k in range(NK):
                act.activation(sq[:, k], xT[:, k], ACT.Square).then_inc(sq_done, 1)
            act.wait_ge(ms_done, 1)
            act.activation(rms[:, 1], rms[:, 0], ACT.Sqrt).then_inc(rt_done, 1)
            hi(SMALL, 0, 0)
            for k in range(NK):
                act.wait_ge(h_made, k + 1)
                act.activation(hTh[:, k], hf[:, k], ACT.Copy).then_inc(h_hi, 1)

            def evac(s, b, t, dst, src, func=ACT.Copy, wait=True, free=True):
                if wait:
                    act.wait_ge(acc_done, 4 * s.b0 + t + 1 + b * 4)
                ins = act.activation(dst, src, func)
                if free:
                    ins.then_inc(acc_free, 1)
                return ins

            order = [SMALL, QI, KV, Q, XBC, Z, GATES]
            for j in range(1, 4):
                hi(SMALL, 0, j)
            hi(QI, 0, 0)
            for t in range(NT):
                step(evac(SMALL, 0, t, dt[:, t], bank[t][:, 0:32], free=False))
                step(evac(SMALL, 0, t, qit[:, t, 512:576], bank[t][:, 32:96], wait=False, free=False))
                evac(SMALL, 0, t, wi[:, t], bank[t][:, 96:104], wait=False)
            for s, nxt in ((QI, KV), (KV, Q)):
                for j in range(1, 4):
                    hi(s, 0, j)
                hi(nxt, 0, 0)
                for t in range(NT):
                    if s is QI:
                        evac(s, 0, t, qit[:, t, 0:512], bank[t][:])
                    else:
                        step(evac(s, 0, t, qk[:, t, 1024:1280], bank[t][:, 0:256], free=False))
                        evac(s, 0, t, vt[:, t], bank[t][:, 256:512], wait=False)
            for b in range(2):
                for j in range(1, 4):
                    hi(Q, b, j)
                hi_next(Q, b, XBC, b == 1)
                for t in range(NT):
                    evac(Q, b, t, qk[:, t, 512 * b:512 * b + 512], bank[t][:])

            def xbc_block(b, first, is_last):
                for j in range(1, 4):
                    hi(XBC, b, j)
                hi_next(XBC, b, Z, is_last)
                for t in range(4):
                    act.wait_ge(acc_done, 4 * XBC.b0 + t + 1 + b * 4)
                    if not first:
                        act.wait_ge(conv_done, b * 4 + (t - 3))
                    act.activation(craw[:, t], bank[t][:], ACT.Copy).then_inc(acc_free, 1)

            def silus(b):
                for t in range(4):
                    act.wait_ge(conv_done, b * 4 + (t + 1))
                    act.activation(xbc[:, bass.ds(b * 4 + t, 1), :], cacc[:, t:t + 1], ACT.Silu).then_inc(silu_done, 1)

            xbc_block(0, True, False)
            with act.Fori(1, XBC.blocks - 1) as b:
                xbc_block(b, False, False)
                silus(b - 1)
            xbc_block(XBC.blocks - 1, False, True)
            silus(XBC.blocks - 2)
            silus(XBC.blocks - 1)

            def staged(s, b, func, n, is_last, nxt):
                for j in range(1, 4):
                    hi(s, b, j)
                hi_next(s, b, nxt, is_last)
                if n >= 2:
                    act.wait_ge(stg_out[n % 2], 16 * (n // 2))
                for t in range(4):
                    act.wait_ge(acc_done, 4 * s.b0 + t + 1 + b * 4)
                    act.activation(stg[:, n % 2, t], bank[t][:], func).then_inc(stg_full, 1)

            for s, func, n0, nxt in ((Z, ACT.Silu, 0, GATES), (GATES, ACT.Sigmoid, 4, BR_S)):
                for b in range(4):
                    staged(s, b, func, n0 + b, b == 3, nxt if not (stop <= 3 and s is GATES) else None)
            if stop <= 1:
                return

            act.wait_ge(rope_arg, 2)
            act.activation(cosT[:], cosT[:], ACT.Sin).then_inc(rope_done, 1)
            act.activation(sinT[:], sinT[:], ACT.Sin).then_inc(rope_done, 1)
            act.wait_ge(qk_ms, 1)
            act.activation(rms[:, 1, 0:80], rms[:, 0, 0:80], ACT.Sqrt).then_inc(qk_rt, 1)
            act.wait_ge(dt_in, 1)
            step(act.activation(ysq[:, 0:128], ysq[:, 128:256], ACT.Exp, scale=-1.0))
            act.activation(alog[:], alog[:], ACT.Exp).then_inc(sp_exp, 1)
            act.wait_ge(sp_ln, 1)
            act.activation(ysq[:, 256:384], ysq[:, 256:384], ACT.Ln).then_inc(sp_relu, 1)
            for n in range(17):
                dst = qT[:, n] if n < 8 else kT[:, n - 8] if n < 12 else qiT[:, n - 12] if n < 16 else kiT[:]
                act.wait_ge(tp_done, n + 1)
                act.activation(dst, bank[4 + n % 4][:], ACT.Copy).then_inc(tp_free, 1)
            act.wait_ge(acs_done, 1)
            step(act.activation(acs[:].rearrange("p a b -> p (a b)"), bank[0][:, 0:128], ACT.Copy))
            act.activation(eacs[:].rearrange("p a b -> p (a b)"), bank[0][:, 0:128], ACT.Exp).then_inc(acs_cp, 1)
            act.wait_ge(acsT_tp, 1)
            act.activation(acsT[:], bank[1][0:SSD_H, :], ACT.Copy).then_inc(acsT_ready, 1)
            for i in range(NT):
                nk = P * (i + 1)
                if i == 0:
                    act.wait_ge(acsd_out, 16)
                for h in range(IH):
                    n = IH * i + h
                    act.wait_ge(ix_done, n + 1)
                    if n >= 4:
                        act.wait_ge(rl_used, n - 3)
                    act.activation(rl[:, n % 4, 0:nk], bank[4 + n % 4][:, 0:nk], ACT.Relu,
                                   scale=DH ** -0.5).then_inc(rl_full, 1)

            def attn_out(i):
                for b in range(2):
                    act.wait_ge(ot_done, 2 * i + b + 1)
                    act.activation(attnT[:, 4 * b:4 * b + 4, i * P:(i + 1) * P],
                                   bank[1 + b][:].rearrange("p (f t) -> p f t", f=4), ACT.Copy).then_inc(attn_ready, 1)

            for i in range(NT):
                nk = P * (i + 1)
                for h in range(AH):
                    n = AH * i + h
                    act.wait_ge(neg_max, n + 1)
                    if n >= 2:
                        act.wait_ge(pt_done, n - 1)
                    if n == 0:
                        act.wait_ge(tp_done, 17)
                    act.activation(pe_[:, n % 2, 0:nk], pm[:, n % 2, 0:nk], ACT.Exp, bias=asm[:, 0, h:h + 1],
                                   accum_out=asm[:, 1, h:h + 1]).then_inc(exp_done, 1)
                    if h == 1 and i:
                        attn_out(i - 1)
            attn_out(NT - 1)
            if stop <= 2:
                return

            for i in range(NT):
                act.wait_ge(b_done, i + 1)
                act.activation(btok[:].rearrange("p g n -> p (g n)"), bank[4][:], ACT.Copy).then_inc(b_copied, 1)
                act.wait_ge(alast_done, i + 1)
                step(act.activation(ssm[:, 1], ssm[:, 1], ACT.Exp))
                act.activation(ssm[:, 2], ssm[:, 0], ACT.Exp).then_inc(decay_done, 1)
                for g in range(SSD_G):
                    act.wait_ge(segmin_done, SSD_G * i + g + 1)
                    act.activation(seg[:, 8 * g:8 * g + 8], seg[:, 8 * g:8 * g + 8], ACT.Exp).then_inc(segexp_done, 1)
                for g in range(SSD_G):
                    act.wait_ge(y_used, SSD_G * i + g + 1)
                    step.wait()
                    step(act.activation(ysq[:], yt[:, 512 * g:512 * g + 512], ACT.Square, accum_out=ssm[:, 3, g:g + 1]))
                step.wait()
                act.sem_inc(ysq_done, 1)
                act.wait_ge(yn_done, 2 * i + 1)
                act.activation(ssm[:, 4, 0:4], ssm[:, 4, 0:4], ACT.Sqrt).then_inc(yrt_done, 1)
                for b in range(2):
                    act.wait_ge(yt_done, 4 * i + b + 1)
                    for f in range(4):
                        m = 4 * b + f
                        ins = act.activation(xbc[:, m, i * P:(i + 1) * P], bank[b][:, f * P:(f + 1) * P], ACT.Copy,
                                             scale=gssd[:, m:m + 1])
                        if f % 2 == 1:
                            ins.then_inc(y_done, 1)
                        else:
                            step(ins)
            if stop <= 3:
                return

            for k in range(NY):
                if k == 0:
                    act.wait_ge(y_done, 8 * NT)
                act.activation(yh[:, k], xbc[:, k], ACT.Copy).then_inc(y_hi, 1)
            act.wait_ge(y_split, NY)
            for k in range(NK):
                act.activation(ah[:, k], attnT[:, k], ACT.Copy).then_inc(a_split_hi, 1)

            def section_hi(s, nxt, between=None):
                for b in range(s.blocks):
                    for j in range(1, s.units):
                        hi(s, b, j)
                    hi_next(s, b, nxt, b == s.blocks - 1)
                    if between:
                        between(b)

            section_hi(BR_S, BR_A)

            def merged_hi(b):
                for t in range(4):
                    m = 4 * b + t
                    act.wait_ge(mg_done, m + 1)
                    act.activation(mh[:, m], mg[:, m], ACT.Copy).then_inc(m_hi, 1)

            section_hi(BR_A, OUT, merged_hi)
            section_hi(OUT, PQ)
            for k in range(NK):
                act.wait_ge(x1_done, k + 1)
                act.activation(sq2[:, k], xT[:, k], ACT.Square).then_inc(sq_done, 1)
            act.wait_ge(ms_done, 2)
            act.activation(rms2[:, 1], rms2[:, 0], ACT.Sqrt).then_inc(rt_done, 1)
            for k in range(NK):
                act.wait_ge(h_made, NK + k + 1)
                act.activation(hTh[:, k], hf2[:, k], ACT.Copy).then_inc(h_hi, 1)
            for b in range(PQ.blocks):
                for j in range(1, 4):
                    hi(PQ, b, j)
                if b == 0:
                    hi(PQ, 1, 0)
                elif stop > 4:
                    act.wait_ge(raw_full[0], 16 * (PU0 // 4 + 1))
                    act.wait_ge(unit_used, PQ.p1)
                    act.activation(whi[:, 0], raw[:, 0], ACT.Copy).then_inc(hi_done, 1)
                for t in range(4):
                    act.wait_ge(acc_done, 4 * (PQ.b0 + b) + t + 1)
                    act.activation(pqT[:, 4 * b + t], bank[t][:], ACT.Copy).then_inc(acc_free, 1)
            if stop <= 4:
                return

            for i in range(NT):
                for q in range(4):
                    act.wait_ge(sc_done, 4 * i + q + 1)
                    if i:
                        act.wait_ge(pk_done, i)
                    act.activation(sc[:, 2 * q:2 * q + 2].rearrange("p h a n -> p (h a n)"), bank[q][:],
                                   ACT.Copy).then_inc(sc_full, 1)
                act.wait_ge(sub_done, i + 1)
                act.activation(sv[:], sv[:], ACT.Exp).then_inc(gexp_done, 1)
                act.wait_ge(selT_tp, i + 1)
                act.activation(selT[:, :, i * P:(i + 1) * P],
                               bank[4][:, 0:3 * P].rearrange("p (a t) -> p a t", a=3), ACT.Copy).then_inc(selT_done, 1)
            def gate_evac(c, first):
                for k in range(2):
                    if not first:
                        act.wait_ge(w_out[k], c * 16)
                    for q in range(8):
                        n = 8 * k + q
                        act.wait_ge(w_done, c * 16 + (n + 1))
                        act.activation(gst[:, k, :, 4 * q:4 * q + 4].rearrange("p e t -> p t e"),
                                       bank[5 + n % 2][:].rearrange("p (t e) -> p t e", t=4),
                                       ACT.Copy).then_inc(w_evac, 1)
            gate_evac(0, True)
            with act.Fori(1, NTC // 2) as c:
                gate_evac(c, False)

            def expert_hi(g, n):
                act.wait_ge(raw_full[n % 4], 16 * (PU0 // 4 + n // 4 + 1) + g * 64)
                expert_free(act, g, n)
                act.activation(whi[:, n % 2], raw[:, n % 4], ACT.Copy).then_inc(hi_done, 1)

            def group(g, is_last):
                for n in range(2 * GT):
                    if n < 2 * GT - 1:
                        expert_hi(g, n + 1)
                    elif not is_last:
                        expert_hi(g + 1, 0)
                    if n < GT:
                        act.wait_ge(up_done, g * GT + (n + 1))
                        gd = g * GT + (n - 1)
                        if not (isinstance(gd, int) and gd <= 0):
                            act.wait_ge(gated, gd)
                        act.activation(gel[:, n % 2], bank[n % 2][:], ACT.Gelu).then_inc(gelu_done, 1)
                        act.wait_ge(gated, g * GT + (n + 1))
                        if not (isinstance(g, int) and g == 0):
                            act.wait_ge(down_done, g * GT)
                        act.activation(ach[:, n], gac[:, n % 2], ACT.Copy).then_inc(act_hi, 1)

            group(0, False)
            with act.Fori(1, NG - 1) as g:
                group(g, False)
            group(NG - 1, True)

        @block.vector
        def _(dve):
            step = Steps(dve, dve_step)

            def do(ins):
                step(ins)
                step.wait()

            def lo(s, b, j):
                dve.wait_ge(hi_done, s.u0 + j + 1 + b * s.units)
                n = 2 * NSMALL if s is SMALL else 1024
                dve.tensor_tensor(wlo[:, j % 2, 0:n], raw[:, j % 4, 0:n], whi[:, j % 2, 0:n].bitcast(F),
                                  ALU.subtract).then_inc(lo_done, 1)

            def lo_next(s, b, nxt, is_last):
                if is_last:
                    if nxt is not None:
                        lo(nxt, 0, 0)
                else:
                    lo(s, b + 1, 0)

            dve.wait_ge(consts_in, 16 * 13)
            do(dve.tensor_copy(posf[:], posi[:]))
            inv = np.float32(ROPE_THETA) ** (-np.arange(0, 2 * ROT, 2, dtype=np.float32) / np.float32(2 * ROT))
            for r in range(ROT):
                step(dve.tensor_scalar(sinT[:, :, r], posf[:], float(inv[r]), None, ALU.mult))
            step.wait()
            rsc = rms[:].rearrange("p a t -> p (a t)")
            v32 = [rsc[:, 32 * n:32 * n + 32].rearrange("p (a r) -> p a r", r=ROT) for n in range(4)]
            do(dve.tensor_copy(v32[3], sinT[:]))
            for dst, turn, quarter in ((sinT, 0.0, 0.0), (cosT, 0.25, float(np.pi / 2))):
                do(dve.tensor_scalar(v32[0], v32[3], 1 / TWO_PI, turn, ALU.mult, ALU.add))
                do(dve.tensor_scalar(v32[1], v32[0], MAGIC, MAGIC, ALU.add, ALU.subtract))
                do(dve.scalar_tensor_tensor(v32[2], v32[1], -C1, v32[3], ALU.mult, ALU.add))
                do(dve.scalar_tensor_tensor(v32[0], v32[1], -C2, v32[2], ALU.mult, ALU.add))
                do(dve.scalar_tensor_tensor(v32[2], v32[1], -C3, v32[0], ALU.mult, ALU.add))
                do(dve.tensor_scalar(v32[0], v32[2], quarter, PI_F, ALU.add, ALU.min))
                do(dve.tensor_scalar(dst[:], v32[0], -PI_F, None, ALU.max))
            dve.sem_inc(rope_arg, 2)

            dve.wait_ge(cond_done, 1)
            for k in range(NK):
                dve.wait_ge(ada_in[k % 2], 16 * (k // 2 + 1))
                if k == 0:
                    ins = dve.tensor_scalar(ada[:, 0:2048], adar[:, 0], cT[:, 0:1], None, ALU.mult)
                else:
                    dve.wait_ge(ada_v_used, k)
                    ins = dve.scalar_tensor_tensor(ada[:, 0:2048], adar[:, k % 2], cT[:, k:k + 1], ada[:, 0:2048],
                                                   ALU.mult, ALU.add)
                ins.then_inc(ada_v_used, 1)
            dve.wait_ge(mod_done, 1)
            do(dve.tensor_tensor(mod[:, 0:16], bank[4][:, 0:16], bada[:, 0:16], ALU.add))
            do(dve.scalar_tensor_tensor(a1[:], mod[:, 8:16], 1.0, g1[:], ALU.add, ALU.mult))
            dve.wait_ge(ssq_done, 1)
            dve.tensor_scalar(rms[:, 0], bank[5][:], 1.0 / D, EPS, ALU.mult, ALU.add).then_inc(ms_done, 1)
            dve.wait_ge(rt_done, 1)
            do(dve.reciprocal(rms[:, 0], rms[:, 1]))
            for k in range(NK):
                do(dve.tensor_tensor(hf[:, k], xT[:, k], rms[:, 0], ALU.mult))
                dve.tensor_scalar(hf[:, k], hf[:, k], a1[:, k:k + 1], mod[:, k:k + 1], ALU.mult,
                                  ALU.add).then_inc(h_made, 1)
                if k:
                    dve.wait_ge(h_hi, k)
                    dve.tensor_tensor(hTl[:, k - 1], hf[:, k - 1], hTh[:, k - 1].bitcast(F), ALU.subtract).then_inc(h_ready, 1)
            dve.wait_ge(h_hi, NK)
            dve.tensor_tensor(hTl[:, NK - 1], hf[:, NK - 1], hTh[:, NK - 1].bitcast(F), ALU.subtract).then_inc(h_ready, 1)
            lo(SMALL, 0, 0)

            for s, nxt in ((SMALL, QI), (QI, KV), (KV, Q), (Q, XBC)):
                for b in range(s.blocks):
                    for j in range(1, 4):
                        lo(s, b, j)
                    lo_next(s, b, nxt, b == s.blocks - 1)
                if s is SMALL:
                    dve.wait_ge(mod_done, 2)
                    do(dve.tensor_tensor(mod[:, 16:48], bank[4][:, 16:48], bada[:, 16:48], ALU.add))
                    do(dve.scalar_tensor_tensor(a2[:], mod[:, 32:40], 1.0, g2[:], ALU.add, ALU.mult))
                    dve.sem_inc(mod_out, 1)

            def conv(b, t, first):
                m = b * 4 + t
                cw = [convw[:].rearrange("p m k -> p (m k)")[:, bass.ds(m * CONV_K + k, 1)] for k in range(CONV_K)]
                dve.wait_ge(acc_free, 4 * XBC.b0 + 1 + m)
                if not first:
                    dve.wait_ge(silu_done, m - 3)
                do(dve.tensor_scalar(cacc[:, t], craw[:, t], cw[3], convb[:, bass.ds(m, 1)], ALU.mult, ALU.add))
                for k in range(1, CONV_K):
                    ins = dve.scalar_tensor_tensor(cacc[:, t, k:], craw[:, t, 0:T - k], cw[3 - k], cacc[:, t, k:],
                                                   ALU.mult, ALU.add)
                    if k < CONV_K - 1:
                        do(ins)
                    else:
                        ins.then_inc(conv_done, 1)

            for j in range(1, 4):
                lo(XBC, 0, j)
            lo(XBC, 1, 0)

            def conv_block(b, is_last, first):
                for j in range(1, 4):
                    lo(XBC, b, j)
                    conv(b - 1, j - 1, first)
                lo_next(XBC, b, Z, is_last)
                conv(b - 1, 3, first)
            conv_block(1, False, True)
            with dve.Fori(2, XBC.blocks - 1) as b:
                step.enter(b - 2, 12)
                conv_block(b, False, False)
                step.leave(XBC.blocks - 3)
            conv_block(XBC.blocks - 1, True, False)
            for t in range(4):
                conv(XBC.blocks - 1, t, False)

            for s, nxt in ((Z, GATES), (GATES, BR_S)):
                for b in range(4):
                    for j in range(1, 4):
                        lo(s, b, j)
                    lo_next(s, b, nxt if not (stop <= 3 and s is GATES) else None, b == 3)
            if stop <= 1:
                return

            dve.wait_ge(silu_done, NX)
            for k in range(2):
                dve.wait_ge(stg_out[k], 16 * 4)
            q4 = qk[:].rearrange("p t (h d) -> p t h d", d=DH)
            do(dve.tensor_tensor(prep[:], qk[:], qk[:], ALU.mult))
            ssq = rms[:, 0, 0:80].rearrange("p (t h) -> p t h", h=20)
            do(dve.tensor_reduce(ssq, prep[:].rearrange("p t (h d) -> p t h d", d=DH), AX.X, ALU.add))
            dve.tensor_scalar(rms[:, 0, 0:80], rms[:, 0, 0:80], 1.0 / DH, EPS, ALU.mult, ALU.add).then_inc(qk_ms, 1)
            dtv = dt[:]
            u_, v_, w_, r_ = (ysq[:, 128 * n:128 * n + 128].rearrange("p (t h) -> p t h", h=SSD_H) for n in range(4))
            dve.wait_ge(qk_rt, 1)
            do(dve.reciprocal(rms[:, 0, 0:80], rms[:, 1, 0:80]))
            for t in range(NT):
                step(dve.tensor_tensor(q4[:, t], q4[:, t],
                                       rms[:, 0, 20 * t:20 * t + 20].unsqueeze(2).to_broadcast([P, 20, DH]), ALU.mult))
            step.wait()
            for t in range(NT):
                step(dve.tensor_tensor(q4[:, t, 0:AH], q4[:, t, 0:AH], qg[:].unsqueeze(1).to_broadcast([P, AH, DH]), ALU.mult))
                step(dve.tensor_tensor(q4[:, t, AH:], q4[:, t, AH:], kg[:].unsqueeze(1).to_broadcast([P, KVH, DH]), ALU.mult))
            step.wait()
            dve.wait_ge(rope_done, 2)
            pv = prep[:].rearrange("p t c -> p (t c)")
            qi4 = qit[:].rearrange("p t (h d) -> p t h d", d=DH)
            for x4, nh in ((q4, 20), (qi4, 9)):
                for t in range(NT):
                    cs = cosT[:, t].unsqueeze(1).to_broadcast([P, nh, ROT])
                    sn = sinT[:, t].unsqueeze(1).to_broadcast([P, nh, ROT])
                    t1, t2 = x4[:, t, :, 0:ROT], x4[:, t, :, ROT:2 * ROT]
                    s4 = [pv[:, (4 * t + k) * 160:(4 * t + k) * 160 + nh * ROT].rearrange("p (h r) -> p h r", r=ROT) for k in range(4)]
                    step(dve.tensor_tensor(s4[0], t1, cs, ALU.mult))
                    step(dve.tensor_tensor(s4[1], t2, sn, ALU.mult))
                    step(dve.tensor_tensor(s4[2], t2, cs, ALU.mult))
                    step(dve.tensor_tensor(s4[3], t1, sn, ALU.mult))
                step.wait()
                for t in range(NT):
                    t1, t2 = x4[:, t, :, 0:ROT], x4[:, t, :, ROT:2 * ROT]
                    s4 = [pv[:, (4 * t + k) * 160:(4 * t + k) * 160 + nh * ROT].rearrange("p (h r) -> p h r", r=ROT) for k in range(4)]
                    step(dve.tensor_tensor(t1, s4[0], s4[1], ALU.subtract))
                    step(dve.tensor_tensor(t2, s4[2], s4[3], ALU.add))
                step.wait()
            dve.wait_ge(silu_done, NX)
            for e in range(2):
                for t in range(NT):
                    step(dve.tensor_copy(kdup[:, t, :, e, :], q4[:, t, AH:]))
                step(dve.tensor_copy(kidup[:, :, e, :], qi4[:, :, IH]))
            step.wait()
            dve.sem_inc(prep_done, 1)

            do(dve.tensor_tensor(dtv, dtv, dtb[:].unsqueeze(1).to_broadcast([P, NT, SSD_H]), ALU.add))
            do(dve.tensor_scalar(u_, dtv, -1.0, None, ALU.mult))
            dve.tensor_tensor(v_, u_, dtv, ALU.max).then_inc(dt_in, 1)
            dve.wait_ge(sp_exp, 1)
            do(dve.tensor_scalar(w_, u_, 1.0, None, ALU.add))
            do(dve.tensor_scalar(v_, w_, 1.0, None, ALU.is_equal))
            do(dve.scalar_tensor_tensor(r_, w_, -1.0, v_, ALU.add, ALU.add))
            dve.sem_inc(sp_ln, 1)
            dve.wait_ge(sp_relu, 1)
            do(dve.tensor_tensor(w_, w_, v_, ALU.add))
            do(dve.tensor_tensor(w_, w_, u_, ALU.mult))
            do(dve.reciprocal(r_, r_))
            do(dve.tensor_tensor(w_, w_, r_, ALU.mult))
            do(dve.scalar_tensor_tensor(dtv, dtv, 0.0, w_, ALU.max, ALU.add))
            dve.scalar_tensor_tensor(v_, dtv, -1.0, alog[:].unsqueeze(1).to_broadcast([P, NT, SSD_H]), ALU.mult,
                                     ALU.mult).then_inc(ad_done, 1)
            dve.wait_ge(tp_done, 17)
            dve.wait_ge(acs_done, 1)
            do(dve.memset(zer[:], 0.0))
            do(dve.tensor_scalar(wi[:], wi[:], IH ** -0.5, None, ALU.mult))

            for i in range(NT):
                nk = P * (i + 1)
                for h in range(IH):
                    n = IH * i + h
                    dve.wait_ge(rl_full, n + 1)
                    if h == 0:
                        ins = dve.tensor_scalar(score[:, 0:nk], rl[:, n % 4, 0:nk], wi[:, i, h:h + 1], None, ALU.mult)
                    else:
                        dve.wait_ge(rl_used, n)
                        ins = dve.scalar_tensor_tensor(score[:, 0:nk], rl[:, n % 4, 0:nk], wi[:, i, h:h + 1],
                                                       score[:, 0:nk], ALU.mult, ALU.add)
                    ins.then_inc(rl_used, 1)
                dve.wait_ge(rl_used, IH * i + IH)
                m = mb[:, i, 0:nk]
                if i == 0:
                    step(dve.memset(m, 0.0))
                    step.wait()
                    do(dve.memset(mb[0:CHUNK, 0, CHUNK:nk], NEG))
                    continue
                do(dve.memset(score[0:CHUNK, nk - CHUNK:nk], NEG))
                for r in range(TOPK // 8):
                    src = score if r == 0 else work
                    do(dve.max(tk8[:, 0:8], src[:, 0:nk]))
                    if r < TOPK // 8 - 1:
                        do(dve.match_replace(work[:, 0:nk], tk8[:, 0:8], src[:, 0:nk], -3e38))
                do(dve.tensor_scalar(selm[:, 0:nk], score[:, 0:nk], tk8[:, 7:8], 0.0, ALU.is_gt, ALU.add,
                                     accum_out=tk8[:, 8:9]))
                do(dve.tensor_scalar(eqm[:, 0:nk], score[:, 0:nk], tk8[:, 7:8], None, ALU.is_equal))
                do(dve.tensor_tensor_scan(cum[:, 0:nk], eqm[:, 0:nk], zer[:, 0:nk], 0.0, ALU.add, ALU.add))
                do(dve.tensor_scalar(tk8[:, 9:10], tk8[:, 8:9], -1.0, float(TOPK), ALU.mult, ALU.add))
                do(dve.scalar_tensor_tensor(cum[:, 0:nk], cum[:, 0:nk], tk8[:, 9:10], eqm[:, 0:nk], ALU.is_le, ALU.mult))
                do(dve.tensor_tensor(selm[:, 0:nk], selm[:, 0:nk], cum[:, 0:nk], ALU.add))
                do(dve.tensor_scalar(m, selm[:, 0:nk], -1.0, -NEG, ALU.add, ALU.mult))

            def pt_copy(n):
                i = n // AH
                nk = P * (i + 1)
                dve.wait_ge(pt_done, n + 1)
                if n >= 2:
                    dve.wait_ge(pv_done, n - 1)
                dve.tensor_copy(pts[:, n % 2, 0:nk], bank[6][:, 0:nk]).then_inc(pt_evac, 1)

            for i in range(NT):
                nk = P * (i + 1)
                for h in range(AH):
                    n = AH * i + h
                    dve.wait_ge(s_done, n + 1)
                    if n >= 2:
                        dve.wait_ge(exp_done, n - 1)
                    do(dve.tensor_tensor_reduce(out=pm[:, n % 2, 0:nk], in0=bank[4 + n % 2][:, 0:nk], in1=mb[:, i, 0:nk],
                                                scale=DH ** -0.5, scalar=-3e38, op0=ALU.add, op1=ALU.max,
                                                accum_out=asm[:, 2, h:h + 1]))
                    if h == 0 and i:
                        dve.wait_ge(exp_done, n)
                    dve.tensor_scalar(asm[:, 0, h:h + 1], asm[:, 2, h:h + 1], -1.0, None, ALU.mult).then_inc(neg_max, 1)
                    if h:
                        pt_copy(n - 1)
                pt_copy(AH * i + AH - 1)
                dve.wait_ge(exp_done, AH * i + AH)
                do(dve.reciprocal(asm[:, 2], asm[:, 1]))
                dve.wait_ge(pv_done, AH * i + AH)
                if i:
                    dve.wait_ge(ot_done, 2 * i)
                for b in range(2):
                    dve.tensor_tensor(otok[:, 512 * b:512 * b + 512].rearrange("p (h d) -> p h d", d=DH),
                                      bank[7 if b == 0 else 3][:].rearrange("p (h d) -> p h d", d=DH),
                                      asm[:, 2, 8 * b:8 * b + 8].unsqueeze(2).to_broadcast([P, 8, DH]),
                                      ALU.mult).then_inc(o_ready, 1)
                dve.wait_ge(o_ready, 2 * i + 2)
            if stop <= 2:
                return

            dve.wait_ge(attn_ready, 2 * NT)
            do(dve.memset(st[:], 0.0))

            def bc(x, n=SSD_P):
                return x.unsqueeze(2).to_broadcast([P, x.shape[1], n])

            for i in range(NT):
                dve.wait_ge(seg_in, 16 * (i + 1))
                do(dve.tensor_copy(ssm[:, 0], seg[:, :, P - 1]))
                dve.tensor_tensor(ssm[:, 1], ssm[:, 0], acs[:, i], ALU.subtract).then_inc(alast_done, 1)
                for h in range(SSD_H):
                    ins = dve.tensor_scalar(seg[:, h], seg[:, h], acs[:, i, h:h + 1], 0.0, ALU.subtract, ALU.min)
                    if h % 8 == 7:
                        ins.then_inc(segmin_done, 1)
                    else:
                        step(ins)
                for b in range(4):
                    dve.wait_ge(xp_done, 4 * i + b + 1)
                    pv_ = bank[b][:].rearrange("p (h d) -> p h d", d=SSD_P)
                    step(dve.tensor_tensor(xd[:, 512 * b:512 * b + 512].rearrange("p (h d) -> p h d", d=SSD_P), pv_,
                                           bc(dt[:, i, 8 * b:8 * b + 8]), ALU.mult))
                    step(dve.tensor_tensor(xsk[:, 512 * b:512 * b + 512].rearrange("p (h d) -> p h d", d=SSD_P), pv_,
                                           bc(dskip[:, 8 * b:8 * b + 8]), ALU.mult))
                dve.wait_ge(cb_done, i + 1)
                do(dve.tensor_tensor(cbm[:], bank[5][:].rearrange("p (g l) -> p g l", g=SSD_G),
                                     tri[:].unsqueeze(1).to_broadcast([P, SSD_G, P]), ALU.mult))
                dve.wait_ge(decay_done, i + 1)
                do(dve.tensor_tensor(xdd[:].rearrange("p (h d) -> p h d", d=SSD_P),
                                     xd[:].rearrange("p (h d) -> p h d", d=SSD_P), bc(ssm[:, 1]), ALU.mult))
                for g in range(SSD_G):
                    dve.wait_ge(segexp_done, SSD_G * i + g + 1)
                    dve.tensor_tensor(seg[:, 8 * g:8 * g + 8], seg[:, 8 * g:8 * g + 8],
                                      cbm[:, g].unsqueeze(1).to_broadcast([P, 8, P]), ALU.mult).then_inc(m_ready, 1)
                dve.wait_ge(z_in, 16 * (i + 1))
                for g in range(SSD_G):
                    c = slice(512 * g, 512 * g + 512)
                    dve.wait_ge(yo_done, SSD_G * i + g + 1)
                    if i:
                        do(dve.tensor_tensor(ytmp[:].rearrange("p (h d) -> p h d", d=SSD_P),
                                             bank[6][:].rearrange("p (h d) -> p h d", d=SSD_P),
                                             bc(eacs[:, i, 8 * g:8 * g + 8]), ALU.mult))
                        do(dve.tensor_tensor(xsk[:, c], xsk[:, c], ytmp[:], ALU.add))
                    do(dve.tensor_tensor(yt[:, c], bank[7][:], xsk[:, c], ALU.add))
                    dve.tensor_tensor(yt[:, c], yt[:, c], zc[:, c], ALU.mult).then_inc(y_used, 1)
                dve.wait_ge(yo_done, SSD_G * i + SSD_G)
                if i < NT - 1:
                    do(dve.tensor_tensor(st[:].rearrange("p (h d) -> p h d", d=SSD_P),
                                         st[:].rearrange("p (h d) -> p h d", d=SSD_P), bc(ssm[:, 2]), ALU.mult))
                    for g in range(SSD_G):
                        c = slice(512 * g, 512 * g + 512)
                        dve.wait_ge(st_mm, SSD_G * i + g + 1)
                        dve.tensor_tensor(st[:, c], st[:, c], bank[4 + g % 2][:], ALU.add).then_inc(st_used, 1)
                dve.wait_ge(ysq_done, i + 1)
                dve.tensor_scalar(ssm[:, 4, 0:4], ssm[:, 3, 0:4], 1.0 / 512, EPS, ALU.mult, ALU.add).then_inc(yn_done, 1)
                dve.wait_ge(yrt_done, i + 1)
                do(dve.reciprocal(ssm[:, 5, 0:4], ssm[:, 4, 0:4]))
                for g in range(SSD_G):
                    c = slice(512 * g, 512 * g + 512)
                    step(dve.tensor_scalar(yt[:, c], yt[:, c], ssm[:, 5, g:g + 1], None, ALU.mult))
                step.wait()
                dve.sem_inc(yn_done, 1)
                for b in range(2, 4):
                    dve.wait_ge(yt_done, 4 * i + b + 1)
                    for f in range(4):
                        m = 4 * b + f
                        ins = dve.tensor_scalar(xbc[:, m, i * P:(i + 1) * P], bank[b][:, f * P:(f + 1) * P],
                                                gssd[:, m:m + 1], None, ALU.mult)
                        if f % 2 == 1:
                            ins.then_inc(y_done, 1)
                        else:
                            step(ins)
            if stop <= 3:
                return

            for k in range(NY):
                dve.wait_ge(y_hi, k + 1)
                if k == 0:
                    dve.wait_ge(y_done, 8 * NT)
                dve.tensor_tensor(yl[:, k], xbc[:, k], yh[:, k].bitcast(F), ALU.subtract).then_inc(y_split, 1)
            for k in range(NK):
                dve.wait_ge(a_split_hi, k + 1)
                dve.tensor_tensor(al[:, k], attnT[:, k], ah[:, k].bitcast(F), ALU.subtract).then_inc(a_split, 1)

            def section_lo(s, nxt, after):
                for b in range(s.blocks):
                    for j in range(1, s.units):
                        lo(s, b, j)
                    lo_next(s, b, nxt, b == s.blocks - 1)
                    for t in range(4):
                        dve.wait_ge(acc_done, 4 * (s.b0 + b) + t + 1)
                        after(4 * b + t, t)

            def ssd_gate(m, t):
                dve.wait_ge(gate_in[m % 2], 16 * (m // 2 + 1))
                dve.tensor_tensor(mg[:, m], bank[t][:], gring[:, m % 2], ALU.mult).then_inc(acc_free, 1)
                dve.wait_ge(acc_free, 4 * BR_S_free0 + m + 1)
                dve.sem_inc(gate_used, 1)

            def attn_gate(m, t):
                dve.wait_ge(gate_in[m % 2], 16 * (NK // 2 + m // 2 + 1))
                dve.tensor_tensor(mtmp[:], bank[t][:], gring[:, m % 2], ALU.mult).then_inc(acc_free, 1)
                dve.wait_ge(acc_free, 4 * BR_S_free0 + NK + m + 1)
                dve.sem_inc(gate_used, 1)
                dve.tensor_tensor(mg[:, m], mg[:, m], mtmp[:], ALU.add).then_inc(mg_done, 1)
                dve.wait_ge(m_hi, m + 1)
                if m == 0:
                    dve.wait_ge(a_split, NK)
                dve.tensor_tensor(ml[:, m], mg[:, m], mh[:, m].bitcast(F), ALU.subtract).then_inc(m_split, 1)

            def residual(m, t):
                dve.scalar_tensor_tensor(xT[:, m], bank[t][:], mod[:, 16 + m:17 + m], xT[:, m], ALU.mult,
                                         ALU.add).then_inc(acc_free, 1)
                dve.wait_ge(acc_free, 4 * BR_S_free0 + 2 * NK + m + 1)
                dve.sem_inc(x1_done, 1)

            section_lo(BR_S, BR_A, ssd_gate)
            section_lo(BR_A, OUT, attn_gate)
            section_lo(OUT, PQ, residual)
            dve.wait_ge(ssq_done, 2)
            dve.tensor_scalar(rms2[:, 0], bank[5][:], 1.0 / D, EPS, ALU.mult, ALU.add).then_inc(ms_done, 1)
            dve.wait_ge(rt_done, 2)
            do(dve.reciprocal(rms2[:, 0], rms2[:, 1]))
            for k in range(NK):
                do(dve.tensor_tensor(hf2[:, k], xT[:, k], rms2[:, 0], ALU.mult))
                dve.tensor_scalar(hf2[:, k], hf2[:, k], a2[:, k:k + 1], mod[:, 24 + k:25 + k], ALU.mult,
                                  ALU.add).then_inc(h_made, 1)
                if k:
                    dve.wait_ge(h_hi, NK + k)
                    dve.tensor_tensor(hTl[:, k - 1], hf2[:, k - 1], hTh[:, k - 1].bitcast(F), ALU.subtract).then_inc(h_ready, 1)
            dve.wait_ge(h_hi, 2 * NK)
            dve.tensor_tensor(hTl[:, NK - 1], hf2[:, NK - 1], hTh[:, NK - 1].bitcast(F), ALU.subtract).then_inc(h_ready, 1)
            for b in range(PQ.blocks):
                for j in range(1, 4):
                    lo(PQ, b, j)
                if b == 0:
                    lo(PQ, 1, 0)
            if stop <= 4:
                return
            dve.wait_ge(hi_done, PU0 + 1)
            dve.tensor_tensor(wlo[:, 0], raw[:, 0], whi[:, 0].bitcast(F), ALU.subtract).then_inc(lo_done, 1)

            for i in range(NT):
                dve.wait_ge(sc_full, 4 * i + 4)
                for h in range(PH):
                    for e in range(2):
                        row = sc[:, h, e]
                        do(dve.max(v8[:, h, e, 0:8], row))
                        step(dve.max_index(i8[:, h, e, 0:8], v8[:, h, e, 0:8], row))
                        step.wait()
                        do(dve.match_replace(row, v8[:, h, e, 0:8], row, -3e38))
                        do(dve.max(v8[:, h, e, 8:16], row))
                        step(dve.max_index(i8[:, h, e, 8:16], v8[:, h, e, 8:16], row))
                step.wait()
                dve.sem_inc(pk_done, 1)
                step(dve.tensor_copy(if8[:], i8[:]))
                for h in range(PH):
                    step(dve.tensor_tensor(cand[:, h], v8[:, h, 0].unsqueeze(2).to_broadcast([P, PK, PK]),
                                           v8[:, h, 1].unsqueeze(1).to_broadcast([P, PK, PK]), ALU.add))
                step.wait()
                for h in range(PH):
                    row = cand[:, h].rearrange("p a b -> p (a b)")
                    do(dve.max(sv[:, h, 0:8], row))
                    step(dve.max_index(ci[:, h, 0:8], sv[:, h, 0:8], row))
                    step.wait()
                    do(dve.match_replace(row, sv[:, h, 0:8], row, -3e38))
                    do(dve.max(sv[:, h, 8:16], row))
                    step(dve.max_index(ci[:, h, 8:16], sv[:, h, 8:16], row))
                step.wait()
                do(dve.tensor_copy(gsm[:, 0], sv[:, :, 0]))
                dve.tensor_tensor(sv[:], sv[:], gsm[:, 0].unsqueeze(2).to_broadcast([P, PH, PK]),
                                  ALU.subtract).then_inc(sub_done, 1)
                step(dve.tensor_scalar(cab[:, 0], ci[:], 4, None, ALU.logical_shift_right))
                step(dve.tensor_scalar(cab[:, 1], ci[:], 15, None, ALU.bitwise_and))
                step.wait()
                do(dve.tensor_copy(cabf[:], cab[:]))
                if i:
                    dve.wait_ge(selT_tp, i)
                for e in range(2):
                    do(dve.tensor_tensor(eqa[:].rearrange("p h k j -> p (h k) j"),
                                         cabf[:, e].rearrange("p h k -> p (h k)").unsqueeze(2).to_broadcast([P, P, PK]),
                                         iota16[:].unsqueeze(1).to_broadcast([P, P, PK]), ALU.is_equal))
                    for h in range(PH):
                        step(dve.tensor_tensor(eqa[:, h], eqa[:, h], if8[:, h, e].unsqueeze(1).to_broadcast([P, PK, PK]), ALU.mult))
                    step.wait()
                    do(dve.tensor_reduce(sel[:, e], eqa[:].rearrange("p h k j -> p (h k) j"), AX.X, ALU.add))
                dve.wait_ge(gexp_done, i + 1)
                do(dve.tensor_reduce(gsm[:, 0], sv[:], AX.X, ALU.add))
                do(dve.reciprocal(gsm[:, 1], gsm[:, 0]))
                dve.tensor_tensor(sel[:, 2].rearrange("p (h k) -> p h k", k=PK), sv[:],
                                  gsm[:, 1].unsqueeze(2).to_broadcast([P, PH, PK]), ALU.mult).then_inc(sel_ready, 1)
                dve.wait_ge(sel_ready, i + 1)
            dve.wait_ge(selT_done, NT)

            def onehots(c, first):
                sT = selT[:].rearrange("p a t -> p (a t)")
                for n in range(2 * TC):
                    r = n % 8
                    if n % 4 == 0 and not (first and n < 8):
                        dve.wait_ge(w_done, c * 16 + (n // 4 - 1))
                    t = c * 64 + n
                    step(dve.tensor_scalar(oh1[:, r], iota[:], sT[:, bass.ds(t, 1)],
                                           sT[:, bass.ds(t + 2 * T, 1)], ALU.is_equal, ALU.mult))
                    ins = dve.tensor_scalar(oh2[:, r], iota[:], sT[:, bass.ds(t + T, 1)], None, ALU.is_equal)
                    if n % 4 == 3:
                        ins.then_inc(oh_made, 1)
                    else:
                        step(ins)
            onehots(0, True)
            with dve.Fori(1, NTC // 2) as c:
                onehots(c, False)
            step.n += (NTC // 2 - 2) * (2 * TC + 3 * TC // 2)

            do(dve.memset(acc[:], 0.0))

            def expert_lo(g, n):
                dve.wait_ge(hi_done, PU0 + n + 1 + g * (2 * GT))
                dve.tensor_tensor(wlo[:, n % 2], raw[:, n % 4], whi[:, n % 2].bitcast(F), ALU.subtract).then_inc(lo_done, 1)

            def group(g, is_last):
                for n in range(2 * GT):
                    if n < 2 * GT - 1:
                        expert_lo(g, n + 1)
                    elif not is_last:
                        expert_lo(g + 1, 0)
                    if n < GT:
                        if n == 0:
                            dve.wait_ge(gg_in, 16 + g * 16)
                        dve.wait_ge(gelu_done, g * GT + (n + 1))
                        if not (isinstance(g, int) and g == 0 and n < 2):
                            dve.wait_ge(act_ready, g * GT + (n - 1))
                        dve.tensor_tensor(gac[:, n % 2].rearrange("p (c t) -> p c t", t=TC),
                                          gel[:, n % 2].rearrange("p (c t) -> p c t", t=TC),
                                          gg[:, :, n, :], ALU.mult).then_inc(gated, 1)
                        dve.wait_ge(act_hi, g * GT + (n + 1))
                        dve.tensor_tensor(acl[:, n], gac[:, n % 2], ach[:, n].bitcast(F), ALU.subtract).then_inc(act_ready, 1)
                    else:
                        m = n - GT
                        dve.wait_ge(down_done, g * GT + (m + 1))
                        if not (isinstance(g, int) and g == 0):
                            dve.wait_ge(added, g * GT + (m - GT + 1))
                        dve.tensor_tensor(acc[:, m], acc[:, m], bank[2 + m % 2][:], ALU.add).then_inc(added, 1)

            group(0, False)
            with dve.Fori(1, NG - 1) as g:
                group(g, False)
            group(NG - 1, True)
            for m in range(NK):
                dve.wait_ge(added, GT * (NG - 1) + m + 1)
                dve.scalar_tensor_tensor(xT[:, m], acc[:, m], mod[:, 40 + m:41 + m], xT[:, m], ALU.mult,
                                         ALU.add).then_inc(out_made, 1)

        @block.tensor
        def _(pe):
            step = Steps(pe, pe_step)
            pe.wait_ge(consts_made, 1)
            for k in range(NK):
                pe.wait_ge(sq_done, k + 1)
                ins = pe.matmul(bank[5][:], ones[:], sq[:, k], start=(k == 0), stop=(k == NK - 1))
            ins.then_inc(ssq_done, 1)
            pe.wait_ge(ada_v_used, NK)
            for m in range(16):
                ins = pe.matmul(bank[4][:, m:m + 1], ada[:, m * P:(m + 1) * P], ones[:, 0:1], start=True, stop=True)
            ins.then_inc(mod_done, 1)

            def free_wait(s, b, t):
                if s is Z or s is GATES:
                    n = (0 if s is Z else 4)
                    if s is Z and isinstance(b, int) and b == 0:
                        pe.wait_ge(acc_free, 4 * (Z.b0 - 1) + t + 1)
                    else:
                        pe.wait_ge(stg_full, 4 * (n - 1) + t + 1 + b * 4)
                elif s is BR_S and b == 0:
                    pe.wait_ge(stg_full, 28 + t + 1)
                else:
                    base = s.b0 if s.b0 < Z.b0 else s.b0 - 8
                    n = 4 * (base - 1) + t + 1 + b * 4
                    if not (isinstance(n, int) and n <= 0):
                        pe.wait_ge(acc_free, n)

            def product(s, b, token_major, mov, ncols=CW, rhs_wait=None):
                mh_, ml_ = mov
                for j in range(s.units):
                    pe.wait_ge(lo_done, s.u0 + j + 1 + b * s.units)
                    wh = whi[:, j % 2, 0:2 * ncols].rearrange("p (a c) -> p a c", a=2)
                    wl = wlo[:, j % 2, 0:2 * ncols].rearrange("p (a c) -> p a c", a=2)
                    for t in range(4):
                        if j == 0:
                            free_wait(s, b, t)
                        for a in range(2):
                            k = 2 * j + a
                            if rhs_wait and t == 0:
                                rhs_wait(k)
                            if token_major:
                                ht, lt = mh_[:, k, t * P:(t + 1) * P], ml_[:, k, t * P:(t + 1) * P]
                                three = ((ht, wh[:, a]), (ht, wl[:, a]), (lt, wh[:, a]))
                            else:
                                wht, wlt = wh[:, a, t * P:(t + 1) * P], wl[:, a, t * P:(t + 1) * P]
                                three = ((wht, mh_[:, k]), (wht, ml_[:, k]), (wlt, mh_[:, k]))
                            for q, (x, y) in enumerate(three):
                                ins = pe.matmul(bank[t][:, 0:ncols] if token_major else bank[t][:], x, y,
                                                start=(j == 0 and a == 0 and q == 0),
                                                stop=(j == s.units - 1 and a == 1 and q == 2))
                        if j == s.units - 1:
                            ins.then_inc(acc_done, 1)
                    if j < s.units - 1:
                        ins.then_inc(unit_used, 1)

            h = (hTh, hTl)
            pe.wait_ge(h_ready, NK)
            product(SMALL, 0, True, h, NSMALL)
            pe.wait_ge(ada_ready, 1)
            for m in range(16, 48):
                ins = pe.matmul(bank[4][:, m:m + 1], ada[:, m * P:(m + 1) * P], ones[:, 0:1], start=True, stop=True)
            ins.then_inc(mod_done, 1)
            product(QI, 0, True, h)
            product(KV, 0, True, h)
            with pe.Fori(0, Q.blocks) as b:
                product(Q, b, True, h)
            with pe.Fori(0, XBC.blocks) as b:
                product(XBC, b, False, h)
            product(Z, 0, True, h)
            with pe.Fori(1, Z.blocks) as b:
                product(Z, b, True, h)
            with pe.Fori(0, GATES.blocks) as b:
                product(GATES, b, False, h)
            if stop <= 1:
                return

            pe.wait_ge(prep_done, 1)
            pe.wait_ge(mod_out, 1)
            pe.wait_ge(stg_full, 32)
            for n in range(17):
                if n >= 4:
                    pe.wait_ge(tp_free, n - 3)
                for t in range(NT):
                    src = qk[:, t, n * P:(n + 1) * P] if n < 8 else \
                        kdup[:, t, n - 8].rearrange("p e d -> p (e d)") if n < 12 else \
                        qit[:, t, (n - 12) * P:(n - 11) * P] if n < 16 else kidup[:, t].rearrange("p e d -> p (e d)")
                    ins = pe.transpose(bank[4 + n % 4][:, t * P:(t + 1) * P], src, ident[:])
                ins.then_inc(tp_done, 1)
            pe.wait_ge(ad_done, 1)
            pe.matmul(bank[0][:, 0:P], tri[:], ysq[:, 128:256], start=True, stop=True).then_inc(acs_done, 1)
            pe.wait_ge(acs_cp, 1)
            for t in range(NT):
                ins = pe.transpose(bank[1][0:SSD_H, t * P:(t + 1) * P], acs[:, t], ident[:])
            ins.then_inc(acsT_tp, 1)
            pe.wait_ge(tp_free, 17)
            for i in range(NT):
                nk = P * (i + 1)
                for h in range(IH):
                    n = IH * i + h
                    if n >= 4:
                        pe.wait_ge(rl_full, n - 3)
                    o = 64 * (h % 2)
                    pe.matmul(bank[4 + n % 4][:, 0:nk], qiT[o:o + 64, h // 2, i * P:(i + 1) * P], kiT[o:o + 64, 0:nk],
                              start=True, stop=True).then_inc(ix_done, 1)

            def weights_t(n):
                i = n // AH
                pe.wait_ge(exp_done, n + 1)
                if n >= 1:
                    pe.wait_ge(pt_evac, n)
                for kt in range(i + 1):
                    ins = pe.transpose(bank[6][:, kt * P:(kt + 1) * P], pe_[:, n % 2, kt * P:(kt + 1) * P], ident[:])
                ins.then_inc(pt_done, 1)

            def values(n):
                i, h = n // AH, n % AH
                pe.wait_ge(pt_evac, n + 1)
                if h == 0 and i:
                    pe.wait_ge(o_ready, 2 * i)
                o = bank[7 if h < 8 else 3][:, (h % 8) * DH:(h % 8 + 1) * DH]
                g = h // (AH // KVH)
                for kt in range(i + 1):
                    ins = pe.matmul(o, pts[:, n % 2, kt * P:(kt + 1) * P], vt[:, kt, g * DH:(g + 1) * DH],
                                    start=(kt == 0), stop=(kt == i))
                ins.then_inc(pv_done, 1)

            pe.wait_ge(rl_full, IH * NT)
            for i in range(NT):
                nk = P * (i + 1)
                for h in range(AH):
                    n = AH * i + h
                    if n >= 2:
                        pe.wait_ge(neg_max, n - 1)
                    o = 64 * (h % 2)
                    pe.matmul(bank[4 + n % 2][:, 0:nk], qT[o:o + 64, h // 2, i * P:(i + 1) * P],
                              kT[o:o + 64, h // (AH // KVH), 0:nk], start=True, stop=True).then_inc(s_done, 1)
                    if n >= 1:
                        weights_t(n - 1)
                    if n >= 2 and not (h == 1 and i):
                        values(n - 2)
                    if h == 0 and i:
                        values(n - 1)
                    if h == 1 and i:
                        out_t(pe, i - 1)
            weights_t(AH * NT - 1)
            values(AH * NT - 2)
            values(AH * NT - 1)
            out_t(pe, NT - 1)
            if stop <= 2:
                return

            for i in range(NT):
                cols = slice(i * P, (i + 1) * P)
                if i == 0:
                    pe.wait_ge(attn_ready, 2 * NT)
                for b in range(4):
                    if i:
                        pe.wait_ge(y_done, 8 * i)
                    for f in range(4):
                        ins = pe.transpose(bank[b][:, f * P:(f + 1) * P], xbc[:, 4 * b + f, cols], ident[:])
                    ins.then_inc(xp_done, 1)
                if i:
                    pe.wait_ge(st_used, SSD_G * i)
                for g in range(SSD_G):
                    ins = pe.transpose(bank[4][:, g * P:(g + 1) * P], xbc[:, NY + g, cols], ident[:])
                ins.then_inc(b_done, 1)
                for g in range(SSD_G):
                    ins = pe.matmul(bank[5][:, g * P:(g + 1) * P], xbc[:, NY + g, cols], xbc[:, NY + SSD_G + g, cols],
                                    start=True, stop=True)
                ins.then_inc(cb_done, 1)
                for g in range(SSD_G):
                    c = slice(512 * g, 512 * g + 512)
                    pe.wait_ge(m_ready, SSD_G * i + g + 1)
                    if i or g:
                        pe.wait_ge(y_used, SSD_G * i + g)
                    if i:
                        pe.matmul(bank[6][:], xbc[:, NY + SSD_G + g, cols], st[:, c], start=True, stop=True)
                    for q in range(8):
                        hh = 8 * g + q
                        ins = pe.matmul(bank[7][:, q * SSD_P:(q + 1) * SSD_P], seg[:, hh],
                                        xd[:, hh * SSD_P:(hh + 1) * SSD_P], start=True, stop=True)
                    ins.then_inc(yo_done, 1)
                if i < NT - 1:
                    pe.wait_ge(b_copied, i + 1)
                    for g in range(SSD_G):
                        if g >= 2:
                            pe.wait_ge(st_used, SSD_G * i + g - 1)
                        pe.matmul(bank[4 + g % 2][:], btok[:, g], xdd[:, 512 * g:512 * g + 512], start=True,
                                  stop=True).then_inc(st_mm, 1)
                pe.wait_ge(yn_done, 2 * i + 2)
                for b in range(4):
                    for f in range(4):
                        ins = pe.transpose(bank[b][:, f * P:(f + 1) * P], yt[:, (4 * b + f) * P:(4 * b + f + 1) * P], ident[:])
                    ins.then_inc(yt_done, 1)
            if stop <= 3:
                return

            pe.wait_ge(y_done, 8 * NT)
            with_wait = lambda sem_, n0: (lambda k: pe.wait_ge(sem_, n0 + k + 1))
            for b in range(2):
                product(BR_S, b, False, (yh, yl), rhs_wait=with_wait(y_split, 0) if b == 0 else None)
            for b in range(2):
                product(BR_A, b, False, (ah, al), rhs_wait=with_wait(a_split, 0) if b == 0 else None)
            for b in range(2):
                product(OUT, b, False, (mh, ml), rhs_wait=with_wait(m_split, 0) if b == 0 else None)
            for k in range(NK):
                pe.wait_ge(sq_done, NK + k + 1)
                ins = pe.matmul(bank[5][:], ones[:], sq2[:, k], start=(k == 0), stop=(k == NK - 1))
            ins.then_inc(ssq_done, 1)
            for b in range(2):
                product(PQ, b, False, h_pair, rhs_wait=with_wait(h_ready, NK) if b == 0 else None)
            if stop <= 4:
                return

            pe.wait_ge(sk_in, 32)
            pe.wait_ge(acc_free, 4 * (PQ.b1 - 8))
            for i in range(NT):
                for q in range(4):
                    if i:
                        pe.wait_ge(sc_full, 4 * (i - 1) + q + 1)
                    for h in range(2):
                        hh = 2 * q + h
                        ins = pe.matmul(bank[q][:, 256 * h:256 * h + 256], pqT[:, hh, i * P:(i + 1) * P],
                                        skbd[:, hh].rearrange("p a n -> p (a n)"), start=True, stop=True)
                    ins.then_inc(sc_done, 1)
                if i:
                    picks_t(pe, i - 1)
            picks_t(pe, NT - 1)

            def gate_tiles(c, first):
                for n in range(16):
                    pe.wait_ge(oh_made, c * 16 + (n + 1))
                    if not (first and n < 2):
                        pe.wait_ge(w_evac, c * 16 + (n - 1))
                    for q in range(4):
                        r = (4 * n + q) % 8
                        ins = pe.matmul(bank[5 + n % 2][:, q * P:(q + 1) * P], oh2[:, r], oh1[:, r], start=True, stop=True)
                    ins.then_inc(w_done, 1)
            gate_tiles(0, True)
            with pe.Fori(1, NTC // 2) as c:
                gate_tiles(c, False)

            def group(g, first):
                for n in range(2 * GT):
                    pe.wait_ge(lo_done, PU0 + n + 1 + g * (2 * GT))
                    up = n < GT
                    o = bank[n % 2] if up else bank[2 + n % 2]
                    if up and not (first and n < 2):
                        pe.wait_ge(gelu_done, g * GT + (n - 1))
                    if not up and not (first and n < GT + 2):
                        pe.wait_ge(added, g * GT + (n - GT - 1))
                    for k in range(NK):
                        if n == GT:
                            pe.wait_ge(act_ready, g * GT + (k + 1))
                        wh, wl = whi[:, n % 2, k * P:(k + 1) * P], wlo[:, n % 2, k * P:(k + 1) * P]
                        xh, xl = (hTh[:, k], hTl[:, k]) if up else (ach[:, k], acl[:, k])
                        for q, (x, y) in enumerate(((wh, xh), (wh, xl), (wl, xh))):
                            ins = pe.matmul(o[:], x, y, start=(k == 0 and q == 0), stop=(k == NK - 1 and q == 2))
                    ins.then_inc(up_done if up else down_done, 1)
            group(0, True)
            with pe.Fori(1, NG) as g:
                group(g, False)


IN_NAMES = ("xT", "cT", "pos", "w_ada", "b_ada", "g1", "g2", "w_in", "w_small", "conv_w", "conv_b", "dt_bias",
            "a_log", "d_skip", "g_ssd", "q_g", "k_g", "w_ssd_br", "w_attn_br", "w_out", "w_peer_q", "subkeys", "U", "V")


def lay_out(inp):
    a = {k: np.asarray(v) for k, v in inp.items()}
    col = lambda v: np.ascontiguousarray(v.reshape(-1, P).T)
    w_in = a["w_in"][0]
    o = {
        "xT": a["x"][0].T, "cT": col(a["c"][0]), "pos": col(a["positions"][0]),
        "w_ada": a["w_ada"][0], "b_ada": col(a["b_ada"][0]), "g1": col(a["g_norm1"][0]), "g2": col(a["g_norm2"][0]),
        "w_in": w_in, "w_small": np.concatenate([w_in[:, C_DT:C_DT + SSD_H], w_in[:, C_KI:C_G]], axis=1),
        "conv_w": a["conv_w"][0].reshape(CONV_K, NX, P).transpose(2, 1, 0).reshape(P, NX * CONV_K),
        "conv_b": col(a["conv_b"][0]), "dt_bias": a["dt_bias"], "a_log": a["a_log"], "d_skip": a["d_skip"],
        "g_ssd": col(a["g_ssd"][0]), "q_g": a["q_norm_g"], "k_g": a["k_norm_g"],
        "w_ssd_br": a["w_ssd_br"][0], "w_attn_br": a["w_attn_br"][0], "w_out": a["w_out"][0],
        "w_peer_q": a["w_peer_q"][0],
        "subkeys": a["peer_subkeys"][0].transpose(1, 3, 0, 2).reshape(P, PH * NKEYS),
        "U": a["peer_u"][0].reshape(NKEYS, P, NK, P).transpose(0, 3, 2, 1).reshape(NKEYS, P, NK * P),
        "V": a["peer_v"][0].reshape(NG, GT, P, NK, P).transpose(0, 3, 2, 1, 4).reshape(NG * NK, P, GT * P),
    }
    return {k: np.ascontiguousarray(v) for k, v in o.items()}


def kernel(**inputs):
    import concourse.bacc as bacc
    from concourse.bass_utils import run_bass_kernel_spmd

    arrays = lay_out(inputs)
    nc = bacc.Bacc("TRN2", target_bir_lowering=False, num_devices=1)
    aps = {n: nc.dram_tensor(n, arrays[n].shape, mybir.dt.from_np(arrays[n].dtype), kind="ExternalInput").ap()
           for n in IN_NAMES}
    aps["out"] = nc.dram_tensor("out", (D, T), mybir.dt.float32, kind="ExternalOutput").ap()
    build(nc, aps)
    r = run_bass_kernel_spmd(nc, [arrays], core_ids=[0])
    return np.ascontiguousarray(r.results[0]["out"].T)[None]
```

```python
from contextlib import ExitStack

import numpy as np

import concourse.bass as bass
from concourse import mybir

P = 128
T, D = 512, 1024
NT, NK = T // P, D // P
CHUNK = 64
EPS = 1e-6
NEG = -1e30
SSD_H, SSD_P, SSD_G, SSD_N = 32, 64, 4, 128
D_SSD = SSD_H * SSD_P
NY = D_SSD // P
NX = (D_SSD + 2 * SSD_G * SSD_N) // P
CONV_K = 4
AH, KVH, DH = 16, 4, 64
IH = 8
TOPK = 128
ROT = 8
ROPE_THETA = 500000.0
PH, PK, NKEYS = 8, 16, 128
C_Z, C_XBC, C_DT = 0, 2048, 5120
C_Q, C_K, C_QI, C_KI, C_G = 5152, 6176, 6688, 7200, 7272
NSMALL = SSD_H + 64 + IH
CW = 512
GT = 8
NG = NKEYS // GT
TC = 32
NTC = T // TC
NUP = NKEYS
ROUTE = 12
GATE0 = NT * ROUTE
GATE1 = GATE0 + 4
TAIL0 = GATE1 + T // 8
TAIL1 = NUP - 4
TWO_PI = 2 * np.pi
C1 = 6.28125
C2 = float(np.float32(int((TWO_PI - C1) * 2 ** 21) / 2 ** 21))
C3 = float(np.float32(TWO_PI - C1 - C2))
MAGIC = 12582912.0
PI_F = 3.1415925


class Steps:

    def __init__(self, eng, sem):
        self.eng, self.sem, self.n, self.off = eng, sem, 0, 0

    def __call__(self, ins):
        ins.then_inc(self.sem, 1)
        self.n += 1
        return ins

    def wait(self):
        self.eng.wait_ge(self.sem, self.n + self.off)

    def enter(self, i, per):
        self.start, self.per, self.off = self.n, per, i * per

    def leave(self, count):
        assert self.n - self.start == self.per, (self.n - self.start, self.per)
        self.n, self.off = self.start + self.per * count, 0


class Section:

    def __init__(self, before, blocks, units):
        self.blocks, self.units = blocks, units
        self.u0 = before.u1 if before else 0
        self.b0 = before.b1 if before else 0
        self.p0 = before.p1 if before else 0
        self.u1 = self.u0 + blocks * units
        self.b1 = self.b0 + blocks
        self.p1 = self.p0 + blocks * (units - 1)


def sections():
    small = Section(None, 1, 4)
    qi = Section(small, 1, 4)
    kv = Section(qi, 1, 4)
    q = Section(kv, 2, 4)
    xbc = Section(q, 6, 4)
    z = Section(xbc, 4, 4)
    gates = Section(z, 4, 4)
    br_s = Section(gates, 2, 8)
    br_a = Section(br_s, 2, 4)
    out = Section(br_a, 2, 4)
    pq = Section(out, 2, 4)
    return small, qi, kv, q, xbc, z, gates, br_s, br_a, out, pq


def build(nc, A, stop=99):
    F, R, U32, I32 = mybir.dt.float32, mybir.dt.float32r, mybir.dt.uint32, mybir.dt.int32
    ALU, ACT, AX = mybir.AluOpType, mybir.ActivationFunctionType, mybir.AxisListType
    SMALL, QI, KV, Q, XBC, Z, GATES, BR_S, BR_A, OUT, PQ = sections()
    PU0 = PQ.u1
    BASE = 16512
    KB = 1024

    def at(name, shape, dt, kb):
        return nc.alloc_sbuf_tensor_at(name, shape, dt, offset=BASE + int(kb * KB))

    xT = at("xT", [P, NK, T], F, 0)
    hTh = at("hTh", [P, NK, T], R, 16)
    hTl = at("hTl", [P, NK, T], R, 32)
    raw = at("raw", [P, 4, 1024], F, 48)
    whi = at("whi", [P, 2, 1024], R, 64)
    wlo = at("wlo", [P, 2, 1024], R, 72)
    cpos = [80 * KB]

    def const(name, shape, dt=F):
        n = 4 * int(np.prod(shape[1:]))
        t = nc.alloc_sbuf_tensor_at(name, shape, dt, offset=BASE + cpos[0])
        cpos[0] += (n + 31) // 32 * 32
        assert cpos[0] <= 88 * KB, name
        return t

    ident = const("ident", [P, P])
    ones = const("ones", [P, P])
    tri = const("tri", [P, P])
    iota = const("iota", [P, P])
    iota16 = const("iota16", [P, PK])
    mod = const("mod", [P, 48])
    cT = const("cT", [P, NK])
    bada = const("bada", [P, 48])
    g1 = const("g1", [P, NK])
    g2 = const("g2", [P, NK])
    a1 = const("a1", [P, NK])
    a2 = const("a2", [P, NK])
    convw = const("convw", [P, NX, CONV_K])
    convb = const("convb", [P, NX])
    gssd = const("gssd", [P, NY])
    dtb = const("dtb", [P, SSD_H])
    alog = const("alog", [P, SSD_H])
    dskip = const("dskip", [P, SSD_H])
    qg = const("qg", [P, DH])
    kg = const("kg", [P, DH])
    posi = const("posi", [P, NT], I32)
    posf = const("posf", [P, NT])
    cosT = const("cosT", [P, NT, ROT])
    sinT = const("sinT", [P, NT, ROT])
    dt = const("dt", [P, NT, SSD_H])
    acs = const("acs", [P, NT, SSD_H])
    eacs = const("eacs", [P, NT, SSD_H])
    wi = const("wi", [P, NT, IH])

    R0 = 88
    ada = at("ada", [P, 6 * D], F, R0)
    adar = at("adar", [P, 4, 2048], F, R0 + 24)
    sq = at("sq", [P, NK, T], F, R0 + 56)
    hf = at("hf", [P, NK, T], F, R0 + 72)
    rms = at("rms", [P, 2, T], F, R0 + 88)
    adat = at("adat", [P, 2048], F, R0 + 92)
    xbc = at("xbc", [P, NX, T], F, R0)
    qk = at("qk", [P, NT, 1280], F, R0 + 48)
    qit = at("qit", [P, NT, 576], F, R0 + 68)
    vt = at("vt", [P, NT, 256], F, R0 + 77)
    craw = at("craw", [P, 4, T], F, R0 + 81)
    cacc = at("cacc", [P, 4, T], F, R0 + 89)
    stg = at("stg", [P, 2, 4, CW], F, R0 + 97)
    qT = at("qT", [P, 8, T], F, 16)
    kT = at("kT", [P, 4, T], F, 32)
    qiT = at("qiT", [P, 4, T], F, 40)
    kdup = at("kdup", [P, NT, KVH, 2, DH], F, R0 + 81)
    kidup = at("kidup", [P, NT, 2, DH], F, R0 + 89)
    kiT = at("kiT", [P, T], F, R0 + 91)
    prep = at("prep", [P, NT, 1280], F, R0 + 93)
    score = at("score", [P, T], F, R0 + 93)
    work = at("work", [P, T], F, R0 + 95)
    mb = at("mb", [P, 4, T], F, R0 + 97)
    rl = at("rl", [P, 4, T], F, R0 + 105)
    pm = at("pm", [P, 2, T], F, R0 + 113)
    pe_ = at("pexp", [P, 2, T], F, R0 + 81)
    pts = at("pts", [P, 2, T], F, R0 + 85)
    otok = at("otok", [P, AH * DH], F, R0 + 64)
    zer = at("zer", [P, T], F, R0 + 68)
    eqm = at("eqm", [P, T], F, R0 + 70)
    cum = at("cum", [P, T], F, R0 + 72)
    selm = at("selm", [P, T], F, R0 + 74)
    asm = at("asm", [P, 3, AH], F, R0 + 89)
    tk8 = at("tk8", [P, 16], F, R0 + 90)
    attnT = at("attnT", [P, NK, T], F, R0 + 48)
    st = at("st", [P, D_SSD], F, 16)
    seg = at("seg", [P, SSD_H, P], F, 24)
    zc = at("zc", [P, D_SSD], F, 40)
    cbm = at("cbm", [P, SSD_G, P], F, R0 + 64)
    btok = at("btok", [P, SSD_G, P], F, R0 + 66)
    ytmp = at("ytmp", [P, T], F, R0 + 68)
    xd = at("xd", [P, D_SSD], F, R0 + 72)
    xsk = at("xsk", [P, D_SSD], F, R0 + 80)
    xdd = at("xdd", [P, D_SSD], F, R0 + 88)
    yt = at("yt", [P, D_SSD], F, R0 + 96)
    ysq = at("ysq", [P, T], F, R0 + 104)
    ssm = at("ssm", [P, 6, SSD_H], F, R0 + 106)
    acsT = at("acsT", [SSD_H, T], F, R0 + 108)
    yh = at("yh", [P, NY, T], R, 16)
    yl = at("yl", [P, NY, T], R, R0 + 64)
    ah = at("ah", [P, NK, T], R, R0)
    al = at("al", [P, NK, T], R, R0 + 16)
    mg = at("mg", [P, NK, T], F, R0 + 32)
    mh = at("mh", [P, NK, T], R, R0 + 96)
    ml = at("ml", [P, NK, T], R, R0 + 48)
    gring = at("gring", [P, 2, T], F, R0 + 112)
    mtmp = at("mtmp", [P, T], F, R0 + 116)
    sq2 = at("sq2", [P, NK, T], F, R0)
    hf2 = at("hf2", [P, NK, T], F, R0 + 16)
    rms2 = at("rms2", [P, 2, T], F, R0 + 64)
    pqT = at("pqT", [P, PH, T], F, R0 + 32)
    sc = at("sc", [P, NT, PH, 2, NKEYS], F, R0)
    skbd = at("skbd", [P, PH, 2, NKEYS], F, R0 + 48)
    cand = at("cand", [P, PH, PK, PK], F, R0 + 56)
    eqa = at("eqa", [P, PH, PK, PK], F, R0 + 64)
    v8 = at("v8", [P, PH, 2, PK], F, R0 + 72)
    i8 = at("i8", [P, PH, 2, PK], U32, R0 + 73)
    if8 = at("if8", [P, PH, 2, PK], F, R0 + 74)
    sv = at("sv", [P, PH, PK], F, R0 + 75)
    ci = at("ci", [P, PH, PK], U32, R0 + 75.5)
    cab = at("cab", [P, 2, PH, PK], U32, R0 + 76)
    cabf = at("cabf", [P, 2, PH, PK], F, R0 + 77)
    sel = at("sel", [P, 3, PH * PK], F, R0 + 78)
    gsm = at("gsm", [P, 2, PH], F, R0 + 79.5)
    oh1 = at("oh1", [P, 16, 2, P], R, R0)
    oh2 = at("oh2", [P, 16, P], R, R0 + 16)
    selT = at("selT", [P, 3, T], F, R0 + 92)
    ghl = at("ghl", [P, 2, T], R, R0 + 98)
    gst = at("gst", [P, 2, NKEYS, TC], F, R0 + 32)
    acc = at("acc", [P, NK, T], F, R0)
    ach = at("ach", [P, 2, GT, T], R, R0 + 16)
    acl = at("acl", [P, 2, GT, T], R, R0 + 48)
    ain = at("ain", [P, GT, T], F, R0 + 80)
    gg = at("gg", [P, NTC, GT, TC], F, R0 + 96)
    gel = at("gel", [P, 2, T], F, R0 + 112)

    z_d = nc.dram_tensor("z_scratch", (NT, P, D_SSD), F, kind="Internal").ap()
    g_d = nc.dram_tensor("gates_scratch", (16, P, T), F, kind="Internal").ap()
    acs_d = nc.dram_tensor("acs_scratch", (SSD_H, T), F, kind="Internal").ap()
    a_d = nc.dram_tensor("activations_scratch", (NUP, P, T), F, kind="Internal").ap()
    w_d = nc.dram_tensor("expert_gates_scratch", (NTC, P, NKEYS * TC), F, kind="Internal").ap()

    ctx = ExitStack()
    with ctx:
        bank = [ctx.enter_context(nc.psum_tensor(f"bank{i}", [P, 512], F)) for i in range(8)]

        def sem(name):
            return ctx.enter_context(nc.semaphore(name))

        raw_full = [sem(f"raw_full{i}") for i in range(4)]
        consts_in = sem("consts_in")
        x_in = sem("x_in")
        ada_in = [sem(f"ada_in{i}") for i in range(4)]
        hi_done, lo_done, unit_used = sem("hi_done"), sem("lo_done"), sem("unit_used")
        acc_done, acc_free = sem("acc_done"), sem("acc_free")
        act_step, dve_step, pool_step, pe_step = sem("act_step"), sem("dve_step"), sem("pool_step"), sem("pe_step")
        consts_made = sem("consts_made")
        cond_done, ada_v_used, ada_p_used = sem("cond_done"), sem("ada_v_used"), sem("ada_p_used")
        ada_ready, mod_done, mod_out = sem("ada_ready"), sem("mod_done"), sem("mod_out")
        sq_done, ssq_done, ms_done, rt_done = sem("sq_done"), sem("ssq_done"), sem("ms_done"), sem("rt_done")
        h_made, h_hi, h_ready = sem("h_made"), sem("h_hi"), sem("h_ready")
        craw_full, conv_done, silu_done = sem("craw_full"), sem("conv_done"), sem("silu_done")
        stg_full, stg_out = sem("stg_full"), [sem(f"stg_out{k}") for k in range(2)]
        tok_done = sem("tok_done")

        rope_arg, rope_done, qk_ms = sem("rope_arg"), sem("rope_done"), sem("qk_ms")
        qk_rt, prep_done, tp_done = sem("qk_rt"), sem("prep_done"), sem("tp_done")
        tp_free, ix_done, rl_full = sem("tp_free"), sem("ix_done"), sem("rl_full")
        rl_used, s_done, neg_max = sem("rl_used"), sem("s_done"), sem("neg_max")
        exp_done, pt_done, pt_evac = sem("exp_done"), sem("pt_done"), sem("pt_evac")
        pv_done, o_ready, ot_done = sem("pv_done"), sem("o_ready"), sem("ot_done")
        attn_ready, dt_in, sp_exp = sem("attn_ready"), sem("dt_in"), sem("sp_exp")
        sp_ln, sp_relu, ad_done = sem("sp_ln"), sem("sp_relu"), sem("ad_done")
        acs_done, acs_cp, acsT_tp = sem("acs_done"), sem("acs_cp"), sem("acsT_tp")
        acsT_ready, acsd_out, seg_in = sem("acsT_ready"), sem("acsd_out"), sem("seg_in")
        z_in, xp_done, b_done = sem("z_in"), sem("xp_done"), sem("b_done")
        b_copied, cb_done, alast_done = sem("b_copied"), sem("cb_done"), sem("alast_done")
        decay_done, segmin_done, segexp_done = sem("decay_done"), sem("segmin_done"), sem("segexp_done")
        m_ready, yo_done, y_used = sem("m_ready"), sem("yo_done"), sem("y_used")
        st_mm, st_used, ysq_done = sem("st_mm"), sem("st_used"), sem("ysq_done")
        yrt_done, yn_done, yt_done = sem("yrt_done"), sem("yn_done"), sem("yt_done")
        y_done, y_hi, y_split = sem("y_done"), sem("y_hi"), sem("y_split")
        a_split_hi, a_split, gate_used = sem("a_split_hi"), sem("a_split"), sem("gate_used")
        mg_done, m_hi, m_split = sem("mg_done"), sem("m_hi"), sem("m_split")
        x1_done, sk_in, sc_done = sem("x1_done"), sem("sk_in"), sem("sc_done")
        sc_full, sub_done = sem("sc_full"), sem("sub_done")
        gexp_done, sel_ready, selT_tp = sem("gexp_done"), sem("sel_ready"), sem("selT_tp")
        selT_done, oh_made, w_done = sem("selT_done"), sem("oh_made"), sem("w_done")
        w_evac, up_done, gelu_done = sem("w_evac"), sem("up_done"), sem("gelu_done")
        gated, act_hi, act_ready = sem("gated"), sem("act_hi"), sem("act_ready")
        down_done, added, gg_in = sem("down_done"), sem("added"), sem("gg_in")
        up_split = sem("up_split")
        ain_in, ghl_hi = sem("ain_in"), sem("ghl_hi")
        out_made, out_done = sem("out_made"), sem("out_done")
        gate_in = [sem(f"gate_in{k}") for k in range(2)]
        w_out = [sem(f"w_out{k}") for k in range(2)]
        spilled = [sem(f"spilled{k}") for k in range(2)]
        block = ctx.enter_context(nc.Block())

        def last_unit_waits(eng, s, b, j):
            if j == 1:
                if not (isinstance(b, int) and s.b0 + b == 0):
                    eng.wait_ge(acc_done, 4 * s.b0 + b * 4)
            else:
                n = s.p0 + b * (s.units - 1) + max(j - 1, 0)
                if not (isinstance(n, int) and n == 0):
                    eng.wait_ge(unit_used, n)

        def src_n(src):
            return int(np.prod(src.shape[1:]))

        def first_units(sp):
            sp.dma_start(raw[:, 0, 0:2 * NSMALL].rearrange("p (a c) -> p a c", a=2),
                         A["w_small"][0:256, :].rearrange("(a p) c -> p a c", a=2)).then_inc(raw_full[0], 16)

        def expert_free(eng, n, r=0):
            if isinstance(r, int) and n + r < 2:
                if n + r == 0:
                    eng.wait_ge(unit_used, PQ.p1)
                else:
                    eng.wait_ge(acc_done, 4 * PQ.b1)
            else:
                eng.wait_ge(up_done, r + (n - 1))

        def down_free(eng, n, r=0):
            if isinstance(r, int) and n + r < 2:
                eng.wait_ge(up_done, NUP - 1 + n + r)
            else:
                eng.wait_ge(down_done, r + (n - 1))

        def picks_evac(i):
            nc.scalar.wait_ge(selT_tp, i + 1)
            nc.scalar.activation(selT[:, :, i * P:(i + 1) * P],
                                 bank[4][:, 0:3 * P].rearrange("p (a t) -> p a t", a=3), ACT.Copy).then_inc(selT_done, 1)

        BR_S_free0 = BR_S.b0 - Z.blocks - GATES.blocks

        h_pair = (hTh, hTl)

        def out_t(pe, i):
            pe.wait_ge(o_ready, 2 * i + 2)
            for b in range(2):
                if i:
                    pe.wait_ge(attn_ready, 2 * i)
                for f in range(4):
                    ins = pe.transpose(bank[1 + b][:, f * P:(f + 1) * P], otok[:, (4 * b + f) * P:(4 * b + f + 1) * P], ident[:])
                ins.then_inc(ot_done, 1)

        def picks_t(pe, i):
            pe.wait_ge(sel_ready, i + 1)
            if i:
                pe.wait_ge(selT_done, i)
            for e in range(3):
                ins = pe.transpose(bank[4][:, e * P:(e + 1) * P], sel[:, e], ident[:])
            ins.then_inc(selT_tp, 1)

        @block.sync
        def _(sp):
            sp.dma_start(cT[:], A["cT"]).then_inc(consts_in, 16)
            for t, n in ((bada, "b_ada"), (g1, "g1"), (g2, "g2"), (convb, "conv_b"), (gssd, "g_ssd"), (posi, "pos")):
                sp.dma_start(t[:], A[n]).then_inc(consts_in, 16)
            sp.dma_start(convw[:], A["conv_w"].rearrange("p (m k) -> p m k", k=CONV_K)).then_inc(consts_in, 16)
            for t, n in ((dtb, "dt_bias"), (alog, "a_log"), (dskip, "d_skip"), (qg, "q_g"), (kg, "k_g")):
                sp.dma_start(t[:], A[n].partition_broadcast(P)).then_inc(consts_in, 16)
            wa = A["w_ada"].rearrange("(k p) n -> k p n", p=P)
            for k in range(NK):
                if k >= 2:
                    sp.wait_ge(ada_v_used, k - 1)
                sp.dma_start(adar[:, k % 2], wa[k, :, 0:2048]).then_inc(ada_in[k % 2], 16)
                if k == 1:
                    sp.dma_start(xT[:], A["xT"].rearrange("(k p) t -> p k t", p=P)).then_inc(x_in, 16)
            for n in range(2 * NK):
                k, c = n // 2, n % 2
                if n >= 2:
                    sp.wait_ge(ada_p_used, n - 1)
                sp.dma_start(adar[:, 2 + c], wa[k, :, 2048 * (c + 1):2048 * (c + 2)]).then_inc(ada_in[2 + c], 16)
                if n == 1:
                    first_units(sp)

            def load(src, s, b, j):
                u = s.u0 + j + b * s.units
                if not (isinstance(u, int) and u < 4):
                    sp.wait_ge(lo_done, u - 3)
                sp.dma_start(raw[:, j % 4, 0:src_n(src)]
                             .rearrange("p (a c) -> p a c", a=2), src).then_inc(raw_full[j % 4], 16)

            def unit_src(w, c0, n, j):
                return w[256 * j:256 * j + 256, c0:c0 + n].rearrange("(a p) c -> p a c", a=2)

            w_in = A["w_in"]
            for j in range(1, 4):
                load(unit_src(A["w_small"], 0, NSMALL, j), SMALL, 0, j)
            for s, c0 in ((QI, C_QI), (KV, C_K)):
                for j in range(4):
                    load(unit_src(w_in, c0, CW, j), s, 0, j)
            for s, c0 in ((Q, C_Q), (XBC, C_XBC), (Z, C_Z), (GATES, C_G)):
                cols = w_in[:, c0:c0 + CW * s.blocks].rearrange("(j a p) (b c) -> j p a b c", a=2, p=P, c=CW)
                with sp.Fori(0, s.blocks) as b:
                    for j in range(4):
                        load(cols[j][:, :, bass.ds(b, 1), :].rearrange("p a o c -> p a (o c)"), s, b, j)
            if stop <= 3:
                return
            for s, n in ((BR_S, "w_ssd_br"), (BR_A, "w_attn_br"), (OUT, "w_out"), (PQ, "w_peer_q")):
                cols = A[n].rearrange("(j a p) (b c) -> j p a b c", a=2, p=P, c=CW)
                with sp.Fori(0, s.blocks) as b:
                    for j in range(s.units):
                        load(cols[j][:, :, bass.ds(b, 1), :].rearrange("p a o c -> p a (o c)"), s, b, j)
            if stop <= 4:
                return
            for src, split, n0, last, n1 in ((A["U"], up_split, 0, lo_done, PU0), (A["V"], lo_done, PU0, up_split, NUP)):
                four = src.rearrange("(c j) p n -> j c p n", j=4)
                for j in range(4):
                    sp.wait_ge(last, n1 + j - 3)
                    sp.dma_start(raw[:, j, :], four[j][0]).then_inc(raw_full[j], 16)
                with sp.Fori(1, NUP // 4) as c:
                    for j in range(4):
                        sp.wait_ge(split, c * 4 + (n0 + j - 3))
                        sp.dma_start(raw[:, j, :], four[j][bass.ds(c, 1)].rearrange("o p n -> p (o n)")
                                     ).then_inc(raw_full[j], 16)
            for m in range(NK):
                sp.wait_ge(out_made, m + 1)
                sp.dma_start(A["out"][m * P:(m + 1) * P, :], xT[:, m, :]).then_inc(out_done, 16)
            sp.wait_ge(out_done, 16 * NK)

        @block.gpsimd
        def _(pool):
            step = Steps(pool, pool_step)
            pool.memset(ident[:], 0.0).then_inc(pool_step, 1)
            step.n += 1
            step(pool.memset(ones[:], 1.0))
            step(pool.memset(tri[:], 1.0))
            step.wait()
            step(pool.affine_select(out=ident[:], in_=ident[:], compare_op=ALU.not_equal, fill=1.0,
                                    base=0, pattern=[[-1, P]], channel_multiplier=1))
            step(pool.affine_select(out=tri[:], in_=tri[:], compare_op=ALU.is_ge, fill=0.0,
                                    base=0, pattern=[[1, P]], channel_multiplier=-1))
            step(pool.iota(iota[:], [[1, P]], base=0, channel_multiplier=0, allow_small_or_imprecise_dtypes=True))
            step(pool.iota(iota16[:], [[1, PK]], base=0, channel_multiplier=0, allow_small_or_imprecise_dtypes=True))
            step.wait()
            pool.sem_inc(consts_made, 1)
            pool.wait_ge(cond_done, 1)
            for n in range(2 * NK):
                k, c = n // 2, n % 2
                dst = ada[:, 2048 * (c + 1):2048 * (c + 2)]
                pool.wait_ge(ada_in[2 + c], 16 * (k + 1))
                if k == 0:
                    step(pool.tensor_scalar(dst, adar[:, 2 + c], cT[:, k:k + 1], 0.0, ALU.mult, ALU.add))
                    step.wait()
                    pool.sem_inc(ada_p_used, 1)
                else:
                    if n > 2:
                        step.wait()
                    step(pool.tensor_scalar(adat[:], adar[:, 2 + c], cT[:, k:k + 1], 0.0, ALU.mult, ALU.add))
                    step.wait()
                    pool.sem_inc(ada_p_used, 1)
                    step(pool.tensor_tensor(dst, dst, adat[:], ALU.add))
            step.wait()
            pool.sem_inc(ada_ready, 1)
            zv = z_d.rearrange("t p (b c) -> p t b c", c=CW)
            gv = g_d.rearrange("(b m) p t -> b p m t", m=4)
            for n in range(8):
                pool.wait_ge(stg_full, 4 * n + 4)
                pool.dma_start(zv[:, :, n, :] if n < 4 else gv[n - 4], stg[:, n % 2]).then_inc(stg_out[n % 2], 16)
            for k in range(2):
                pool.wait_ge(stg_out[k], 16 * 4)
            if stop <= 1:
                return
            pool.wait_ge(acsT_ready, 1)
            pool.dma_start(acs_d, acsT[:]).then_inc(acsd_out, 16)
            pool.wait_ge(acsd_out, 16)
            if stop <= 2:
                return
            pool.wait_ge(attn_ready, 2 * NT)
            for i in range(NT):
                if i:
                    pool.wait_ge(y_done, 8 * i)
                pool.dma_start(seg[:], acs_d[:, i * P:(i + 1) * P].partition_broadcast(P)).then_inc(seg_in, 16)
                pool.dma_start(zc[:], z_d[i]).then_inc(z_in, 16)
            if stop <= 3:
                return
            for n in range(16):
                if n >= 2:
                    pool.wait_ge(gate_used, n - 1)
                else:
                    pool.wait_ge(y_done, 8 * NT)
                pool.dma_start(gring[:, n % 2], g_d[n]).then_inc(gate_in[n % 2], 16)
            if stop <= 4:
                return
            pool.wait_ge(h_ready, 2 * NK)
            step(pool.memset(skbd[:], 0.0))
            step.wait()
            skv = A["subkeys"].rearrange("p (h n) -> p h n", n=NKEYS)
            for half in range(2):
                pool.dma_start(skbd[64 * half:64 * half + 64, :, half, :],
                               skv[64 * half:64 * half + 64]).then_inc(sk_in, 16)
            pool.wait_ge(sk_in, 32)

            def up_lo(n, r=0):
                pool.wait_ge(hi_done, r + (PU0 + n + 1))
                pool.tensor_tensor(wlo[:, n % 2], raw[:, n % 4], whi[:, n % 2].bitcast(F), ALU.subtract).then_inc(up_split, 1)

            wv = w_d.rearrange("c p (g n) -> p c g n", n=GT * TC)

            av = a_d.rearrange("(g e) p t -> g p e t", e=GT)

            def load_group(g):
                pool.dma_start(ain[:], av[bass.ds(g, 1)].rearrange("o p e t -> p (o e) t")).then_inc(ain_in, 16)
                pool.dma_start(gg[:].rearrange("p c e t -> p c (e t)"),
                               wv[:, :, bass.ds(g, 1), :].rearrange("p c o n -> p c (o n)")).then_inc(gg_in, 16)

            with pool.Fori(0, TAIL0 + 8, 4) as r:
                for j in range(4):
                    up_lo(j, r)
            for k in range(2):
                pool.wait_ge(w_out[k], 16 * NTC // 2)
                pool.wait_ge(spilled[k], 16 * GT // 2)
            load_group(0)
            with pool.Fori(TAIL0 + 8, NUP, 4) as r:
                for j in range(4):
                    up_lo(j, r)
            for k in range(2):
                pool.wait_ge(spilled[k], 16 * NUP // 2)
            with pool.Fori(1, NG) as g:
                pool.wait_ge(act_ready, g * GT)
                load_group(g)
            pool.wait_ge(gg_in, 16 * NG)
            pool.wait_ge(ain_in, 16 * NG)

        @block.scalar
        def _(act):
            step = Steps(act, act_step)

            def hi(s, b, j):
                u = s.u0 + j + b * s.units
                act.wait_ge(raw_full[j % 4], 16 * (s.u0 // 4 + j // 4 + 1) + b * (4 * s.units))
                last_unit_waits(act, s, b, j)
                n = 2 * NSMALL if s is SMALL else 1024
                act.activation(whi[:, j % 2, 0:n], raw[:, j % 4, 0:n], ACT.Copy).then_inc(hi_done, 1)

            def hi_next(s, b, nxt, is_last):
                if is_last:
                    if nxt is not None:
                        hi(nxt, 0, 0)
                else:
                    hi(s, b + 1, 0)

            act.wait_ge(consts_in, 16 * 13)
            step(act.activation(cT[:], cT[:], ACT.Silu))
            step.wait()
            act.sem_inc(cond_done, 1)
            act.wait_ge(x_in, 16)
            for k in range(NK):
                act.activation(sq[:, k], xT[:, k], ACT.Square).then_inc(sq_done, 1)
            act.wait_ge(ms_done, 1)
            act.activation(rms[:, 1], rms[:, 0], ACT.Sqrt).then_inc(rt_done, 1)
            hi(SMALL, 0, 0)
            for k in range(NK):
                act.wait_ge(h_made, k + 1)
                act.activation(hTh[:, k], hf[:, k], ACT.Copy).then_inc(h_hi, 1)

            def evac(s, b, t, dst, src, func=ACT.Copy, wait=True, free=True):
                if wait:
                    act.wait_ge(acc_done, 4 * s.b0 + t + 1 + b * 4)
                ins = act.activation(dst, src, func)
                if free:
                    ins.then_inc(acc_free, 1)
                return ins

            order = [SMALL, QI, KV, Q, XBC, Z, GATES]
            for j in range(1, 4):
                hi(SMALL, 0, j)
            hi(QI, 0, 0)
            for t in range(NT):
                step(evac(SMALL, 0, t, dt[:, t], bank[t][:, 0:32], free=False))
                step(evac(SMALL, 0, t, qit[:, t, 512:576], bank[t][:, 32:96], wait=False, free=False))
                evac(SMALL, 0, t, wi[:, t], bank[t][:, 96:104], wait=False)
            for s, nxt in ((QI, KV), (KV, Q)):
                for j in range(1, 4):
                    hi(s, 0, j)
                hi(nxt, 0, 0)
                for t in range(NT):
                    if s is QI:
                        evac(s, 0, t, qit[:, t, 0:512], bank[t][:])
                    else:
                        step(evac(s, 0, t, qk[:, t, 1024:1280], bank[t][:, 0:256], free=False))
                        evac(s, 0, t, vt[:, t], bank[t][:, 256:512], wait=False)
            for b in range(2):
                for j in range(1, 4):
                    hi(Q, b, j)
                hi_next(Q, b, XBC, b == 1)
                for t in range(NT):
                    evac(Q, b, t, qk[:, t, 512 * b:512 * b + 512], bank[t][:])

            def xbc_block(b, first, is_last):
                for j in range(1, 4):
                    hi(XBC, b, j)
                hi_next(XBC, b, Z, is_last)
                for t in range(4):
                    act.wait_ge(acc_done, 4 * XBC.b0 + t + 1 + b * 4)
                    if not first:
                        act.wait_ge(conv_done, b * 4 + (t - 3))
                    act.activation(craw[:, t], bank[t][:], ACT.Copy).then_inc(acc_free, 1)

            def silus(b):
                for t in range(4):
                    act.wait_ge(conv_done, b * 4 + (t + 1))
                    act.activation(xbc[:, bass.ds(b * 4 + t, 1), :], cacc[:, t:t + 1], ACT.Silu).then_inc(silu_done, 1)

            xbc_block(0, True, False)
            with act.Fori(1, XBC.blocks - 1) as b:
                xbc_block(b, False, False)
                silus(b - 1)
            xbc_block(XBC.blocks - 1, False, True)
            silus(XBC.blocks - 2)
            silus(XBC.blocks - 1)

            def staged(s, b, func, n, is_last, nxt):
                for j in range(1, 4):
                    hi(s, b, j)
                hi_next(s, b, nxt, is_last)
                if n >= 2:
                    act.wait_ge(stg_out[n % 2], 16 * (n // 2))
                for t in range(4):
                    act.wait_ge(acc_done, 4 * s.b0 + t + 1 + b * 4)
                    act.activation(stg[:, n % 2, t], bank[t][:], func).then_inc(stg_full, 1)

            for s, func, n0, nxt in ((Z, ACT.Silu, 0, GATES), (GATES, ACT.Sigmoid, 4, BR_S)):
                for b in range(4):
                    staged(s, b, func, n0 + b, b == 3, nxt if not (stop <= 3 and s is GATES) else None)
            if stop <= 1:
                return

            act.wait_ge(rope_arg, 2)
            act.activation(cosT[:], cosT[:], ACT.Sin).then_inc(rope_done, 1)
            act.activation(sinT[:], sinT[:], ACT.Sin).then_inc(rope_done, 1)
            act.wait_ge(qk_ms, 1)
            act.activation(rms[:, 1, 0:80], rms[:, 0, 0:80], ACT.Sqrt).then_inc(qk_rt, 1)
            act.wait_ge(dt_in, 1)
            step(act.activation(ysq[:, 0:128], ysq[:, 128:256], ACT.Exp, scale=-1.0))
            act.activation(alog[:], alog[:], ACT.Exp).then_inc(sp_exp, 1)
            act.wait_ge(sp_ln, 1)
            act.activation(ysq[:, 256:384], ysq[:, 256:384], ACT.Ln).then_inc(sp_relu, 1)
            for n in range(17):
                dst = qT[:, n] if n < 8 else kT[:, n - 8] if n < 12 else qiT[:, n - 12] if n < 16 else kiT[:]
                act.wait_ge(tp_done, n + 1)
                act.activation(dst, bank[4 + n % 4][:], ACT.Copy).then_inc(tp_free, 1)
            act.wait_ge(acs_done, 1)
            step(act.activation(acs[:].rearrange("p a b -> p (a b)"), bank[0][:, 0:128], ACT.Copy))
            act.activation(eacs[:].rearrange("p a b -> p (a b)"), bank[0][:, 0:128], ACT.Exp).then_inc(acs_cp, 1)
            act.wait_ge(acsT_tp, 1)
            act.activation(acsT[:], bank[1][0:SSD_H, :], ACT.Copy).then_inc(acsT_ready, 1)
            for i in range(NT):
                nk = P * (i + 1)
                if i == 0:
                    act.wait_ge(acsd_out, 16)
                for h in range(IH):
                    n = IH * i + h
                    act.wait_ge(ix_done, n + 1)
                    if n >= 4:
                        act.wait_ge(rl_used, n - 3)
                    act.activation(rl[:, n % 4, 0:nk], bank[4 + n % 4][:, 0:nk], ACT.Relu,
                                   scale=DH ** -0.5).then_inc(rl_full, 1)

            def attn_out(i):
                for b in range(2):
                    act.wait_ge(ot_done, 2 * i + b + 1)
                    act.activation(attnT[:, 4 * b:4 * b + 4, i * P:(i + 1) * P],
                                   bank[1 + b][:].rearrange("p (f t) -> p f t", f=4), ACT.Copy).then_inc(attn_ready, 1)

            for i in range(NT):
                nk = P * (i + 1)
                for h in range(AH):
                    n = AH * i + h
                    act.wait_ge(neg_max, n + 1)
                    if n >= 2:
                        act.wait_ge(pt_done, n - 1)
                    if n == 0:
                        act.wait_ge(tp_done, 17)
                    act.activation(pe_[:, n % 2, 0:nk], pm[:, n % 2, 0:nk], ACT.Exp, bias=asm[:, 0, h:h + 1],
                                   accum_out=asm[:, 1, h:h + 1]).then_inc(exp_done, 1)
                    if h == 1 and i:
                        attn_out(i - 1)
            attn_out(NT - 1)
            if stop <= 2:
                return

            for i in range(NT):
                act.wait_ge(b_done, i + 1)
                act.activation(btok[:].rearrange("p g n -> p (g n)"), bank[4][:], ACT.Copy).then_inc(b_copied, 1)
                act.wait_ge(alast_done, i + 1)
                step(act.activation(ssm[:, 1], ssm[:, 1], ACT.Exp))
                act.activation(ssm[:, 2], ssm[:, 0], ACT.Exp).then_inc(decay_done, 1)
                for g in range(SSD_G):
                    act.wait_ge(segmin_done, SSD_G * i + g + 1)
                    act.activation(seg[:, 8 * g:8 * g + 8], seg[:, 8 * g:8 * g + 8], ACT.Exp).then_inc(segexp_done, 1)
                for g in range(SSD_G):
                    act.wait_ge(y_used, SSD_G * i + g + 1)
                    step.wait()
                    step(act.activation(ysq[:], yt[:, 512 * g:512 * g + 512], ACT.Square, accum_out=ssm[:, 3, g:g + 1]))
                step.wait()
                act.sem_inc(ysq_done, 1)
                act.wait_ge(yn_done, 2 * i + 1)
                act.activation(ssm[:, 4, 0:4], ssm[:, 4, 0:4], ACT.Sqrt).then_inc(yrt_done, 1)
                for b in range(2):
                    act.wait_ge(yt_done, 4 * i + b + 1)
                    for f in range(4):
                        m = 4 * b + f
                        ins = act.activation(xbc[:, m, i * P:(i + 1) * P], bank[b][:, f * P:(f + 1) * P], ACT.Copy,
                                             scale=gssd[:, m:m + 1])
                        if f % 2 == 1:
                            ins.then_inc(y_done, 1)
                        else:
                            step(ins)
            if stop <= 3:
                return

            for k in range(NY):
                if k == 0:
                    act.wait_ge(y_done, 8 * NT)
                act.activation(yh[:, k], xbc[:, k], ACT.Copy).then_inc(y_hi, 1)
            act.wait_ge(y_split, NY)
            for k in range(NK):
                act.activation(ah[:, k], attnT[:, k], ACT.Copy).then_inc(a_split_hi, 1)

            def section_hi(s, nxt, between=None):
                for b in range(s.blocks):
                    for j in range(1, s.units):
                        hi(s, b, j)
                    hi_next(s, b, nxt, b == s.blocks - 1)
                    if between:
                        between(b)

            section_hi(BR_S, BR_A)

            def merged_hi(b):
                for t in range(4):
                    m = 4 * b + t
                    act.wait_ge(mg_done, m + 1)
                    act.activation(mh[:, m], mg[:, m], ACT.Copy).then_inc(m_hi, 1)

            section_hi(BR_A, OUT, merged_hi)
            section_hi(OUT, PQ)
            for k in range(NK):
                act.wait_ge(x1_done, k + 1)
                act.activation(sq2[:, k], xT[:, k], ACT.Square).then_inc(sq_done, 1)
            act.wait_ge(ms_done, 2)
            act.activation(rms2[:, 1], rms2[:, 0], ACT.Sqrt).then_inc(rt_done, 1)
            for k in range(NK):
                act.wait_ge(h_made, NK + k + 1)
                act.activation(hTh[:, k], hf2[:, k], ACT.Copy).then_inc(h_hi, 1)
            for b in range(PQ.blocks):
                for j in range(1, 4):
                    hi(PQ, b, j)
                if b == 0:
                    hi(PQ, 1, 0)
                elif stop > 4:
                    act.wait_ge(raw_full[0], 16 * (PU0 // 4 + 1))
                    act.wait_ge(unit_used, PQ.p1)
                    act.activation(whi[:, 0], raw[:, 0], ACT.Copy).then_inc(hi_done, 1)
                for t in range(4):
                    act.wait_ge(acc_done, 4 * (PQ.b0 + b) + t + 1)
                    act.activation(pqT[:, 4 * b + t], bank[t][:], ACT.Copy).then_inc(acc_free, 1)
            if stop <= 4:
                return

            for n in range(4 * NT):
                act.wait_ge(sc_done, n + 1)
                act.activation(sc[:, n // 4, 2 * (n % 4):2 * (n % 4) + 2].rearrange("p h a n -> p (h a n)"),
                               bank[2 + n % 2][:], ACT.Copy).then_inc(sc_full, 1)

            av = a_d.rearrange("(c j) p t -> j c p t", j=4)

            def up_hi(n, r=0):
                act.wait_ge(raw_full[n % 4], 16 * (PU0 // 4 + n // 4 + 1) + r * 4)
                expert_free(act, n, r)
                act.activation(whi[:, n % 2], raw[:, n % 4], ACT.Copy).then_inc(hi_done, 1)

            def down_hi(n, r=0):
                act.wait_ge(raw_full[n % 4], 16 * ((PU0 + NUP) // 4 + n // 4 + 1) + r * 4)
                down_free(act, n, r)
                act.activation(whi[:, n % 2], raw[:, n % 4], ACT.Copy).then_inc(hi_done, 1)

            def up_unit(n, c=0, is_last=False, first=False):
                r = c * 4
                if is_last:
                    down_hi(0)
                else:
                    up_hi(n + 1, r)
                act.wait_ge(up_done, r + (n + 1))
                if not first:
                    act.wait_ge(spilled[n % 2], 16 * (n // 2) + r * 8)
                act.activation(gel[:, n % 2], bank[n % 2][:], ACT.Gelu).then_inc(gelu_done, 1)
                act.wait_ge(gelu_done, r + (n + 1))
                act.dma_start(av[n % 4][bass.ds(c + n // 4, 1)].rearrange("o p t -> p (o t)"), gel[:, n % 2]).then_inc(spilled[n % 2], 16)

            def act_part(g, t, par):
                act.wait_ge(gated, g * GT + (t + 1))
                act.activation(ach[:, par, t], ain[:, t], ACT.Copy).then_inc(act_hi, 1)

            for i in range(NT):
                if i == 0:
                    for n in range(4):
                        up_unit(n, first=n < 2)
                with act.Fori(ROUTE // 4 * i + (1 if i == 0 else 0), ROUTE // 4 * (i + 1)) as c:
                    for n in range(4):
                        up_unit(n, c)
                act.wait_ge(sub_done, i + 1)
                act.activation(sv[:], sv[:], ACT.Exp).then_inc(gexp_done, 1)
                if i:
                    picks_evac(i - 1)
            for n in range(4):
                up_unit(GATE0 + n)
            picks_evac(NT - 1)
            act.wait_ge(selT_done, NT)
            act.activation(ghl[:, 0], selT[:, 2], ACT.Copy).then_inc(ghl_hi, 1)
            wpair = w_d.rearrange("(c k) p n -> c k p n", k=2)

            def gate_evac(c, n, first):
                k = n // 4
                if n % 4 == 0 and not first:
                    act.wait_ge(w_out[k], c * 16)
                for q in range(2):
                    act.wait_ge(w_done, c * 16 + (2 * n + q + 1))
                    c0 = 8 * (n % 4) + 4 * q
                    act.activation(gst[:, k, :, c0:c0 + 4].rearrange("p e t -> p t e"),
                                   bank[4 + (2 * n + q) % 4][:].rearrange("p (t e) -> p t e", t=4), ACT.Copy).then_inc(w_evac, 1)
                if n % 4 == 3:
                    act.wait_ge(w_evac, c * 16 + (2 * n + 2))
                    act.dma_start(wpair[bass.ds(c, 1), k].rearrange("o p n -> p (o n)"),
                                  gst[:, k].rearrange("p e t -> p (e t)")).then_inc(w_out[k], 16)

            for n in range(8):
                up_unit(GATE1 + n)
                gate_evac(0, n, True)
            with act.Fori(1, (TAIL0 - GATE1) // 8) as c:
                for n in range(8):
                    up_unit(n, c * 2 + GATE1 // 4)
                    gate_evac(c, n, False)
            with act.Fori(TAIL0 // 4, TAIL1 // 4) as c:
                for n in range(4):
                    up_unit(n, c)
            for t in range(GT):
                act_part(0, t, 0)
            for n in range(4):
                up_unit(TAIL1 + n, 0, is_last=n == 3)

            def down_group(g, par, first, is_last):
                for m in range(GT):
                    if not (is_last and m == GT - 1):
                        down_hi(par * GT + m + 1, (g - par) * GT)
                    if m >= 4 and not is_last:
                        if m == 4 and not first:
                            act.wait_ge(down_done, g * GT)
                        for t in (2 * (m - 4), 2 * (m - 4) + 1):
                            act_part(g + 1, t, 1 - par)

            down_group(0, 0, True, False)
            down_group(1, 1, False, False)
            with act.Fori(2, NG - 2, 2) as g:
                down_group(g, 0, False, False)
                down_group(g + 1, 1, False, False)
            down_group(NG - 2, 0, False, False)
            down_group(NG - 1, 1, False, True)

        @block.vector
        def _(dve):
            step = Steps(dve, dve_step)

            def do(ins):
                step(ins)
                step.wait()

            def lo(s, b, j):
                dve.wait_ge(hi_done, s.u0 + j + 1 + b * s.units)
                n = 2 * NSMALL if s is SMALL else 1024
                dve.tensor_tensor(wlo[:, j % 2, 0:n], raw[:, j % 4, 0:n], whi[:, j % 2, 0:n].bitcast(F),
                                  ALU.subtract).then_inc(lo_done, 1)

            def lo_next(s, b, nxt, is_last):
                if is_last:
                    if nxt is not None:
                        lo(nxt, 0, 0)
                else:
                    lo(s, b + 1, 0)

            dve.wait_ge(consts_in, 16 * 13)
            do(dve.tensor_copy(posf[:], posi[:]))
            inv = np.float32(ROPE_THETA) ** (-np.arange(0, 2 * ROT, 2, dtype=np.float32) / np.float32(2 * ROT))
            for r in range(ROT):
                step(dve.tensor_scalar(sinT[:, :, r], posf[:], float(inv[r]), None, ALU.mult))
            step.wait()
            rsc = rms[:].rearrange("p a t -> p (a t)")
            v32 = [rsc[:, 32 * n:32 * n + 32].rearrange("p (a r) -> p a r", r=ROT) for n in range(4)]
            do(dve.tensor_copy(v32[3], sinT[:]))
            for dst, turn, quarter in ((sinT, 0.0, 0.0), (cosT, 0.25, float(np.pi / 2))):
                do(dve.tensor_scalar(v32[0], v32[3], 1 / TWO_PI, turn, ALU.mult, ALU.add))
                do(dve.tensor_scalar(v32[1], v32[0], MAGIC, MAGIC, ALU.add, ALU.subtract))
                do(dve.scalar_tensor_tensor(v32[2], v32[1], -C1, v32[3], ALU.mult, ALU.add))
                do(dve.scalar_tensor_tensor(v32[0], v32[1], -C2, v32[2], ALU.mult, ALU.add))
                do(dve.scalar_tensor_tensor(v32[2], v32[1], -C3, v32[0], ALU.mult, ALU.add))
                do(dve.tensor_scalar(v32[0], v32[2], quarter, PI_F, ALU.add, ALU.min))
                do(dve.tensor_scalar(dst[:], v32[0], -PI_F, None, ALU.max))
            dve.sem_inc(rope_arg, 2)

            dve.wait_ge(cond_done, 1)
            for k in range(NK):
                dve.wait_ge(ada_in[k % 2], 16 * (k // 2 + 1))
                if k == 0:
                    ins = dve.tensor_scalar(ada[:, 0:2048], adar[:, 0], cT[:, 0:1], None, ALU.mult)
                else:
                    dve.wait_ge(ada_v_used, k)
                    ins = dve.scalar_tensor_tensor(ada[:, 0:2048], adar[:, k % 2], cT[:, k:k + 1], ada[:, 0:2048],
                                                   ALU.mult, ALU.add)
                ins.then_inc(ada_v_used, 1)
            dve.wait_ge(mod_done, 1)
            do(dve.tensor_tensor(mod[:, 0:16], bank[4][:, 0:16], bada[:, 0:16], ALU.add))
            do(dve.scalar_tensor_tensor(a1[:], mod[:, 8:16], 1.0, g1[:], ALU.add, ALU.mult))
            dve.wait_ge(ssq_done, 1)
            dve.tensor_scalar(rms[:, 0], bank[5][:], 1.0 / D, EPS, ALU.mult, ALU.add).then_inc(ms_done, 1)
            dve.wait_ge(rt_done, 1)
            do(dve.reciprocal(rms[:, 0], rms[:, 1]))
            for k in range(NK):
                do(dve.tensor_tensor(hf[:, k], xT[:, k], rms[:, 0], ALU.mult))
                dve.tensor_scalar(hf[:, k], hf[:, k], a1[:, k:k + 1], mod[:, k:k + 1], ALU.mult,
                                  ALU.add).then_inc(h_made, 1)
                if k:
                    dve.wait_ge(h_hi, k)
                    dve.tensor_tensor(hTl[:, k - 1], hf[:, k - 1], hTh[:, k - 1].bitcast(F), ALU.subtract).then_inc(h_ready, 1)
            dve.wait_ge(h_hi, NK)
            dve.tensor_tensor(hTl[:, NK - 1], hf[:, NK - 1], hTh[:, NK - 1].bitcast(F), ALU.subtract).then_inc(h_ready, 1)
            lo(SMALL, 0, 0)

            for s, nxt in ((SMALL, QI), (QI, KV), (KV, Q), (Q, XBC)):
                for b in range(s.blocks):
                    for j in range(1, 4):
                        lo(s, b, j)
                    lo_next(s, b, nxt, b == s.blocks - 1)
                if s is SMALL:
                    dve.wait_ge(mod_done, 2)
                    do(dve.tensor_tensor(mod[:, 16:48], bank[4][:, 16:48], bada[:, 16:48], ALU.add))
                    do(dve.scalar_tensor_tensor(a2[:], mod[:, 32:40], 1.0, g2[:], ALU.add, ALU.mult))
                    dve.sem_inc(mod_out, 1)

            def conv(b, t, first):
                m = b * 4 + t
                cw = [convw[:].rearrange("p m k -> p (m k)")[:, bass.ds(m * CONV_K + k, 1)] for k in range(CONV_K)]
                dve.wait_ge(acc_free, 4 * XBC.b0 + 1 + m)
                if not first:
                    dve.wait_ge(silu_done, m - 3)
                do(dve.tensor_scalar(cacc[:, t], craw[:, t], cw[3], convb[:, bass.ds(m, 1)], ALU.mult, ALU.add))
                for k in range(1, CONV_K):
                    ins = dve.scalar_tensor_tensor(cacc[:, t, k:], craw[:, t, 0:T - k], cw[3 - k], cacc[:, t, k:],
                                                   ALU.mult, ALU.add)
                    if k < CONV_K - 1:
                        do(ins)
                    else:
                        ins.then_inc(conv_done, 1)

            for j in range(1, 4):
                lo(XBC, 0, j)
            lo(XBC, 1, 0)

            def conv_block(b, is_last, first):
                for j in range(1, 4):
                    lo(XBC, b, j)
                    conv(b - 1, j - 1, first)
                lo_next(XBC, b, Z, is_last)
                conv(b - 1, 3, first)
            conv_block(1, False, True)
            with dve.Fori(2, XBC.blocks - 1) as b:
                step.enter(b - 2, 12)
                conv_block(b, False, False)
                step.leave(XBC.blocks - 3)
            conv_block(XBC.blocks - 1, True, False)
            for t in range(4):
                conv(XBC.blocks - 1, t, False)

            for s, nxt in ((Z, GATES), (GATES, BR_S)):
                for b in range(4):
                    for j in range(1, 4):
                        lo(s, b, j)
                    lo_next(s, b, nxt if not (stop <= 3 and s is GATES) else None, b == 3)
            if stop <= 1:
                return

            dve.wait_ge(silu_done, NX)
            for k in range(2):
                dve.wait_ge(stg_out[k], 16 * 4)
            q4 = qk[:].rearrange("p t (h d) -> p t h d", d=DH)
            do(dve.tensor_tensor(prep[:], qk[:], qk[:], ALU.mult))
            ssq = rms[:, 0, 0:80].rearrange("p (t h) -> p t h", h=20)
            do(dve.tensor_reduce(ssq, prep[:].rearrange("p t (h d) -> p t h d", d=DH), AX.X, ALU.add))
            dve.tensor_scalar(rms[:, 0, 0:80], rms[:, 0, 0:80], 1.0 / DH, EPS, ALU.mult, ALU.add).then_inc(qk_ms, 1)
            dtv = dt[:]
            u_, v_, w_, r_ = (ysq[:, 128 * n:128 * n + 128].rearrange("p (t h) -> p t h", h=SSD_H) for n in range(4))
            dve.wait_ge(qk_rt, 1)
            do(dve.reciprocal(rms[:, 0, 0:80], rms[:, 1, 0:80]))
            for t in range(NT):
                step(dve.tensor_tensor(q4[:, t], q4[:, t],
                                       rms[:, 0, 20 * t:20 * t + 20].unsqueeze(2).to_broadcast([P, 20, DH]), ALU.mult))
            step.wait()
            for t in range(NT):
                step(dve.tensor_tensor(q4[:, t, 0:AH], q4[:, t, 0:AH], qg[:].unsqueeze(1).to_broadcast([P, AH, DH]), ALU.mult))
                step(dve.tensor_tensor(q4[:, t, AH:], q4[:, t, AH:], kg[:].unsqueeze(1).to_broadcast([P, KVH, DH]), ALU.mult))
            step.wait()
            dve.wait_ge(rope_done, 2)
            pv = prep[:].rearrange("p t c -> p (t c)")
            qi4 = qit[:].rearrange("p t (h d) -> p t h d", d=DH)
            for x4, nh in ((q4, 20), (qi4, 9)):
                for t in range(NT):
                    cs = cosT[:, t].unsqueeze(1).to_broadcast([P, nh, ROT])
                    sn = sinT[:, t].unsqueeze(1).to_broadcast([P, nh, ROT])
                    t1, t2 = x4[:, t, :, 0:ROT], x4[:, t, :, ROT:2 * ROT]
                    s4 = [pv[:, (4 * t + k) * 160:(4 * t + k) * 160 + nh * ROT].rearrange("p (h r) -> p h r", r=ROT) for k in range(4)]
                    step(dve.tensor_tensor(s4[0], t1, cs, ALU.mult))
                    step(dve.tensor_tensor(s4[1], t2, sn, ALU.mult))
                    step(dve.tensor_tensor(s4[2], t2, cs, ALU.mult))
                    step(dve.tensor_tensor(s4[3], t1, sn, ALU.mult))
                step.wait()
                for t in range(NT):
                    t1, t2 = x4[:, t, :, 0:ROT], x4[:, t, :, ROT:2 * ROT]
                    s4 = [pv[:, (4 * t + k) * 160:(4 * t + k) * 160 + nh * ROT].rearrange("p (h r) -> p h r", r=ROT) for k in range(4)]
                    step(dve.tensor_tensor(t1, s4[0], s4[1], ALU.subtract))
                    step(dve.tensor_tensor(t2, s4[2], s4[3], ALU.add))
                step.wait()
            dve.wait_ge(silu_done, NX)
            for e in range(2):
                for t in range(NT):
                    step(dve.tensor_copy(kdup[:, t, :, e, :], q4[:, t, AH:]))
                step(dve.tensor_copy(kidup[:, :, e, :], qi4[:, :, IH]))
            step.wait()
            dve.sem_inc(prep_done, 1)

            do(dve.tensor_tensor(dtv, dtv, dtb[:].unsqueeze(1).to_broadcast([P, NT, SSD_H]), ALU.add))
            do(dve.tensor_scalar(u_, dtv, -1.0, None, ALU.mult))
            dve.tensor_tensor(v_, u_, dtv, ALU.max).then_inc(dt_in, 1)
            dve.wait_ge(sp_exp, 1)
            do(dve.tensor_scalar(w_, u_, 1.0, None, ALU.add))
            do(dve.tensor_scalar(v_, w_, 1.0, None, ALU.is_equal))
            do(dve.scalar_tensor_tensor(r_, w_, -1.0, v_, ALU.add, ALU.add))
            dve.sem_inc(sp_ln, 1)
            dve.wait_ge(sp_relu, 1)
            do(dve.tensor_tensor(w_, w_, v_, ALU.add))
            do(dve.tensor_tensor(w_, w_, u_, ALU.mult))
            do(dve.reciprocal(r_, r_))
            do(dve.tensor_tensor(w_, w_, r_, ALU.mult))
            do(dve.scalar_tensor_tensor(dtv, dtv, 0.0, w_, ALU.max, ALU.add))
            dve.scalar_tensor_tensor(v_, dtv, -1.0, alog[:].unsqueeze(1).to_broadcast([P, NT, SSD_H]), ALU.mult,
                                     ALU.mult).then_inc(ad_done, 1)
            dve.wait_ge(tp_done, 17)
            dve.wait_ge(acs_done, 1)
            do(dve.memset(zer[:], 0.0))
            do(dve.tensor_scalar(wi[:], wi[:], IH ** -0.5, None, ALU.mult))

            for i in range(NT):
                nk = P * (i + 1)
                for h in range(IH):
                    n = IH * i + h
                    dve.wait_ge(rl_full, n + 1)
                    if h == 0:
                        ins = dve.tensor_scalar(score[:, 0:nk], rl[:, n % 4, 0:nk], wi[:, i, h:h + 1], None, ALU.mult)
                    else:
                        dve.wait_ge(rl_used, n)
                        ins = dve.scalar_tensor_tensor(score[:, 0:nk], rl[:, n % 4, 0:nk], wi[:, i, h:h + 1],
                                                       score[:, 0:nk], ALU.mult, ALU.add)
                    ins.then_inc(rl_used, 1)
                dve.wait_ge(rl_used, IH * i + IH)
                m = mb[:, i, 0:nk]
                if i == 0:
                    step(dve.memset(m, 0.0))
                    step.wait()
                    do(dve.memset(mb[0:CHUNK, 0, CHUNK:nk], NEG))
                    continue
                do(dve.memset(score[0:CHUNK, nk - CHUNK:nk], NEG))
                for r in range(TOPK // 8):
                    src = score if r == 0 else work
                    do(dve.max(tk8[:, 0:8], src[:, 0:nk]))
                    if r < TOPK // 8 - 1:
                        do(dve.match_replace(work[:, 0:nk], tk8[:, 0:8], src[:, 0:nk], -3e38))
                do(dve.tensor_scalar(selm[:, 0:nk], score[:, 0:nk], tk8[:, 7:8], 0.0, ALU.is_gt, ALU.add,
                                     accum_out=tk8[:, 8:9]))
                do(dve.tensor_scalar(eqm[:, 0:nk], score[:, 0:nk], tk8[:, 7:8], None, ALU.is_equal))
                do(dve.tensor_tensor_scan(cum[:, 0:nk], eqm[:, 0:nk], zer[:, 0:nk], 0.0, ALU.add, ALU.add))
                do(dve.tensor_scalar(tk8[:, 9:10], tk8[:, 8:9], -1.0, float(TOPK), ALU.mult, ALU.add))
                do(dve.scalar_tensor_tensor(cum[:, 0:nk], cum[:, 0:nk], tk8[:, 9:10], eqm[:, 0:nk], ALU.is_le, ALU.mult))
                do(dve.tensor_tensor(selm[:, 0:nk], selm[:, 0:nk], cum[:, 0:nk], ALU.add))
                do(dve.tensor_scalar(m, selm[:, 0:nk], -1.0, -NEG, ALU.add, ALU.mult))

            def pt_copy(n):
                i = n // AH
                nk = P * (i + 1)
                dve.wait_ge(pt_done, n + 1)
                if n >= 2:
                    dve.wait_ge(pv_done, n - 1)
                dve.tensor_copy(pts[:, n % 2, 0:nk], bank[6][:, 0:nk]).then_inc(pt_evac, 1)

            for i in range(NT):
                nk = P * (i + 1)
                for h in range(AH):
                    n = AH * i + h
                    dve.wait_ge(s_done, n + 1)
                    if n >= 2:
                        dve.wait_ge(exp_done, n - 1)
                    do(dve.tensor_tensor_reduce(out=pm[:, n % 2, 0:nk], in0=bank[4 + n % 2][:, 0:nk], in1=mb[:, i, 0:nk],
                                                scale=DH ** -0.5, scalar=-3e38, op0=ALU.add, op1=ALU.max,
                                                accum_out=asm[:, 2, h:h + 1]))
                    if h == 0 and i:
                        dve.wait_ge(exp_done, n)
                    dve.tensor_scalar(asm[:, 0, h:h + 1], asm[:, 2, h:h + 1], -1.0, None, ALU.mult).then_inc(neg_max, 1)
                    if h:
                        pt_copy(n - 1)
                pt_copy(AH * i + AH - 1)
                dve.wait_ge(exp_done, AH * i + AH)
                do(dve.reciprocal(asm[:, 2], asm[:, 1]))
                dve.wait_ge(pv_done, AH * i + AH)
                if i:
                    dve.wait_ge(ot_done, 2 * i)
                for b in range(2):
                    dve.tensor_tensor(otok[:, 512 * b:512 * b + 512].rearrange("p (h d) -> p h d", d=DH),
                                      bank[7 if b == 0 else 3][:].rearrange("p (h d) -> p h d", d=DH),
                                      asm[:, 2, 8 * b:8 * b + 8].unsqueeze(2).to_broadcast([P, 8, DH]),
                                      ALU.mult).then_inc(o_ready, 1)
                dve.wait_ge(o_ready, 2 * i + 2)
            if stop <= 2:
                return

            dve.wait_ge(attn_ready, 2 * NT)
            do(dve.memset(st[:], 0.0))

            def bc(x, n=SSD_P):
                return x.unsqueeze(2).to_broadcast([P, x.shape[1], n])

            for i in range(NT):
                dve.wait_ge(seg_in, 16 * (i + 1))
                do(dve.tensor_copy(ssm[:, 0], seg[:, :, P - 1]))
                dve.tensor_tensor(ssm[:, 1], ssm[:, 0], acs[:, i], ALU.subtract).then_inc(alast_done, 1)
                for h in range(SSD_H):
                    ins = dve.tensor_scalar(seg[:, h], seg[:, h], acs[:, i, h:h + 1], 0.0, ALU.subtract, ALU.min)
                    if h % 8 == 7:
                        ins.then_inc(segmin_done, 1)
                    else:
                        step(ins)
                for b in range(4):
                    dve.wait_ge(xp_done, 4 * i + b + 1)
                    pv_ = bank[b][:].rearrange("p (h d) -> p h d", d=SSD_P)
                    step(dve.tensor_tensor(xd[:, 512 * b:512 * b + 512].rearrange("p (h d) -> p h d", d=SSD_P), pv_,
                                           bc(dt[:, i, 8 * b:8 * b + 8]), ALU.mult))
                    step(dve.tensor_tensor(xsk[:, 512 * b:512 * b + 512].rearrange("p (h d) -> p h d", d=SSD_P), pv_,
                                           bc(dskip[:, 8 * b:8 * b + 8]), ALU.mult))
                dve.wait_ge(cb_done, i + 1)
                do(dve.tensor_tensor(cbm[:], bank[5][:].rearrange("p (g l) -> p g l", g=SSD_G),
                                     tri[:].unsqueeze(1).to_broadcast([P, SSD_G, P]), ALU.mult))
                dve.wait_ge(decay_done, i + 1)
                do(dve.tensor_tensor(xdd[:].rearrange("p (h d) -> p h d", d=SSD_P),
                                     xd[:].rearrange("p (h d) -> p h d", d=SSD_P), bc(ssm[:, 1]), ALU.mult))
                for g in range(SSD_G):
                    dve.wait_ge(segexp_done, SSD_G * i + g + 1)
                    dve.tensor_tensor(seg[:, 8 * g:8 * g + 8], seg[:, 8 * g:8 * g + 8],
                                      cbm[:, g].unsqueeze(1).to_broadcast([P, 8, P]), ALU.mult).then_inc(m_ready, 1)
                dve.wait_ge(z_in, 16 * (i + 1))
                for g in range(SSD_G):
                    c = slice(512 * g, 512 * g + 512)
                    dve.wait_ge(yo_done, SSD_G * i + g + 1)
                    if i:
                        do(dve.tensor_tensor(ytmp[:].rearrange("p (h d) -> p h d", d=SSD_P),
                                             bank[6][:].rearrange("p (h d) -> p h d", d=SSD_P),
                                             bc(eacs[:, i, 8 * g:8 * g + 8]), ALU.mult))
                        do(dve.tensor_tensor(xsk[:, c], xsk[:, c], ytmp[:], ALU.add))
                    do(dve.tensor_tensor(yt[:, c], bank[7][:], xsk[:, c], ALU.add))
                    dve.tensor_tensor(yt[:, c], yt[:, c], zc[:, c], ALU.mult).then_inc(y_used, 1)
                dve.wait_ge(yo_done, SSD_G * i + SSD_G)
                if i < NT - 1:
                    do(dve.tensor_tensor(st[:].rearrange("p (h d) -> p h d", d=SSD_P),
                                         st[:].rearrange("p (h d) -> p h d", d=SSD_P), bc(ssm[:, 2]), ALU.mult))
                    for g in range(SSD_G):
                        c = slice(512 * g, 512 * g + 512)
                        dve.wait_ge(st_mm, SSD_G * i + g + 1)
                        dve.tensor_tensor(st[:, c], st[:, c], bank[4 + g % 2][:], ALU.add).then_inc(st_used, 1)
                dve.wait_ge(ysq_done, i + 1)
                dve.tensor_scalar(ssm[:, 4, 0:4], ssm[:, 3, 0:4], 1.0 / 512, EPS, ALU.mult, ALU.add).then_inc(yn_done, 1)
                dve.wait_ge(yrt_done, i + 1)
                do(dve.reciprocal(ssm[:, 5, 0:4], ssm[:, 4, 0:4]))
                for g in range(SSD_G):
                    c = slice(512 * g, 512 * g + 512)
                    step(dve.tensor_scalar(yt[:, c], yt[:, c], ssm[:, 5, g:g + 1], None, ALU.mult))
                step.wait()
                dve.sem_inc(yn_done, 1)
                for b in range(2, 4):
                    dve.wait_ge(yt_done, 4 * i + b + 1)
                    for f in range(4):
                        m = 4 * b + f
                        ins = dve.tensor_scalar(xbc[:, m, i * P:(i + 1) * P], bank[b][:, f * P:(f + 1) * P],
                                                gssd[:, m:m + 1], None, ALU.mult)
                        if f % 2 == 1:
                            ins.then_inc(y_done, 1)
                        else:
                            step(ins)
            if stop <= 3:
                return

            for k in range(NY):
                dve.wait_ge(y_hi, k + 1)
                if k == 0:
                    dve.wait_ge(y_done, 8 * NT)
                dve.tensor_tensor(yl[:, k], xbc[:, k], yh[:, k].bitcast(F), ALU.subtract).then_inc(y_split, 1)
            for k in range(NK):
                dve.wait_ge(a_split_hi, k + 1)
                dve.tensor_tensor(al[:, k], attnT[:, k], ah[:, k].bitcast(F), ALU.subtract).then_inc(a_split, 1)

            def section_lo(s, nxt, after):
                for b in range(s.blocks):
                    for j in range(1, s.units):
                        lo(s, b, j)
                    lo_next(s, b, nxt, b == s.blocks - 1)
                    for t in range(4):
                        dve.wait_ge(acc_done, 4 * (s.b0 + b) + t + 1)
                        after(4 * b + t, t)

            def ssd_gate(m, t):
                dve.wait_ge(gate_in[m % 2], 16 * (m // 2 + 1))
                dve.tensor_tensor(mg[:, m], bank[t][:], gring[:, m % 2], ALU.mult).then_inc(acc_free, 1)
                dve.wait_ge(acc_free, 4 * BR_S_free0 + m + 1)
                dve.sem_inc(gate_used, 1)

            def attn_gate(m, t):
                dve.wait_ge(gate_in[m % 2], 16 * (NK // 2 + m // 2 + 1))
                dve.tensor_tensor(mtmp[:], bank[t][:], gring[:, m % 2], ALU.mult).then_inc(acc_free, 1)
                dve.wait_ge(acc_free, 4 * BR_S_free0 + NK + m + 1)
                dve.sem_inc(gate_used, 1)
                dve.tensor_tensor(mg[:, m], mg[:, m], mtmp[:], ALU.add).then_inc(mg_done, 1)
                dve.wait_ge(m_hi, m + 1)
                if m == 0:
                    dve.wait_ge(a_split, NK)
                dve.tensor_tensor(ml[:, m], mg[:, m], mh[:, m].bitcast(F), ALU.subtract).then_inc(m_split, 1)

            def residual(m, t):
                dve.scalar_tensor_tensor(xT[:, m], bank[t][:], mod[:, 16 + m:17 + m], xT[:, m], ALU.mult,
                                         ALU.add).then_inc(acc_free, 1)
                dve.wait_ge(acc_free, 4 * BR_S_free0 + 2 * NK + m + 1)
                dve.sem_inc(x1_done, 1)

            section_lo(BR_S, BR_A, ssd_gate)
            section_lo(BR_A, OUT, attn_gate)
            section_lo(OUT, PQ, residual)
            dve.wait_ge(ssq_done, 2)
            dve.tensor_scalar(rms2[:, 0], bank[5][:], 1.0 / D, EPS, ALU.mult, ALU.add).then_inc(ms_done, 1)
            dve.wait_ge(rt_done, 2)
            do(dve.reciprocal(rms2[:, 0], rms2[:, 1]))
            for k in range(NK):
                do(dve.tensor_tensor(hf2[:, k], xT[:, k], rms2[:, 0], ALU.mult))
                dve.tensor_scalar(hf2[:, k], hf2[:, k], a2[:, k:k + 1], mod[:, 24 + k:25 + k], ALU.mult,
                                  ALU.add).then_inc(h_made, 1)
                if k:
                    dve.wait_ge(h_hi, NK + k)
                    dve.tensor_tensor(hTl[:, k - 1], hf2[:, k - 1], hTh[:, k - 1].bitcast(F), ALU.subtract).then_inc(h_ready, 1)
            dve.wait_ge(h_hi, 2 * NK)
            dve.tensor_tensor(hTl[:, NK - 1], hf2[:, NK - 1], hTh[:, NK - 1].bitcast(F), ALU.subtract).then_inc(h_ready, 1)
            for b in range(PQ.blocks):
                for j in range(1, 4):
                    lo(PQ, b, j)
                if b == 0:
                    lo(PQ, 1, 0)
            if stop <= 4:
                return
            for i in range(NT):
                dve.wait_ge(sc_full, 4 * i + 4)
                for h in range(PH):
                    for e in range(2):
                        row = sc[:, i, h, e]
                        do(dve.max(v8[:, h, e, 0:8], row))
                        step(dve.max_index(i8[:, h, e, 0:8], v8[:, h, e, 0:8], row))
                        step.wait()
                        do(dve.match_replace(row, v8[:, h, e, 0:8], row, -3e38))
                        do(dve.max(v8[:, h, e, 8:16], row))
                        step(dve.max_index(i8[:, h, e, 8:16], v8[:, h, e, 8:16], row))
                step.wait()
                step(dve.tensor_copy(if8[:], i8[:]))
                for h in range(PH):
                    step(dve.tensor_tensor(cand[:, h], v8[:, h, 0].unsqueeze(2).to_broadcast([P, PK, PK]),
                                           v8[:, h, 1].unsqueeze(1).to_broadcast([P, PK, PK]), ALU.add))
                step.wait()
                for h in range(PH):
                    row = cand[:, h].rearrange("p a b -> p (a b)")
                    do(dve.max(sv[:, h, 0:8], row))
                    step(dve.max_index(ci[:, h, 0:8], sv[:, h, 0:8], row))
                    step.wait()
                    do(dve.match_replace(row, sv[:, h, 0:8], row, -3e38))
                    do(dve.max(sv[:, h, 8:16], row))
                    step(dve.max_index(ci[:, h, 8:16], sv[:, h, 8:16], row))
                step.wait()
                do(dve.tensor_copy(gsm[:, 0], sv[:, :, 0]))
                dve.tensor_tensor(sv[:], sv[:], gsm[:, 0].unsqueeze(2).to_broadcast([P, PH, PK]),
                                  ALU.subtract).then_inc(sub_done, 1)
                step(dve.tensor_scalar(cab[:, 0], ci[:], 4, None, ALU.logical_shift_right))
                step(dve.tensor_scalar(cab[:, 1], ci[:], 15, None, ALU.bitwise_and))
                step.wait()
                do(dve.tensor_copy(cabf[:], cab[:]))
                if i:
                    dve.wait_ge(selT_tp, i)
                for e in range(2):
                    do(dve.tensor_tensor(eqa[:].rearrange("p h k j -> p (h k) j"),
                                         cabf[:, e].rearrange("p h k -> p (h k)").unsqueeze(2).to_broadcast([P, P, PK]),
                                         iota16[:].unsqueeze(1).to_broadcast([P, P, PK]), ALU.is_equal))
                    for h in range(PH):
                        step(dve.tensor_tensor(eqa[:, h], eqa[:, h], if8[:, h, e].unsqueeze(1).to_broadcast([P, PK, PK]), ALU.mult))
                    step.wait()
                    do(dve.tensor_reduce(sel[:, e], eqa[:].rearrange("p h k j -> p (h k) j"), AX.X, ALU.add))
                dve.wait_ge(gexp_done, i + 1)
                do(dve.tensor_reduce(gsm[:, 0], sv[:], AX.X, ALU.add))
                do(dve.reciprocal(gsm[:, 1], gsm[:, 0]))
                dve.tensor_tensor(sel[:, 2].rearrange("p (h k) -> p h k", k=PK), sv[:],
                                  gsm[:, 1].unsqueeze(2).to_broadcast([P, PH, PK]), ALU.mult).then_inc(sel_ready, 1)
                dve.wait_ge(sel_ready, i + 1)
            dve.wait_ge(ghl_hi, 1)
            do(dve.tensor_tensor(ghl[:, 1], selT[:, 2], ghl[:, 0].bitcast(F), ALU.subtract))

            def onehots(c, first):
                sT = selT[:].rearrange("p a t -> p (a t)")
                gT = ghl[:].rearrange("p a t -> p (a t)").bitcast(F)
                for n in range(2 * TC):
                    q = n % 16
                    if n % 4 == 0 and not (first and n < 16):
                        dve.wait_ge(w_done, c * 16 + (n // 4 - 3))
                    t = c * 64 + n
                    for e in range(2):
                        step(dve.tensor_scalar(oh1[:, q, e], iota[:], sT[:, bass.ds(t, 1)],
                                               gT[:, bass.ds(t + e * T, 1)], ALU.is_equal, ALU.mult))
                    ins = dve.tensor_scalar(oh2[:, q], iota[:], sT[:, bass.ds(t + T, 1)], None, ALU.is_equal)
                    if n % 4 == 3:
                        ins.then_inc(oh_made, 1)
                    else:
                        step(ins)
            onehots(0, True)
            with dve.Fori(1, NTC // 2) as c:
                onehots(c, False)
            step.n += (NTC // 2 - 2) * (2 * 2 * TC + 3 * TC // 2)

            dve.wait_ge(w_done, T // 4)
            do(dve.memset(acc[:], 0.0))

            def gate_tiles(g, ts, par):
                for t in ts:
                    dve.tensor_tensor(ain[:, t].rearrange("p (c t) -> p c t", t=TC),
                                      ain[:, t].rearrange("p (c t) -> p c t", t=TC), gg[:, :, t, :],
                                      ALU.mult).then_inc(gated, 1)
                for t in ts:
                    dve.wait_ge(act_hi, g * GT + (t + 1))
                    dve.tensor_tensor(acl[:, par, t], ain[:, t], ach[:, par, t].bitcast(F), ALU.subtract).then_inc(act_ready, 1)

            for t in range(0, GT, 2):
                if t == 0:
                    dve.wait_ge(ain_in, 16)
                    dve.wait_ge(gg_in, 16)
                gate_tiles(0, (t, t + 1), 0)

            def down_lo(n, r=0):
                dve.wait_ge(hi_done, r + (PU0 + NUP + n + 1))
                dve.tensor_tensor(wlo[:, n % 2], raw[:, n % 4], whi[:, n % 2].bitcast(F), ALU.subtract).then_inc(lo_done, 1)

            def down_group(g, par, first, is_last):
                for m in range(GT):
                    if not (is_last and m == GT - 1):
                        down_lo(par * GT + m + 1, (g - par) * GT)
                    if m >= 4 and not is_last:
                        if m == 4:
                            dve.wait_ge(ain_in, 16 * (2) + g * 16)
                            dve.wait_ge(gg_in, 16 * (2) + g * 16)
                            if not first:
                                dve.wait_ge(down_done, g * GT)
                        gate_tiles(g + 1, (2 * (m - 4), 2 * (m - 4) + 1), 1 - par)
                    dve.wait_ge(down_done, g * GT + (m + 1))
                    if not first:
                        dve.wait_ge(added, g * GT + (m - GT + 1))
                    dve.tensor_tensor(acc[:, m], acc[:, m], bank[2 + m % 2][:], ALU.add).then_inc(added, 1)

            down_lo(0)
            down_group(0, 0, True, False)
            down_group(1, 1, False, False)
            with dve.Fori(2, NG - 2, 2) as g:
                down_group(g, 0, False, False)
                down_group(g + 1, 1, False, False)
            down_group(NG - 2, 0, False, False)
            down_group(NG - 1, 1, False, True)
            for m in range(NK):
                dve.wait_ge(added, GT * (NG - 1) + m + 1)
                dve.scalar_tensor_tensor(xT[:, m], acc[:, m], mod[:, 40 + m:41 + m], xT[:, m], ALU.mult,
                                         ALU.add).then_inc(out_made, 1)

        @block.tensor
        def _(pe):
            step = Steps(pe, pe_step)
            pe.wait_ge(consts_made, 1)
            for k in range(NK):
                pe.wait_ge(sq_done, k + 1)
                ins = pe.matmul(bank[5][:], ones[:], sq[:, k], start=(k == 0), stop=(k == NK - 1))
            ins.then_inc(ssq_done, 1)
            pe.wait_ge(ada_v_used, NK)
            for m in range(16):
                ins = pe.matmul(bank[4][:, m:m + 1], ada[:, m * P:(m + 1) * P], ones[:, 0:1], start=True, stop=True)
            ins.then_inc(mod_done, 1)

            def free_wait(s, b, t):
                if s is Z or s is GATES:
                    n = (0 if s is Z else 4)
                    if s is Z and isinstance(b, int) and b == 0:
                        pe.wait_ge(acc_free, 4 * (Z.b0 - 1) + t + 1)
                    else:
                        pe.wait_ge(stg_full, 4 * (n - 1) + t + 1 + b * 4)
                elif s is BR_S and b == 0:
                    pe.wait_ge(stg_full, 28 + t + 1)
                else:
                    base = s.b0 if s.b0 < Z.b0 else s.b0 - 8
                    n = 4 * (base - 1) + t + 1 + b * 4
                    if not (isinstance(n, int) and n <= 0):
                        pe.wait_ge(acc_free, n)

            def product(s, b, token_major, mov, ncols=CW, rhs_wait=None):
                mh_, ml_ = mov
                for j in range(s.units):
                    pe.wait_ge(lo_done, s.u0 + j + 1 + b * s.units)
                    wh = whi[:, j % 2, 0:2 * ncols].rearrange("p (a c) -> p a c", a=2)
                    wl = wlo[:, j % 2, 0:2 * ncols].rearrange("p (a c) -> p a c", a=2)
                    for t in range(4):
                        if j == 0:
                            free_wait(s, b, t)
                        for a in range(2):
                            k = 2 * j + a
                            if rhs_wait and t == 0:
                                rhs_wait(k)
                            if token_major:
                                ht, lt = mh_[:, k, t * P:(t + 1) * P], ml_[:, k, t * P:(t + 1) * P]
                                three = ((ht, wh[:, a]), (ht, wl[:, a]), (lt, wh[:, a]))
                            else:
                                wht, wlt = wh[:, a, t * P:(t + 1) * P], wl[:, a, t * P:(t + 1) * P]
                                three = ((wht, mh_[:, k]), (wht, ml_[:, k]), (wlt, mh_[:, k]))
                            for q, (x, y) in enumerate(three):
                                ins = pe.matmul(bank[t][:, 0:ncols] if token_major else bank[t][:], x, y,
                                                start=(j == 0 and a == 0 and q == 0),
                                                stop=(j == s.units - 1 and a == 1 and q == 2))
                        if j == s.units - 1:
                            ins.then_inc(acc_done, 1)
                    if j < s.units - 1:
                        ins.then_inc(unit_used, 1)

            h = (hTh, hTl)
            pe.wait_ge(h_ready, NK)
            product(SMALL, 0, True, h, NSMALL)
            pe.wait_ge(ada_ready, 1)
            for m in range(16, 48):
                ins = pe.matmul(bank[4][:, m:m + 1], ada[:, m * P:(m + 1) * P], ones[:, 0:1], start=True, stop=True)
            ins.then_inc(mod_done, 1)
            product(QI, 0, True, h)
            product(KV, 0, True, h)
            with pe.Fori(0, Q.blocks) as b:
                product(Q, b, True, h)
            with pe.Fori(0, XBC.blocks) as b:
                product(XBC, b, False, h)
            product(Z, 0, True, h)
            with pe.Fori(1, Z.blocks) as b:
                product(Z, b, True, h)
            with pe.Fori(0, GATES.blocks) as b:
                product(GATES, b, False, h)
            if stop <= 1:
                return

            pe.wait_ge(prep_done, 1)
            pe.wait_ge(mod_out, 1)
            pe.wait_ge(stg_full, 32)
            for n in range(17):
                if n >= 4:
                    pe.wait_ge(tp_free, n - 3)
                for t in range(NT):
                    src = qk[:, t, n * P:(n + 1) * P] if n < 8 else \
                        kdup[:, t, n - 8].rearrange("p e d -> p (e d)") if n < 12 else \
                        qit[:, t, (n - 12) * P:(n - 11) * P] if n < 16 else kidup[:, t].rearrange("p e d -> p (e d)")
                    ins = pe.transpose(bank[4 + n % 4][:, t * P:(t + 1) * P], src, ident[:])
                ins.then_inc(tp_done, 1)
            pe.wait_ge(ad_done, 1)
            pe.matmul(bank[0][:, 0:P], tri[:], ysq[:, 128:256], start=True, stop=True).then_inc(acs_done, 1)
            pe.wait_ge(acs_cp, 1)
            for t in range(NT):
                ins = pe.transpose(bank[1][0:SSD_H, t * P:(t + 1) * P], acs[:, t], ident[:])
            ins.then_inc(acsT_tp, 1)
            pe.wait_ge(tp_free, 17)
            for i in range(NT):
                nk = P * (i + 1)
                for h in range(IH):
                    n = IH * i + h
                    if n >= 4:
                        pe.wait_ge(rl_full, n - 3)
                    o = 64 * (h % 2)
                    pe.matmul(bank[4 + n % 4][:, 0:nk], qiT[o:o + 64, h // 2, i * P:(i + 1) * P], kiT[o:o + 64, 0:nk],
                              start=True, stop=True).then_inc(ix_done, 1)

            def weights_t(n):
                i = n // AH
                pe.wait_ge(exp_done, n + 1)
                if n >= 1:
                    pe.wait_ge(pt_evac, n)
                for kt in range(i + 1):
                    ins = pe.transpose(bank[6][:, kt * P:(kt + 1) * P], pe_[:, n % 2, kt * P:(kt + 1) * P], ident[:])
                ins.then_inc(pt_done, 1)

            def values(n):
                i, h = n // AH, n % AH
                pe.wait_ge(pt_evac, n + 1)
                if h == 0 and i:
                    pe.wait_ge(o_ready, 2 * i)
                o = bank[7 if h < 8 else 3][:, (h % 8) * DH:(h % 8 + 1) * DH]
                g = h // (AH // KVH)
                for kt in range(i + 1):
                    ins = pe.matmul(o, pts[:, n % 2, kt * P:(kt + 1) * P], vt[:, kt, g * DH:(g + 1) * DH],
                                    start=(kt == 0), stop=(kt == i))
                ins.then_inc(pv_done, 1)

            pe.wait_ge(rl_full, IH * NT)
            for i in range(NT):
                nk = P * (i + 1)
                for h in range(AH):
                    n = AH * i + h
                    if n >= 2:
                        pe.wait_ge(neg_max, n - 1)
                    o = 64 * (h % 2)
                    pe.matmul(bank[4 + n % 2][:, 0:nk], qT[o:o + 64, h // 2, i * P:(i + 1) * P],
                              kT[o:o + 64, h // (AH // KVH), 0:nk], start=True, stop=True).then_inc(s_done, 1)
                    if n >= 1:
                        weights_t(n - 1)
                    if n >= 2 and not (h == 1 and i):
                        values(n - 2)
                    if h == 0 and i:
                        values(n - 1)
                    if h == 1 and i:
                        out_t(pe, i - 1)
            weights_t(AH * NT - 1)
            values(AH * NT - 2)
            values(AH * NT - 1)
            out_t(pe, NT - 1)
            if stop <= 2:
                return

            for i in range(NT):
                cols = slice(i * P, (i + 1) * P)
                if i == 0:
                    pe.wait_ge(attn_ready, 2 * NT)
                for b in range(4):
                    if i:
                        pe.wait_ge(y_done, 8 * i)
                    for f in range(4):
                        ins = pe.transpose(bank[b][:, f * P:(f + 1) * P], xbc[:, 4 * b + f, cols], ident[:])
                    ins.then_inc(xp_done, 1)
                if i:
                    pe.wait_ge(st_used, SSD_G * i)
                for g in range(SSD_G):
                    ins = pe.transpose(bank[4][:, g * P:(g + 1) * P], xbc[:, NY + g, cols], ident[:])
                ins.then_inc(b_done, 1)
                for g in range(SSD_G):
                    ins = pe.matmul(bank[5][:, g * P:(g + 1) * P], xbc[:, NY + g, cols], xbc[:, NY + SSD_G + g, cols],
                                    start=True, stop=True)
                ins.then_inc(cb_done, 1)
                for g in range(SSD_G):
                    c = slice(512 * g, 512 * g + 512)
                    pe.wait_ge(m_ready, SSD_G * i + g + 1)
                    if i or g:
                        pe.wait_ge(y_used, SSD_G * i + g)
                    if i:
                        pe.matmul(bank[6][:], xbc[:, NY + SSD_G + g, cols], st[:, c], start=True, stop=True)
                    for q in range(8):
                        hh = 8 * g + q
                        ins = pe.matmul(bank[7][:, q * SSD_P:(q + 1) * SSD_P], seg[:, hh],
                                        xd[:, hh * SSD_P:(hh + 1) * SSD_P], start=True, stop=True)
                    ins.then_inc(yo_done, 1)
                if i < NT - 1:
                    pe.wait_ge(b_copied, i + 1)
                    for g in range(SSD_G):
                        if g >= 2:
                            pe.wait_ge(st_used, SSD_G * i + g - 1)
                        pe.matmul(bank[4 + g % 2][:], btok[:, g], xdd[:, 512 * g:512 * g + 512], start=True,
                                  stop=True).then_inc(st_mm, 1)
                pe.wait_ge(yn_done, 2 * i + 2)
                for b in range(4):
                    for f in range(4):
                        ins = pe.transpose(bank[b][:, f * P:(f + 1) * P], yt[:, (4 * b + f) * P:(4 * b + f + 1) * P], ident[:])
                    ins.then_inc(yt_done, 1)
            if stop <= 3:
                return

            pe.wait_ge(y_done, 8 * NT)
            with_wait = lambda sem_, n0: (lambda k: pe.wait_ge(sem_, n0 + k + 1))
            for b in range(2):
                product(BR_S, b, False, (yh, yl), rhs_wait=with_wait(y_split, 0) if b == 0 else None)
            for b in range(2):
                product(BR_A, b, False, (ah, al), rhs_wait=with_wait(a_split, 0) if b == 0 else None)
            for b in range(2):
                product(OUT, b, False, (mh, ml), rhs_wait=with_wait(m_split, 0) if b == 0 else None)
            for k in range(NK):
                pe.wait_ge(sq_done, NK + k + 1)
                ins = pe.matmul(bank[5][:], ones[:], sq2[:, k], start=(k == 0), stop=(k == NK - 1))
            ins.then_inc(ssq_done, 1)
            for b in range(2):
                product(PQ, b, False, h_pair, rhs_wait=with_wait(h_ready, NK) if b == 0 else None)
            if stop <= 4:
                return

            pe.wait_ge(sk_in, 32)
            pe.wait_ge(acc_free, 4 * (PQ.b1 - 8))
            for n in range(4 * NT):
                i = n // 4
                if n >= 2:
                    pe.wait_ge(sc_full, n - 1)
                for h in range(2):
                    hh = 2 * (n % 4) + h
                    ins = pe.matmul(bank[2 + n % 2][:, 256 * h:256 * h + 256], pqT[:, hh, i * P:(i + 1) * P],
                                    skbd[:, hh].rearrange("p a n -> p (a n)"), start=True, stop=True)
                ins.then_inc(sc_done, 1)

            def three_pass(o, slot, xh, xl, wait=None):
                for k in range(NK):
                    if wait:
                        wait(k)
                    wh, wl = whi[:, slot, k * P:(k + 1) * P], wlo[:, slot, k * P:(k + 1) * P]
                    for q, (x, y) in enumerate(((wh, xh(k)), (wh, xl(k)), (wl, xh(k)))):
                        ins = pe.matmul(o[:], x, y, start=(k == 0 and q == 0), stop=(k == NK - 1 and q == 2))
                return ins

            def up_unit(n, r=0, first=False):
                pe.wait_ge(up_split, r + (n + 1))
                if not first:
                    pe.wait_ge(gelu_done, r + (n - 1))
                three_pass(bank[n % 2], n % 2, lambda k: hTh[:, k], lambda k: hTl[:, k]).then_inc(up_done, 1)

            def gate_banks(c, n, first):
                for q in range(2):
                    i = 2 * n + q
                    pe.wait_ge(oh_made, c * 16 + (i + 1))
                    if not (first and i < 4):
                        pe.wait_ge(w_evac, c * 16 + (i - 3))
                    for k in range(4):
                        s = (4 * i + k) % 16
                        for e in range(2):
                            ins = pe.matmul(bank[4 + i % 4][:, k * P:(k + 1) * P], oh2[:, s], oh1[:, s, e],
                                            start=(e == 0), stop=(e == 1))
                    ins.then_inc(w_done, 1)

            for i in range(NT):
                if i == 0:
                    for n in range(4):
                        up_unit(n, first=n < 2)
                with pe.Fori(ROUTE * i + (4 if i == 0 else 0), ROUTE * (i + 1), 4) as r:
                    for n in range(4):
                        up_unit(n, r)
                if i:
                    picks_t(pe, i - 1)
            for n in range(4):
                up_unit(GATE0 + n)
            picks_t(pe, NT - 1)
            pe.wait_ge(selT_done, NT)
            for n in range(8):
                up_unit(GATE1 + n)
                gate_banks(0, n, True)
            with pe.Fori(1, (TAIL0 - GATE1) // 8) as c:
                for n in range(8):
                    up_unit(n, c * 8 + GATE1)
                    gate_banks(c, n, False)
            with pe.Fori(TAIL0, NUP, 4) as r:
                for n in range(4):
                    up_unit(n, r)

            def down_group(g, par, first):
                for m in range(GT):
                    pe.wait_ge(lo_done, g * GT + (PU0 + m + 1))
                    if first and m < 2:
                        pe.wait_ge(sc_full, 4 * NT)
                    else:
                        pe.wait_ge(added, g * GT + (m - 1))
                    three_pass(bank[2 + m % 2], m % 2, lambda k: ach[:, par, k], lambda k: acl[:, par, k],
                               (lambda k: pe.wait_ge(act_ready, g * GT + (k + 1))) if m == 0 else None
                               ).then_inc(down_done, 1)

            down_group(0, 0, True)
            down_group(1, 1, False)
            with pe.Fori(2, NG, 2) as g:
                down_group(g, 0, False)
                down_group(g + 1, 1, False)


IN_NAMES = ("xT", "cT", "pos", "w_ada", "b_ada", "g1", "g2", "w_in", "w_small", "conv_w", "conv_b", "dt_bias",
            "a_log", "d_skip", "g_ssd", "q_g", "k_g", "w_ssd_br", "w_attn_br", "w_out", "w_peer_q", "subkeys", "U", "V")


def lay_out(inp):
    a = {k: np.asarray(v) for k, v in inp.items()}
    col = lambda v: np.ascontiguousarray(v.reshape(-1, P).T)
    w_in = a["w_in"][0]
    o = {
        "xT": a["x"][0].T, "cT": col(a["c"][0]), "pos": col(a["positions"][0]),
        "w_ada": a["w_ada"][0], "b_ada": col(a["b_ada"][0]), "g1": col(a["g_norm1"][0]), "g2": col(a["g_norm2"][0]),
        "w_in": w_in, "w_small": np.concatenate([w_in[:, C_DT:C_DT + SSD_H], w_in[:, C_KI:C_G]], axis=1),
        "conv_w": a["conv_w"][0].reshape(CONV_K, NX, P).transpose(2, 1, 0).reshape(P, NX * CONV_K),
        "conv_b": col(a["conv_b"][0]), "dt_bias": a["dt_bias"], "a_log": a["a_log"], "d_skip": a["d_skip"],
        "g_ssd": col(a["g_ssd"][0]), "q_g": a["q_norm_g"], "k_g": a["k_norm_g"],
        "w_ssd_br": a["w_ssd_br"][0], "w_attn_br": a["w_attn_br"][0], "w_out": a["w_out"][0],
        "w_peer_q": a["w_peer_q"][0],
        "subkeys": a["peer_subkeys"][0].transpose(1, 3, 0, 2).reshape(P, PH * NKEYS),
        "U": a["peer_u"][0].reshape(NKEYS, P, NK, P).transpose(0, 3, 2, 1).reshape(NKEYS, P, NK * P),
        "V": a["peer_v"][0].reshape(NG, GT, P, NK, P).transpose(0, 3, 2, 1, 4).reshape(NG * NK, P, GT * P),
    }
    return {k: np.ascontiguousarray(v) for k, v in o.items()}


def kernel(**inputs):
    import concourse.bacc as bacc
    from concourse.bass_utils import run_bass_kernel_spmd

    arrays = lay_out(inputs)
    nc = bacc.Bacc("TRN2", target_bir_lowering=False, num_devices=1)
    aps = {n: nc.dram_tensor(n, arrays[n].shape, mybir.dt.from_np(arrays[n].dtype), kind="ExternalInput").ap()
           for n in IN_NAMES}
    aps["out"] = nc.dram_tensor("out", (D, T), mybir.dt.float32, kind="ExternalOutput").ap()
    build(nc, aps)
    r = run_bass_kernel_spmd(nc, [arrays], core_ids=[0])
    return np.ascontiguousarray(r.results[0]["out"].T)[None]
```

```python
from contextlib import ExitStack

import numpy as np

import concourse.bass as bass
from concourse import mybir

P = 128
T, D = 512, 1024
NT, NK = T // P, D // P
CHUNK = 64
EPS = 1e-6
NEG = -1e30
SSD_H, SSD_P, SSD_G, SSD_N = 32, 64, 4, 128
D_SSD = SSD_H * SSD_P
NY = D_SSD // P
NX = (D_SSD + 2 * SSD_G * SSD_N) // P
CONV_K = 4
AH, KVH, DH = 16, 4, 64
IH = 8
TOPK = 128
ROT = 8
ROPE_THETA = 500000.0
PH, PK, NKEYS = 8, 16, 128
C_Z, C_XBC, C_DT = 0, 2048, 5120
C_Q, C_K, C_QI, C_KI, C_G = 5152, 6176, 6688, 7200, 7272
NSMALL = SSD_H + 64 + IH
CW = 512
GT = 8
NG = NKEYS // GT
TC = 32
NTC = T // TC
NUP = NKEYS
ROUTE = 12
GATE0 = NT * ROUTE
GATE1 = GATE0 + 4
TAIL0 = GATE1 + T // 8
TAIL1 = NUP - 4
TWO_PI = 2 * np.pi
C1 = 6.28125
C2 = float(np.float32(int((TWO_PI - C1) * 2 ** 21) / 2 ** 21))
C3 = float(np.float32(TWO_PI - C1 - C2))
MAGIC = 12582912.0
PI_F = 3.1415925


class Steps:

    def __init__(self, eng, sem):
        self.eng, self.sem, self.n, self.off = eng, sem, 0, 0

    def __call__(self, ins):
        ins.then_inc(self.sem, 1)
        self.n += 1
        return ins

    def wait(self):
        self.eng.wait_ge(self.sem, self.n + self.off)

    def enter(self, i, per):
        self.start, self.per, self.off = self.n, per, i * per

    def leave(self, count):
        assert self.n - self.start == self.per, (self.n - self.start, self.per)
        self.n, self.off = self.start + self.per * count, 0


class Section:

    def __init__(self, before, blocks, units):
        self.blocks, self.units = blocks, units
        self.u0 = before.u1 if before else 0
        self.b0 = before.b1 if before else 0
        self.p0 = before.p1 if before else 0
        self.u1 = self.u0 + blocks * units
        self.b1 = self.b0 + blocks
        self.p1 = self.p0 + blocks * (units - 1)


def sections():
    small = Section(None, 1, 4)
    qi = Section(small, 1, 4)
    kv = Section(qi, 1, 4)
    q = Section(kv, 2, 4)
    z = Section(q, 4, 4)
    gates = Section(z, 4, 4)
    xbc = Section(gates, 6, 4)
    br_s = Section(xbc, 2, 8)
    br_a = Section(br_s, 2, 4)
    out = Section(br_a, 2, 4)
    pq = Section(out, 2, 4)
    return small, qi, kv, q, z, gates, xbc, br_s, br_a, out, pq


def build(nc, A):
    F, R, U32, I32 = mybir.dt.float32, mybir.dt.float32r, mybir.dt.uint32, mybir.dt.int32
    ALU, ACT, AX = mybir.AluOpType, mybir.ActivationFunctionType, mybir.AxisListType
    SMALL, QI, KV, Q, Z, GATES, XBC, BR_S, BR_A, OUT, PQ = sections()
    PU0 = PQ.u1
    NMID = Z.blocks + GATES.blocks
    S0 = Z.u0
    BASE = 16512
    KB = 1024

    def at(name, shape, dt, kb):
        return nc.alloc_sbuf_tensor_at(name, shape, dt, offset=BASE + int(kb * KB))

    xT = at("xT", [P, NK, T], F, 0)
    hTh = at("hTh", [P, NK, T], R, 16)
    hTl = at("hTl", [P, NK, T], R, 32)
    raw = at("raw", [P, 4, 1024], F, 48)
    whi = at("whi", [P, 2, 1024], R, 64)
    wlo = at("wlo", [P, 2, 1024], R, 72)
    cpos = [80 * KB]

    def const(name, shape, dt=F):
        n = 4 * int(np.prod(shape[1:]))
        t = nc.alloc_sbuf_tensor_at(name, shape, dt, offset=BASE + cpos[0])
        cpos[0] += (n + 31) // 32 * 32
        assert cpos[0] <= 88 * KB, name
        return t

    ident = const("ident", [P, P])
    ones = const("ones", [P, P])
    tri = const("tri", [P, P])
    iota = const("iota", [P, P])
    iota16 = const("iota16", [P, PK])
    mod = const("mod", [P, 48])
    cT = const("cT", [P, NK])
    bada = const("bada", [P, 48])
    g1 = const("g1", [P, NK])
    g2 = const("g2", [P, NK])
    a1 = const("a1", [P, NK])
    a2 = const("a2", [P, NK])
    convw = const("convw", [P, NX, CONV_K])
    convb = const("convb", [P, NX])
    gssd = const("gssd", [P, NY])
    dtb = const("dtb", [P, SSD_H])
    alog = const("alog", [P, SSD_H])
    dskip = const("dskip", [P, SSD_H])
    qg = const("qg", [P, DH])
    kg = const("kg", [P, DH])
    posi = const("posi", [P, NT], I32)
    posf = const("posf", [P, NT])
    cosT = const("cosT", [P, NT, ROT])
    sinT = const("sinT", [P, NT, ROT])
    dt = const("dt", [P, NT, SSD_H])
    acs = const("acs", [P, NT, SSD_H])
    eacs = const("eacs", [P, NT, SSD_H])
    wi = const("wi", [P, NT, IH])

    R0 = 88
    ada = at("ada", [P, 6 * D], F, R0)
    adar = at("adar", [P, 2, 2048], F, R0 + 24)
    adap = at("adap", [P, 2, 2048], F, R0 + 97)
    sq = at("sq", [P, NK, T], F, R0 + 56)
    hf = at("hf", [P, NK, T], F, R0 + 72)
    rms = at("rms", [P, 2, T], F, R0 + 88)
    adat = at("adat", [P, 2048], F, R0 + 40)
    xbc = at("xbc", [P, NX, T], F, R0)
    qk = at("qk", [P, NT, 1280], F, R0 + 48)
    qit = at("qit", [P, NT, 576], F, R0 + 68)
    vt = at("vt", [P, NT, 256], F, R0 + 77)
    craw = at("craw", [P, 4, T], F, R0 + 81)
    cacc = at("cacc", [P, 4, T], F, R0 + 89)
    stg = at("stg", [P, 2, 4, CW], F, R0 + 32)
    qT = at("qT", [P, 8, T], F, R0)
    kT = at("kT", [P, 4, T], F, R0 + 16)
    qiT = at("qiT", [P, 4, T], F, R0 + 24)
    qTh = at("qTh", [P, 8, T], R, 0)
    qTl = at("qTl", [P, 8, T], R, R0)
    kTh = at("kTh", [P, 4, T], R, R0 + 24)
    kTl = at("kTl", [P, 4, T], R, R0 + 16)
    kdup = at("kdup", [P, NT, KVH, 2, DH], F, R0 + 81)
    kidup = at("kidup", [P, NT, 2, DH], F, R0 + 89)
    kiT = at("kiT", [P, T], F, R0 + 91)
    prep = at("prep", [P, NT, 1280], F, R0 + 93)
    score = at("score", [P, NT - 1, T], F, R0 + 113)
    work = at("work", [P, T], F, R0 + 95)
    mb = at("mb", [P, 4, T], F, R0 + 97)
    rl = at("rl", [P, 4, T], F, R0 + 105)
    pm = at("pm", [P, 3, T], F, R0 + 105)
    pe_ = at("pexp", [P, 3, T], F, R0 + 81)
    pts = at("pts", [P, 2, T], F, R0 + 93)
    otok = at("otok", [P, AH * DH], F, R0 + 64)
    zer = at("zer", [P, T], F, R0 + 68)
    eqm = at("eqm", [P, T], F, R0 + 70)
    cum = at("cum", [P, T], F, R0 + 72)
    selm = at("selm", [P, T], F, R0 + 74)
    asm = at("asm", [P, 3, AH], F, R0 + 89)
    tk8 = at("tk8", [P, 16], F, R0 + 90)
    attnT = at("attnT", [P, NK, T], F, R0 + 48)
    st = at("st", [P, D_SSD], F, 16)
    segs = (at("seg0", [P, SSD_H, P], F, 0),
            at("seg1", [P, SSD_H, P], F, 24))
    zc = at("zc", [P, D_SSD], F, 40)
    cbm = at("cbm", [P, SSD_G, P], F, R0 + 64)
    btok = at("btok", [P, SSD_G, P], F, R0 + 66)
    ytmp = at("ytmp", [P, T], F, R0 + 68)
    xd = at("xd", [P, D_SSD], F, R0 + 72)
    xsk = at("xsk", [P, D_SSD], F, R0 + 80)
    xdd = at("xdd", [P, D_SSD], F, R0 + 88)
    yt = at("yt", [P, D_SSD], F, R0 + 96)
    ysq = at("ysq", [P, T], F, R0 + 104)
    ssm = at("ssm", [P, 6, SSD_H], F, R0 + 106)
    acsT = at("acsT", [SSD_H, T], F, R0 + 108)
    yh = at("yh", [P, NY, T], R, 16)
    yl = at("yl", [P, NY, T], R, R0 + 64)
    ah = at("ah", [P, NK, T], R, R0)
    al = at("al", [P, NK, T], R, R0 + 16)
    mg = at("mg", [P, NK, T], F, R0 + 32)
    mh = at("mh", [P, NK, T], R, R0 + 96)
    ml = at("ml", [P, NK, T], R, R0 + 48)
    gring = at("gring", [P, 2, T], F, R0 + 112)
    mtmp = at("mtmp", [P, T], F, R0 + 116)
    sq2 = at("sq2", [P, NK, T], F, R0)
    hf2 = at("hf2", [P, NK, T], F, R0 + 16)
    rms2 = at("rms2", [P, 2, T], F, R0 + 64)
    pqT = at("pqT", [P, PH, T], F, R0 + 32)
    sc = at("sc", [P, NT, PH, 2, NKEYS], F, R0)
    skbd = at("skbd", [P, PH, 2, NKEYS], F, R0 + 48)
    cand = at("cand", [P, PH, PK, PK], F, R0 + 56)
    eqa = at("eqa", [P, PH, PK, PK], F, R0 + 64)
    v8 = at("v8", [P, PH, 2, PK], F, R0 + 72)
    i8 = at("i8", [P, PH, 2, PK], U32, R0 + 73)
    if8 = at("if8", [P, PH, 2, PK], F, R0 + 74)
    sv = at("sv", [P, PH, PK], F, R0 + 75)
    ci = at("ci", [P, PH, PK], U32, R0 + 75.5)
    cab = at("cab", [P, 2, PH, PK], U32, R0 + 76)
    cabf = at("cabf", [P, 2, PH, PK], F, R0 + 77)
    sel = at("sel", [P, 3, PH * PK], F, R0 + 78)
    gsm = at("gsm", [P, 2, PH], F, R0 + 79.5)
    oh1 = at("oh1", [P, 16, 2, P], R, R0)
    oh2 = at("oh2", [P, 16, P], R, R0 + 16)
    selT = at("selT", [P, 3, T], F, R0 + 96)
    ghl = at("ghl", [P, 2, T], R, R0 + 102)
    gst = at("gst", [P, 2, NKEYS, TC], F, R0 + 32)
    acc = at("acc", [P, NK, T], F, R0)
    ach = at("ach", [P, 2, GT, T], R, R0 + 16)
    acl = at("acl", [P, 2, GT, T], R, R0 + 48)
    ain = at("ain", [P, GT, T], F, R0 + 80)
    gg = at("gg", [P, NTC, GT, TC], F, R0 + 96)
    gel = at("gel", [P, 2, T], F, R0 + 112)

    z_d = nc.dram_tensor("z_scratch", (NT, P, D_SSD), F, kind="Internal").ap()
    g_d = nc.dram_tensor("gates_scratch", (16, P, T), F, kind="Internal").ap()
    acs_d = nc.dram_tensor("acs_scratch", (SSD_H, T), F, kind="Internal").ap()
    a_d = nc.dram_tensor("activations_scratch", (NUP, P, T), F, kind="Internal").ap()
    w_d = nc.dram_tensor("expert_gates_scratch", (NTC, P, NKEYS * TC), F, kind="Internal").ap()

    ctx = ExitStack()
    with ctx:
        bank = [ctx.enter_context(nc.psum_tensor(f"bank{i}", [P, 512], F)) for i in range(8)]

        def sem(name):
            return ctx.enter_context(nc.semaphore(name))

        raw_full = [sem(f"raw_full{i}") for i in range(4)]
        consts_in = sem("consts_in")
        x_in = sem("x_in")
        ada_in = [sem(f"ada_in{i}") for i in range(4)]
        adap_in = [sem(f"adap_in{i}") for i in range(2)]
        hi_done, lo_done, unit_used = sem("hi_done"), sem("lo_done"), sem("unit_used")
        acc_done, acc_free = sem("acc_done"), sem("acc_free")
        act_step, dve_step, pool_step, pe_step = sem("act_step"), sem("dve_step"), sem("pool_step"), sem("pe_step")
        consts_made = sem("consts_made")
        cond_done, ada_v_used = sem("cond_done"), sem("ada_v_used")
        ada_ready, mod_done, mod_out = sem("ada_ready"), sem("mod_done"), sem("mod_out")
        sq_done, ssq_done, ms_done, rt_done = sem("sq_done"), sem("ssq_done"), sem("ms_done"), sem("rt_done")
        h_made, h_hi, h_ready = sem("h_made"), sem("h_hi"), sem("h_ready")
        conv_done, silu_done = sem("conv_done"), sem("silu_done")
        stg_full, stg_out = sem("stg_full"), [sem(f"stg_out{k}") for k in range(2)]

        rope_arg, rope_done, qk_ms = sem("rope_arg"), sem("rope_done"), sem("qk_ms")
        qk_rt, prep_done, tp_done = sem("qk_rt"), sem("prep_done"), sem("tp_done")
        tp_free, ix_done, rl_full = sem("tp_free"), sem("ix_done"), sem("rl_full")
        rl_used, s_done, neg_max = sem("rl_used"), sem("s_done"), sem("neg_max")
        exp_done, pt_done, pt_evac = sem("exp_done"), sem("pt_done"), sem("pt_evac")
        pv_done, o_ready, ot_done = sem("pv_done"), sem("o_ready"), sem("ot_done")
        attn_ready, dt_in, sp_exp = sem("attn_ready"), sem("dt_in"), sem("sp_exp")
        sp_ln, sp_relu, ad_done = sem("sp_ln"), sem("sp_relu"), sem("ad_done")
        acs_done, acs_cp, acsT_tp = sem("acs_done"), sem("acs_cp"), sem("acsT_tp")
        acsT_ready, acsd_out, seg_in = sem("acsT_ready"), sem("acsd_out"), [sem(f"seg_in{k}") for k in range(2)]
        z_in, xp_done, b_done = sem("z_in"), sem("xp_done"), sem("b_done")
        b_copied, cb_done, alast_done = sem("b_copied"), sem("cb_done"), sem("alast_done")
        decay_done, segmin_done, segexp_done = sem("decay_done"), sem("segmin_done"), sem("segexp_done")
        m_ready, yo_done, y_used = sem("m_ready"), sem("yo_done"), sem("y_used")
        qk_hi, qk_split, x_again = sem("qk_hi"), sem("qk_split"), sem("x_again")
        xd_done, xdd_done, st_decayed = sem("xd_done"), sem("xdd_done"), sem("st_decayed")
        st_mm, st_used, ysq_done = sem("st_mm"), sem("st_used"), sem("ysq_done")
        yrt_done, yn_done, yt_done = sem("yrt_done"), sem("yn_done"), sem("yt_done")
        y_done, y_hi, y_split = sem("y_done"), sem("y_hi"), sem("y_split")
        a_split_hi, a_split, gate_used = sem("a_split_hi"), sem("a_split"), sem("gate_used")
        mg_done, m_hi, m_split = sem("mg_done"), sem("m_hi"), sem("m_split")
        x1_done, sk_in, sc_done = sem("x1_done"), sem("sk_in"), sem("sc_done")
        sc_full, sub_done = sem("sc_full"), sem("sub_done")
        gexp_done, sel_ready, selT_tp = sem("gexp_done"), sem("sel_ready"), sem("selT_tp")
        selT_done, oh_made, w_done = sem("selT_done"), sem("oh_made"), sem("w_done")
        w_evac, up_done, gelu_done = sem("w_evac"), sem("up_done"), sem("gelu_done")
        gated, act_hi, act_ready = sem("gated"), sem("act_hi"), sem("act_ready")
        down_done, added, gg_in = sem("down_done"), sem("added"), sem("gg_in")
        pool_split = sem("pool_split")
        ain_in, ghl_hi = sem("ain_in"), sem("ghl_hi")
        out_made, out_done = sem("out_made"), sem("out_done")
        gate_in = [sem(f"gate_in{k}") for k in range(2)]
        w_out = [sem(f"w_out{k}") for k in range(2)]
        spilled = [sem(f"spilled{k}") for k in range(2)]
        block = ctx.enter_context(nc.Block())

        def last_unit_waits(eng, s, b, j):
            if j == 1:
                if not (isinstance(b, int) and s.b0 + b == 0):
                    eng.wait_ge(acc_done, 4 * s.b0 + b * 4)
            else:
                n = s.p0 + b * (s.units - 1) + max(j - 1, 0)
                if not (isinstance(n, int) and n == 0):
                    eng.wait_ge(unit_used, n)

        def src_n(src):
            return int(np.prod(src.shape[1:]))

        def first_units(sp):
            sp.dma_start(raw[:, 0, 0:2 * NSMALL].rearrange("p (a c) -> p a c", a=2),
                         A["w_small"][0:256, :].rearrange("(a p) c -> p a c", a=2)).then_inc(raw_full[0], 16)

        def expert_free(eng, n, r=0):
            if isinstance(r, int) and n + r < 2:
                if n + r == 0:
                    eng.wait_ge(unit_used, PQ.p1)
                else:
                    eng.wait_ge(acc_done, 4 * PQ.b1)
            else:
                eng.wait_ge(up_done, r + (n - 1))

        def down_free(eng, n, r=0):
            if isinstance(r, int) and n + r < 2:
                eng.wait_ge(up_done, NUP - 1 + n + r)
            else:
                eng.wait_ge(down_done, r + (n - 1))

        def picks_evac(i):
            nc.scalar.wait_ge(selT_tp, i + 1)
            nc.scalar.activation(selT[:, :, i * P:(i + 1) * P],
                                 bank[4][:, 0:3 * P].rearrange("p (a t) -> p a t", a=3), ACT.Copy).then_inc(selT_done, 1)

        BR_S_free0 = BR_S.b0 - NMID

        h_pair = (hTh, hTl)
        sb = (4, 5, 0)
        yb = (6, 0)

        def out_t(pe, i):
            pe.wait_ge(o_ready, 2 * i + 2)
            for b in range(2):
                if i:
                    pe.wait_ge(attn_ready, 2 * i)
                for f in range(4):
                    ins = pe.transpose(bank[1 + b][:, f * P:(f + 1) * P], otok[:, (4 * b + f) * P:(4 * b + f + 1) * P], ident[:])
                ins.then_inc(ot_done, 1)

        def picks_t(pe, i):
            pe.wait_ge(sel_ready, i + 1)
            if i:
                pe.wait_ge(selT_done, i)
            for e in range(3):
                ins = pe.transpose(bank[4][:, e * P:(e + 1) * P], sel[:, e], ident[:])
            ins.then_inc(selT_tp, 1)

        @block.sync
        def _(sp):
            sp.dma_start(cT[:], A["cT"]).then_inc(consts_in, 16)
            for t, n in ((bada, "b_ada"), (g1, "g1"), (g2, "g2"), (convb, "conv_b"), (gssd, "g_ssd"), (posi, "pos")):
                sp.dma_start(t[:], A[n]).then_inc(consts_in, 16)
            sp.dma_start(convw[:], A["conv_w"].rearrange("p (m k) -> p m k", k=CONV_K)).then_inc(consts_in, 16)
            for t, n in ((dtb, "dt_bias"), (alog, "a_log"), (dskip, "d_skip"), (qg, "q_g"), (kg, "k_g")):
                sp.dma_start(t[:], A[n].partition_broadcast(P)).then_inc(consts_in, 16)
            wa = A["w_ada"].rearrange("(k p) n -> k p n", p=P)
            for k in range(NK):
                if k >= 4:
                    sp.wait_ge(ada_v_used, k - 3)
                slot = adar[:, k % 4] if k % 4 < 2 else adap[:, k % 4 - 2]
                sp.dma_start(slot, wa[k, :, 0:2048]).then_inc(ada_in[k % 4], 16)
                if k == 1:
                    sp.dma_start(xT[:], A["xT"].rearrange("(k p) t -> p k t", p=P)).then_inc(x_in, 16)
            first_units(sp)

            def load(src, s, b, j):
                if s.u0 < S0 or s is Z and isinstance(b, int):
                    if s is not SMALL:
                        sp.wait_ge(lo_done, s.u0 + j - 3 + b * s.units)
                else:
                    sp.wait_ge(pool_split, s.u0 - S0 + j - 3 + b * s.units)
                sp.dma_start(raw[:, j % 4, 0:src_n(src)]
                             .rearrange("p (a c) -> p a c", a=2), src).then_inc(raw_full[j % 4], 16)

            def unit_src(w, c0, n, j):
                return w[256 * j:256 * j + 256, c0:c0 + n].rearrange("(a p) c -> p a c", a=2)

            w_in = A["w_in"]
            for j in range(1, 4):
                load(unit_src(A["w_small"], 0, NSMALL, j), SMALL, 0, j)
            for s, c0 in ((QI, C_QI), (KV, C_K)):
                for j in range(4):
                    load(unit_src(w_in, c0, CW, j), s, 0, j)
            for s, c0 in ((Q, C_Q), (Z, C_Z), (GATES, C_G), (XBC, C_XBC)):
                cols = w_in[:, c0:c0 + CW * s.blocks].rearrange("(j a p) (b c) -> j p a b c", a=2, p=P, c=CW)
                peeled = s is Z
                if peeled:
                    for j in range(4):
                        load(unit_src(w_in, c0, CW, j), s, 0, j)
                with sp.Fori(1 if peeled else 0, s.blocks) as b:
                    for j in range(4):
                        load(cols[j][:, :, bass.ds(b, 1), :].rearrange("p a o c -> p a (o c)"), s, b, j)
            for s, n in ((BR_S, "w_ssd_br"), (BR_A, "w_attn_br"), (OUT, "w_out"), (PQ, "w_peer_q")):
                cols = A[n].rearrange("(j a p) (b c) -> j p a b c", a=2, p=P, c=CW)
                with sp.Fori(0, s.blocks) as b:
                    for j in range(s.units):
                        load(cols[j][:, :, bass.ds(b, 1), :].rearrange("p a o c -> p a (o c)"), s, b, j)
            for src in (A["U"], A["V"]):
                four = src.rearrange("(c j) p n -> j c p n", j=4)
                up = src is A["U"]
                for j in range(4):
                    sp.wait_ge(pool_split, PU0 - S0 + j - 3 + (0 if up else NUP))
                    sp.dma_start(raw[:, j, :], four[j][0]).then_inc(raw_full[j], 16)
                with sp.Fori(1, NUP // 4) as c:
                    for j in range(4):
                        if up:
                            sp.wait_ge(pool_split, c * 4 + (PU0 - S0 + j - 3))
                        else:
                            sp.wait_ge(lo_done, c * 4 + (S0 + j - 3))
                        sp.dma_start(raw[:, j, :], four[j][bass.ds(c, 1)].rearrange("o p n -> p (o n)")
                                     ).then_inc(raw_full[j], 16)
            for m in range(NK):
                sp.wait_ge(out_made, m + 1)
                sp.dma_start(A["out"][m * P:(m + 1) * P, :], xT[:, m, :]).then_inc(out_done, 16)
            sp.wait_ge(out_done, 16 * NK)

        @block.gpsimd
        def _(pool):
            step = Steps(pool, pool_step)
            pool.memset(ident[:], 0.0).then_inc(pool_step, 1)
            step.n += 1
            step(pool.memset(ones[:], 1.0))
            step(pool.memset(tri[:], 1.0))
            step.wait()
            step(pool.affine_select(out=ident[:], in_=ident[:], compare_op=ALU.not_equal, fill=1.0,
                                    base=0, pattern=[[-1, P]], channel_multiplier=1))
            step(pool.affine_select(out=tri[:], in_=tri[:], compare_op=ALU.is_ge, fill=0.0,
                                    base=0, pattern=[[1, P]], channel_multiplier=-1))
            step(pool.iota(iota[:], [[1, P]], base=0, channel_multiplier=0, allow_small_or_imprecise_dtypes=True))
            step(pool.iota(iota16[:], [[1, PK]], base=0, channel_multiplier=0, allow_small_or_imprecise_dtypes=True))
            step.wait()
            pool.sem_inc(consts_made, 1)
            wa = A["w_ada"].rearrange("(k p) n -> k p n", p=P)

            def load_ada(n):
                k, c = n // 2, n % 2
                pool.dma_start(adap[:, c], wa[k, :, 2048 * (c + 1):2048 * (c + 2)]).then_inc(adap_in[c], 16)

            pool.wait_ge(ada_v_used, NK)
            load_ada(0)
            load_ada(1)
            pool.wait_ge(cond_done, 1)
            for n in range(2 * NK):
                k, c = n // 2, n % 2
                dst = ada[:, 2048 * (c + 1):2048 * (c + 2)]
                pool.wait_ge(adap_in[c], 16 * (k + 1))
                if k == 0:
                    step(pool.tensor_scalar(dst, adap[:, c], cT[:, k:k + 1], 0.0, ALU.mult, ALU.add))
                    step.wait()
                else:
                    if n > 2:
                        step.wait()
                    step(pool.tensor_scalar(adat[:], adap[:, c], cT[:, k:k + 1], 0.0, ALU.mult, ALU.add))
                    step.wait()
                    step(pool.tensor_tensor(dst, dst, adat[:], ALU.add))
                if n + 2 < 2 * NK:
                    load_ada(n + 2)
            step.wait()
            pool.sem_inc(ada_ready, 1)
            zv = z_d.rearrange("t p (b c) -> p t b c", c=CW)
            gv = g_d.rearrange("(b m) p t -> b p m t", m=4)

            def pool_lo(n, r=0):
                pool.wait_ge(hi_done, r + (S0 + n + 1))
                pool.tensor_tensor(wlo[:, n % 2], raw[:, n % 4], whi[:, n % 2].bitcast(F),
                                   ALU.subtract).then_inc(pool_split, 1)

            pool_lo(0)
            for n in range(NMID):
                for j in range(1, 5):
                    pool_lo(4 * n + j)
                pool.wait_ge(stg_full, 4 * n + 4)
                pool.dma_start(zv[:, :, n, :] if n < 4 else gv[n - 4], stg[:, n % 2]).then_inc(stg_out[n % 2], 16)
                if n == 1:
                    pool.wait_ge(acsT_ready, 1)
                    pool.dma_start(acs_d, acsT[:]).then_inc(acsd_out, 16)
            for k in range(2):
                pool.wait_ge(stg_out[k], 16 * NMID // 2)
            pool.wait_ge(acsd_out, 16)

            def load_seg(i):
                pool.dma_start(segs[i % 2][:], acs_d[:, i * P:(i + 1) * P].partition_broadcast(P)).then_inc(seg_in[i % 2], 16)

            pool.wait_ge(s_done, AH * NT)
            load_seg(0)
            with pool.Fori(0, XBC.blocks) as b:
                for j in range(1, 5):
                    pool_lo(XBC.u0 - S0 + j, b * 4)
            pool.wait_ge(acc_done, 4 * XBC.b1)
            for i in range(NT):
                if i:
                    pool.wait_ge(y_used, SSD_G * i)
                pool.dma_start(zc[:], z_d[i]).then_inc(z_in, 16)
                if i == 0:
                    load_seg(1)
                if i == NT - 1:
                    continue
                pool.wait_ge(decay_done, i + 1)
                pool.wait_ge(xd_done, i + 1)
                pool.tensor_tensor(xdd[:].rearrange("p (h d) -> p h d", d=SSD_P),
                                   xd[:].rearrange("p (h d) -> p h d", d=SSD_P),
                                   ssm[:, 1].unsqueeze(2).to_broadcast([P, SSD_H, SSD_P]), ALU.mult).then_inc(xdd_done, 1)
                pool.wait_ge(yo_done, SSD_G * i + SSD_G)
                pool.tensor_tensor(st[:].rearrange("p (h d) -> p h d", d=SSD_P),
                                   st[:].rearrange("p (h d) -> p h d", d=SSD_P),
                                   ssm[:, 2].unsqueeze(2).to_broadcast([P, SSD_H, SSD_P]), ALU.mult).then_inc(st_decayed, 1)
                if i + 2 < NT:
                    load_seg(i + 2)
                else:
                    pool.dma_start(xT[:], A["xT"].rearrange("(k p) t -> p k t", p=P)).then_inc(x_again, 16)
            def load_gate(n):
                if n >= 2:
                    pool.wait_ge(gate_used, n - 1)
                pool.dma_start(gring[:, n % 2], g_d[n]).then_inc(gate_in[n % 2], 16)

            pool.wait_ge(y_done, 8 * NT)
            load_gate(0)
            load_gate(1)
            gate = 2
            for s in (BR_S, BR_A, OUT, PQ):
                for b in range(s.blocks):
                    for j in range(1, s.units + 1):
                        if not (s is PQ and b == s.blocks - 1 and j == s.units):
                            pool_lo(s.u0 - S0 + b * s.units + j)
                        if j == s.units or j == 1 and not (s is BR_S and b == 0):
                            for n in range(gate, min(gate + 2, 16)):
                                load_gate(n)
                            gate += 2
            pool.wait_ge(h_ready, 2 * NK)
            step(pool.memset(skbd[:], 0.0))
            step.wait()
            skv = A["subkeys"].rearrange("p (h n) -> p h n", n=NKEYS)
            for half in range(2):
                pool.dma_start(skbd[64 * half:64 * half + 64, :, half, :],
                               skv[64 * half:64 * half + 64]).then_inc(sk_in, 16)
            def up_lo(n, r=0):
                pool_lo(PU0 - S0 + n, r)

            wv = w_d.rearrange("c p (g n) -> p c g n", n=GT * TC)

            av = a_d.rearrange("(g e) p t -> g p e t", e=GT)

            def load_activations(g):
                pool.dma_start(ain[:], av[bass.ds(g, 1)].rearrange("o p e t -> p (o e) t")).then_inc(ain_in, 16)

            def load_gates(g):
                pool.dma_start(gg[:].rearrange("p c e t -> p c (e t)"),
                               wv[:, :, bass.ds(g, 1), :].rearrange("p c o n -> p c (o n)")).then_inc(gg_in, 16)

            with pool.Fori(0, TAIL0, 4) as r:
                for j in range(4):
                    up_lo(j, r)
            for k in range(2):
                pool.wait_ge(spilled[k], 16 * GT // 2)
            load_activations(0)
            for j in range(2):
                up_lo(TAIL0 + j)
            for k in range(2):
                pool.wait_ge(w_out[k], 16 * NTC // 2)
            load_gates(0)
            for j in range(2, 4):
                up_lo(TAIL0 + j)
            with pool.Fori(TAIL0 + 4, NUP, 4) as r:
                for j in range(4):
                    up_lo(j, r)
            for k in range(2):
                pool.wait_ge(spilled[k], 16 * NUP // 2)
            with pool.Fori(1, NG) as g:
                pool.wait_ge(act_ready, g * GT)
                load_activations(g)
                load_gates(g)
            pool.wait_ge(sk_in, 32)
            pool.wait_ge(gg_in, 16 * NG)
            pool.wait_ge(ain_in, 16 * NG)

        @block.scalar
        def _(act):
            step = Steps(act, act_step)

            def hi(s, b, j):
                u = s.u0 + j + b * s.units
                act.wait_ge(raw_full[j % 4], 16 * (s.u0 // 4 + j // 4 + 1) + b * (4 * s.units))
                last_unit_waits(act, s, b, j)
                n = 2 * NSMALL if s is SMALL else 1024
                act.activation(whi[:, j % 2, 0:n], raw[:, j % 4, 0:n], ACT.Copy).then_inc(hi_done, 1)

            def hi_next(s, b, nxt, is_last):
                if is_last:
                    if nxt is not None:
                        hi(nxt, 0, 0)
                else:
                    hi(s, b + 1, 0)

            act.wait_ge(consts_in, 16 * 13)
            step(act.activation(cT[:], cT[:], ACT.Silu))
            step.wait()
            act.sem_inc(cond_done, 1)
            act.wait_ge(x_in, 16)
            for k in range(NK):
                act.activation(sq[:, k], xT[:, k], ACT.Square).then_inc(sq_done, 1)
            act.wait_ge(ms_done, 1)
            act.activation(rms[:, 1], rms[:, 0], ACT.Sqrt).then_inc(rt_done, 1)
            hi(SMALL, 0, 0)
            for k in range(NK):
                act.wait_ge(h_made, k + 1)
                act.activation(hTh[:, k], hf[:, k], ACT.Copy).then_inc(h_hi, 1)

            def evac(s, b, t, dst, src, func=ACT.Copy, wait=True, free=True):
                if wait:
                    act.wait_ge(acc_done, 4 * s.b0 + t + 1 + b * 4)
                ins = act.activation(dst, src, func)
                if free:
                    ins.then_inc(acc_free, 1)
                return ins

            for j in range(1, 4):
                hi(SMALL, 0, j)
            hi(QI, 0, 0)
            for t in range(NT):
                step(evac(SMALL, 0, t, dt[:, t], bank[t][:, 0:32], free=False))
                step(evac(SMALL, 0, t, qit[:, t, 512:576], bank[t][:, 32:96], wait=False, free=False))
                evac(SMALL, 0, t, wi[:, t], bank[t][:, 96:104], wait=False)
            for s, nxt in ((QI, KV), (KV, Q)):
                for j in range(1, 4):
                    hi(s, 0, j)
                hi(nxt, 0, 0)
                for t in range(NT):
                    if s is QI:
                        evac(s, 0, t, qit[:, t, 0:512], bank[t][:])
                    else:
                        step(evac(s, 0, t, qk[:, t, 1024:1280], bank[t][:, 0:256], free=False))
                        evac(s, 0, t, vt[:, t], bank[t][:, 256:512], wait=False)
            for b in range(2):
                for j in range(1, 4):
                    hi(Q, b, j)
                hi_next(Q, b, Z, b == 1)
                for t in range(NT):
                    evac(Q, b, t, qk[:, t, 512 * b:512 * b + 512], bank[t][:])

            def staged(s, b, func, n, is_last, nxt):
                for j in range(1, 4):
                    hi(s, b, j)
                hi_next(s, b, nxt, is_last)
                if n >= 2:
                    act.wait_ge(stg_out[n % 2], 16 * (n // 2))
                for t in range(4):
                    act.wait_ge(acc_done, 4 * s.b0 + t + 1 + b * 4)
                    act.activation(stg[:, n % 2, t], bank[t][:], func).then_inc(stg_full, 1)

            def mid_block(n):
                if n < Z.blocks:
                    staged(Z, n, ACT.Silu, n, n == Z.blocks - 1, GATES)
                else:
                    staged(GATES, n - Z.blocks, ACT.Sigmoid, n, n == NMID - 1, XBC)

            act.wait_ge(rope_arg, 2)
            act.activation(cosT[:], cosT[:], ACT.Sin).then_inc(rope_done, 1)
            act.activation(sinT[:], sinT[:], ACT.Sin).then_inc(rope_done, 1)
            mid_block(0)
            act.wait_ge(qk_ms, 1)
            act.activation(rms[:, 1, 0:80], rms[:, 0, 0:80], ACT.Sqrt).then_inc(qk_rt, 1)
            mid_block(1)
            act.wait_ge(dt_in, 1)
            step(act.activation(ysq[:, 0:128], ysq[:, 128:256], ACT.Exp, scale=-1.0))
            act.activation(alog[:], alog[:], ACT.Exp).then_inc(sp_exp, 1)
            act.wait_ge(sp_ln, 1)
            act.activation(ysq[:, 256:384], ysq[:, 256:384], ACT.Ln).then_inc(sp_relu, 1)
            for n in range(17):
                dst = qT[:, n] if n < 8 else kT[:, n - 8] if n < 12 else qiT[:, n - 12] if n < 16 else kiT[:]
                act.wait_ge(tp_done, n + 1)
                act.activation(dst, bank[4 + n % 4][:], ACT.Copy).then_inc(tp_free, 1)
            act.wait_ge(acs_done, 1)
            step(act.activation(acs[:].rearrange("p a b -> p (a b)"), bank[4][:, 0:128], ACT.Copy))
            act.activation(eacs[:].rearrange("p a b -> p (a b)"), bank[4][:, 0:128], ACT.Exp).then_inc(acs_cp, 1)
            act.wait_ge(acsT_tp, 1)
            act.activation(acsT[:], bank[5][0:SSD_H, :], ACT.Copy).then_inc(acsT_ready, 1)
            act.wait_ge(acsd_out, 16)
            for i in range(1, NT):
                nk = P * (i + 1)
                for h in range(IH):
                    n = IH * (i - 1) + h
                    act.wait_ge(ix_done, n + 1)
                    if n >= 4:
                        act.wait_ge(rl_used, n - 3)
                    act.activation(rl[:, n % 4, 0:nk], bank[4 + n % 4][:, 0:nk], ACT.Relu,
                                   scale=DH ** -0.5).then_inc(rl_full, 1)
            for n in range(2, NMID):
                mid_block(n)
                if n == 2:
                    for m in range(6):
                        act.activation(qTh[:, m], qT[:, m], ACT.Copy).then_inc(qk_hi, 1)
                if n == 3:
                    for m in range(6, 8):
                        act.activation(qTh[:, m], qT[:, m], ACT.Copy).then_inc(qk_hi, 1)
                    for m in range(4):
                        act.activation(kTh[:, m], kT[:, m], ACT.Copy).then_inc(qk_hi, 1)

            def attn_out(i):
                for b in range(2):
                    act.wait_ge(ot_done, 2 * i + b + 1)
                    act.activation(attnT[:, 4 * b:4 * b + 4, i * P:(i + 1) * P],
                                   bank[1 + b][:].rearrange("p (f t) -> p f t", f=4), ACT.Copy).then_inc(attn_ready, 1)

            for i in range(NT):
                nk = P * (i + 1)
                for h in range(AH):
                    n = AH * i + h
                    act.wait_ge(neg_max, n + 1)
                    if n >= 3:
                        act.wait_ge(pt_done, n - 2)
                    if n == 0:
                        act.wait_ge(tp_done, 17)
                    act.activation(pe_[:, n % 3, 0:nk], pm[:, n % 3, 0:nk], ACT.Exp, bias=asm[:, 0, h:h + 1],
                                   accum_out=asm[:, 1, h:h + 1]).then_inc(exp_done, 1)
                    if h == 1 and i:
                        attn_out(i - 1)
            attn_out(NT - 1)
            def xbc_block(b, first, is_last):
                for j in range(1 if first else 2, 4):
                    hi(XBC, b, j)
                hi_next(XBC, b, BR_S, is_last)
                for t in range(4):
                    act.wait_ge(acc_done, 4 * XBC.b0 + t + 1 + b * 4)
                    if not first:
                        act.wait_ge(conv_done, b * 4 + (t - 3))
                    act.activation(craw[:, t], bank[t][:], ACT.Copy).then_inc(acc_free, 1)
                if not is_last:
                    hi(XBC, b + 1, 1)

            def silus(b):
                for t in range(4):
                    act.wait_ge(conv_done, b * 4 + (t + 1))
                    act.activation(xbc[:, bass.ds(b * 4 + t, 1), :], cacc[:, t:t + 1], ACT.Silu).then_inc(silu_done, 1)

            for k in range(2):
                act.wait_ge(stg_out[k], 16 * NMID // 2)
            xbc_block(0, True, False)
            with act.Fori(1, XBC.blocks - 1) as b:
                xbc_block(b, False, False)
                silus(b - 1)
            xbc_block(XBC.blocks - 1, False, True)
            silus(XBC.blocks - 2)
            silus(XBC.blocks - 1)


            for i in range(NT):
                act.wait_ge(b_done, i + 1)
                act.activation(btok[:].rearrange("p g n -> p (g n)"), bank[4][:], ACT.Copy).then_inc(b_copied, 1)
                act.wait_ge(alast_done, i + 1)
                step(act.activation(ssm[:, 1], ssm[:, 1], ACT.Exp))
                act.activation(ssm[:, 2], ssm[:, 0], ACT.Exp).then_inc(decay_done, 1)
                for g in range(SSD_G):
                    act.wait_ge(segmin_done, SSD_G * i + g + 1)
                    act.activation(segs[i % 2][:, 8 * g:8 * g + 8], segs[i % 2][:, 8 * g:8 * g + 8], ACT.Exp).then_inc(segexp_done, 1)
                for g in range(SSD_G):
                    act.wait_ge(y_used, SSD_G * i + g + 1)
                    step.wait()
                    step(act.activation(ysq[:], yt[:, 512 * g:512 * g + 512], ACT.Square, accum_out=ssm[:, 3, g:g + 1]))
                step.wait()
                act.sem_inc(ysq_done, 1)
                act.wait_ge(yn_done, 2 * i + 1)
                act.activation(ssm[:, 4, 0:4], ssm[:, 4, 0:4], ACT.Sqrt).then_inc(yrt_done, 1)
                for b in range(2):
                    act.wait_ge(yt_done, 4 * i + b + 1)
                    for f in range(4):
                        m = 4 * b + f
                        ins = act.activation(xbc[:, m, i * P:(i + 1) * P], bank[b][:, f * P:(f + 1) * P], ACT.Copy,
                                             scale=gssd[:, m:m + 1])
                        if f % 2 == 1:
                            ins.then_inc(y_done, 1)
                        else:
                            step(ins)

            for k in range(NY):
                if k == 0:
                    act.wait_ge(y_done, 8 * NT)
                act.activation(yh[:, k], xbc[:, k], ACT.Copy).then_inc(y_hi, 1)
                if k == 3:
                    hi(BR_S, 0, 1)
            hi(BR_S, 0, 2)
            act.wait_ge(y_split, NY)
            for k in range(NK):
                act.activation(ah[:, k], attnT[:, k], ACT.Copy).then_inc(a_split_hi, 1)

            def section_hi(s, nxt, between=None):
                for b in range(s.blocks):
                    for j in range(3 if s is BR_S and b == 0 else 1, s.units):
                        hi(s, b, j)
                    hi_next(s, b, nxt, b == s.blocks - 1)
                    if between:
                        between(b)

            section_hi(BR_S, BR_A)

            def merged_hi(b):
                for t in range(4):
                    m = 4 * b + t
                    act.wait_ge(mg_done, m + 1)
                    act.activation(mh[:, m], mg[:, m], ACT.Copy).then_inc(m_hi, 1)

            section_hi(BR_A, OUT, merged_hi)
            section_hi(OUT, PQ)
            for k in range(NK):
                act.wait_ge(x1_done, k + 1)
                act.activation(sq2[:, k], xT[:, k], ACT.Square).then_inc(sq_done, 1)
            act.wait_ge(ms_done, 2)
            act.activation(rms2[:, 1], rms2[:, 0], ACT.Sqrt).then_inc(rt_done, 1)
            for k in range(NK):
                act.wait_ge(h_made, NK + k + 1)
                act.activation(hTh[:, k], hf2[:, k], ACT.Identity, bias=mod[:, 24 + k:25 + k]).then_inc(h_hi, 1)
            for b in range(PQ.blocks):
                for j in range(1, 4):
                    hi(PQ, b, j)
                if b == 0:
                    hi(PQ, 1, 0)
                else:
                    act.wait_ge(raw_full[0], 16 * (PU0 // 4 + 1))
                    act.wait_ge(unit_used, PQ.p1)
                    act.activation(whi[:, 0], raw[:, 0], ACT.Copy).then_inc(hi_done, 1)
                for t in range(4):
                    act.wait_ge(acc_done, 4 * (PQ.b0 + b) + t + 1)
                    act.activation(pqT[:, 4 * b + t], bank[t][:], ACT.Copy).then_inc(acc_free, 1)

            for n in range(4 * NT):
                act.wait_ge(sc_done, n + 1)
                act.activation(sc[:, n // 4, 2 * (n % 4):2 * (n % 4) + 2].rearrange("p h a n -> p (h a n)"),
                               bank[2 + n % 2][:], ACT.Copy).then_inc(sc_full, 1)

            av = a_d.rearrange("(c j) p t -> j c p t", j=4)

            def up_hi(n, r=0):
                act.wait_ge(raw_full[n % 4], 16 * (PU0 // 4 + n // 4 + 1) + r * 4)
                expert_free(act, n, r)
                act.activation(whi[:, n % 2], raw[:, n % 4], ACT.Copy).then_inc(hi_done, 1)

            def down_hi(n, r=0):
                act.wait_ge(raw_full[n % 4], 16 * ((PU0 + NUP) // 4 + n // 4 + 1) + r * 4)
                down_free(act, n, r)
                act.activation(whi[:, n % 2], raw[:, n % 4], ACT.Copy).then_inc(hi_done, 1)

            def up_unit(n, c=0, is_last=False, first=False):
                r = c * 4
                act.wait_ge(up_done, r + (n + 1))
                if is_last:
                    down_hi(n + 2 - NUP)
                else:
                    up_hi(n + 2, r)
                if not first:
                    act.wait_ge(spilled[n % 2], 16 * (n // 2) + r * 8)
                act.activation(gel[:, n % 2], bank[n % 2][:], ACT.Gelu).then_inc(gelu_done, 1)
                act.wait_ge(gelu_done, r + (n + 1))
                act.dma_start(av[n % 4][bass.ds(c + n // 4, 1)].rearrange("o p t -> p (o t)"), gel[:, n % 2]).then_inc(spilled[n % 2], 16)

            def act_part(g, t, par):
                act.wait_ge(gated, g * GT + (t + 1))
                act.activation(ach[:, par, t], ain[:, t], ACT.Copy).then_inc(act_hi, 1)

            up_hi(1)
            for i in range(NT):
                if i == 0:
                    for n in range(4):
                        up_unit(n, first=n < 2)
                with act.Fori(ROUTE // 4 * i + (1 if i == 0 else 0), ROUTE // 4 * (i + 1)) as c:
                    for n in range(4):
                        up_unit(n, c)
                act.wait_ge(sub_done, i + 1)
                act.activation(sv[:], sv[:], ACT.Exp).then_inc(gexp_done, 1)
                if i:
                    picks_evac(i - 1)
            for n in range(4):
                up_unit(GATE0 + n)
            picks_evac(NT - 1)
            act.wait_ge(selT_done, NT)
            act.activation(ghl[:, 0], selT[:, 2], ACT.Copy).then_inc(ghl_hi, 1)
            wpair = w_d.rearrange("(c k) p n -> c k p n", k=2)

            def gate_evac(c, n, first):
                k = n // 4
                if n % 4 == 0 and not first:
                    act.wait_ge(w_out[k], c * 16)
                for q in range(2):
                    act.wait_ge(w_done, c * 16 + (2 * n + q + 1))
                    c0 = 8 * (n % 4) + 4 * q
                    act.activation(gst[:, k, :, c0:c0 + 4].rearrange("p e t -> p t e"),
                                   bank[4 + (2 * n + q) % 4][:].rearrange("p (t e) -> p t e", t=4), ACT.Copy).then_inc(w_evac, 1)
                if n % 4 == 3:
                    act.wait_ge(w_evac, c * 16 + (2 * n + 2))
                    act.dma_start(wpair[bass.ds(c, 1), k].rearrange("o p n -> p (o n)"),
                                  gst[:, k].rearrange("p e t -> p (e t)")).then_inc(w_out[k], 16)

            for n in range(8):
                up_unit(GATE1 + n)
                gate_evac(0, n, True)
            with act.Fori(1, (TAIL0 - GATE1) // 8) as c:
                for n in range(8):
                    up_unit(n, c * 2 + GATE1 // 4)
                    gate_evac(c, n, False)
            with act.Fori(TAIL0 // 4, TAIL1 // 4) as c:
                for n in range(4):
                    up_unit(n, c)
            for t in range(GT):
                act_part(0, t, 0)
            for n in range(4):
                up_unit(TAIL1 + n, 0, is_last=n >= 2)

            def down_group(g, par, first, is_last):
                for m in range(GT):
                    if not (is_last and m >= GT - 2):
                        down_hi(par * GT + m + 2, (g - par) * GT)
                    if m >= 4 and not is_last:
                        if m == 4 and not first:
                            act.wait_ge(down_done, g * GT)
                        for t in (2 * (m - 4), 2 * (m - 4) + 1):
                            act_part(g + 1, t, 1 - par)

            down_group(0, 0, True, False)
            down_group(1, 1, False, False)
            with act.Fori(2, NG - 2, 2) as g:
                down_group(g, 0, False, False)
                down_group(g + 1, 1, False, False)
            down_group(NG - 2, 0, False, False)
            down_group(NG - 1, 1, False, True)

        @block.vector
        def _(dve):
            step = Steps(dve, dve_step)

            def do(ins):
                step(ins)
                step.wait()

            def lo(s, b, j):
                dve.wait_ge(hi_done, s.u0 + j + 1 + b * s.units)
                n = 2 * NSMALL if s is SMALL else 1024
                dve.tensor_tensor(wlo[:, j % 2, 0:n], raw[:, j % 4, 0:n], whi[:, j % 2, 0:n].bitcast(F),
                                  ALU.subtract).then_inc(lo_done, 1)

            def lo_next(s, b, nxt, is_last):
                if is_last:
                    if nxt is not None:
                        lo(nxt, 0, 0)
                else:
                    lo(s, b + 1, 0)

            dve.wait_ge(consts_in, 16 * 13)
            do(dve.tensor_copy(posf[:], posi[:]))
            inv = np.float32(ROPE_THETA) ** (-np.arange(0, 2 * ROT, 2, dtype=np.float32) / np.float32(2 * ROT))
            for r in range(ROT):
                step(dve.tensor_scalar(sinT[:, :, r], posf[:], float(inv[r]), None, ALU.mult))
            step.wait()
            rsc = rms[:].rearrange("p a t -> p (a t)")
            v32 = [rsc[:, 32 * n:32 * n + 32].rearrange("p (a r) -> p a r", r=ROT) for n in range(4)]
            do(dve.tensor_copy(v32[3], sinT[:]))
            for dst, turn, quarter in ((sinT, 0.0, 0.0), (cosT, 0.25, float(np.pi / 2))):
                do(dve.tensor_scalar(v32[0], v32[3], 1 / TWO_PI, turn, ALU.mult, ALU.add))
                do(dve.tensor_scalar(v32[1], v32[0], MAGIC, MAGIC, ALU.add, ALU.subtract))
                do(dve.scalar_tensor_tensor(v32[2], v32[1], -C1, v32[3], ALU.mult, ALU.add))
                do(dve.scalar_tensor_tensor(v32[0], v32[1], -C2, v32[2], ALU.mult, ALU.add))
                do(dve.scalar_tensor_tensor(v32[2], v32[1], -C3, v32[0], ALU.mult, ALU.add))
                do(dve.tensor_scalar(v32[0], v32[2], quarter, PI_F, ALU.add, ALU.min))
                do(dve.tensor_scalar(dst[:], v32[0], -PI_F, None, ALU.max))
            dve.sem_inc(rope_arg, 2)

            dve.wait_ge(cond_done, 1)
            for k in range(NK):
                dve.wait_ge(ada_in[k % 4], 16 * (k // 4 + 1))
                slot = adar[:, k % 4] if k % 4 < 2 else adap[:, k % 4 - 2]
                if k == 0:
                    ins = dve.tensor_scalar(ada[:, 0:2048], slot, cT[:, 0:1], None, ALU.mult)
                else:
                    dve.wait_ge(ada_v_used, k)
                    ins = dve.scalar_tensor_tensor(ada[:, 0:2048], slot, cT[:, k:k + 1], ada[:, 0:2048],
                                                   ALU.mult, ALU.add)
                ins.then_inc(ada_v_used, 1)
                if k == 3:
                    dve.wait_ge(ssq_done, 1)
                    dve.tensor_scalar(rms[:, 0], bank[5][:], 1.0 / D, EPS, ALU.mult, ALU.add).then_inc(ms_done, 1)
                if k == 4:
                    dve.wait_ge(rt_done, 1)
                    do(dve.reciprocal(rms[:, 0], rms[:, 1]))
                if k in (5, 6, 7):
                    for m in range(3 * (k - 5), min(3 * (k - 4), NK)):
                        step(dve.tensor_tensor(hf[:, m], xT[:, m], rms[:, 0], ALU.mult))
            step.wait()
            dve.wait_ge(mod_done, 1)
            do(dve.tensor_tensor(mod[:, 0:16], bank[4][:, 0:16], bada[:, 0:16], ALU.add))
            do(dve.scalar_tensor_tensor(a1[:], mod[:, 8:16], 1.0, g1[:], ALU.add, ALU.mult))
            for k in range(NK):
                dve.tensor_scalar(hf[:, k], hf[:, k], a1[:, k:k + 1], mod[:, k:k + 1], ALU.mult,
                                  ALU.add).then_inc(h_made, 1)
                if k == 0:
                    lo(SMALL, 0, 0)
                else:
                    dve.wait_ge(h_hi, k)
                    dve.tensor_tensor(hTl[:, k - 1], hf[:, k - 1], hTh[:, k - 1].bitcast(F), ALU.subtract).then_inc(h_ready, 1)
            dve.wait_ge(h_hi, NK)
            dve.tensor_tensor(hTl[:, NK - 1], hf[:, NK - 1], hTh[:, NK - 1].bitcast(F), ALU.subtract).then_inc(h_ready, 1)

            for s, nxt in ((SMALL, QI), (QI, KV), (KV, Q), (Q, None)):
                for b in range(s.blocks):
                    for j in range(1, 4):
                        lo(s, b, j)
                    lo_next(s, b, nxt, b == s.blocks - 1)
                if s is Q:
                    dve.wait_ge(mod_done, 2)
                    do(dve.tensor_tensor(mod[:, 16:48], bank[4][:, 16:48], bada[:, 16:48], ALU.add))
                    do(dve.scalar_tensor_tensor(a2[:], mod[:, 32:40], 1.0, g2[:], ALU.add, ALU.mult))
                    dve.sem_inc(mod_out, 1)

            dve.wait_ge(acc_free, 4 * Q.b1)
            q4 = qk[:].rearrange("p t (h d) -> p t h d", d=DH)
            do(dve.tensor_tensor(prep[:], qk[:], qk[:], ALU.mult))
            ssq = rms[:, 0, 0:80].rearrange("p (t h) -> p t h", h=20)
            do(dve.tensor_reduce(ssq, prep[:].rearrange("p t (h d) -> p t h d", d=DH), AX.X, ALU.add))
            dve.tensor_scalar(rms[:, 0, 0:80], rms[:, 0, 0:80], 1.0 / DH, EPS, ALU.mult, ALU.add).then_inc(qk_ms, 1)
            dtv = dt[:]
            u_, v_, w_, r_ = (ysq[:, 128 * n:128 * n + 128].rearrange("p (t h) -> p t h", h=SSD_H) for n in range(4))
            dve.wait_ge(qk_rt, 1)
            do(dve.reciprocal(rms[:, 0, 0:80], rms[:, 1, 0:80]))
            for t in range(NT):
                step(dve.tensor_tensor(q4[:, t], q4[:, t],
                                       rms[:, 0, 20 * t:20 * t + 20].unsqueeze(2).to_broadcast([P, 20, DH]), ALU.mult))
            step.wait()
            for t in range(NT):
                step(dve.tensor_tensor(q4[:, t, 0:AH], q4[:, t, 0:AH], qg[:].unsqueeze(1).to_broadcast([P, AH, DH]), ALU.mult))
                step(dve.tensor_tensor(q4[:, t, AH:], q4[:, t, AH:], kg[:].unsqueeze(1).to_broadcast([P, KVH, DH]), ALU.mult))
            step.wait()
            dve.wait_ge(rope_done, 2)
            pv = prep[:].rearrange("p t c -> p (t c)")
            qi4 = qit[:].rearrange("p t (h d) -> p t h d", d=DH)
            for x4, nh in ((q4, 20), (qi4, 9)):
                for t in range(NT):
                    cs = cosT[:, t].unsqueeze(1).to_broadcast([P, nh, ROT])
                    sn = sinT[:, t].unsqueeze(1).to_broadcast([P, nh, ROT])
                    t1, t2 = x4[:, t, :, 0:ROT], x4[:, t, :, ROT:2 * ROT]
                    s4 = [pv[:, (4 * t + k) * 160:(4 * t + k) * 160 + nh * ROT].rearrange("p (h r) -> p h r", r=ROT) for k in range(4)]
                    step(dve.tensor_tensor(s4[0], t1, cs, ALU.mult))
                    step(dve.tensor_tensor(s4[1], t2, sn, ALU.mult))
                    step(dve.tensor_tensor(s4[2], t2, cs, ALU.mult))
                    step(dve.tensor_tensor(s4[3], t1, sn, ALU.mult))
                step.wait()
                for t in range(NT):
                    t1, t2 = x4[:, t, :, 0:ROT], x4[:, t, :, ROT:2 * ROT]
                    s4 = [pv[:, (4 * t + k) * 160:(4 * t + k) * 160 + nh * ROT].rearrange("p (h r) -> p h r", r=ROT) for k in range(4)]
                    step(dve.tensor_tensor(t1, s4[0], s4[1], ALU.subtract))
                    step(dve.tensor_tensor(t2, s4[2], s4[3], ALU.add))
                step.wait()
            for e in range(2):
                for t in range(NT):
                    step(dve.tensor_copy(kdup[:, t, :, e, :], q4[:, t, AH:]))
                step(dve.tensor_copy(kidup[:, :, e, :], qi4[:, :, IH]))
            step.wait()
            dve.sem_inc(prep_done, 1)

            do(dve.tensor_tensor(dtv, dtv, dtb[:].unsqueeze(1).to_broadcast([P, NT, SSD_H]), ALU.add))
            do(dve.tensor_scalar(u_, dtv, -1.0, None, ALU.mult))
            dve.tensor_tensor(v_, u_, dtv, ALU.max).then_inc(dt_in, 1)
            dve.wait_ge(sp_exp, 1)
            do(dve.tensor_scalar(w_, u_, 1.0, None, ALU.add))
            do(dve.tensor_scalar(v_, w_, 1.0, None, ALU.is_equal))
            do(dve.scalar_tensor_tensor(r_, w_, -1.0, v_, ALU.add, ALU.add))
            dve.sem_inc(sp_ln, 1)
            dve.wait_ge(sp_relu, 1)
            do(dve.tensor_tensor(w_, w_, v_, ALU.add))
            do(dve.tensor_tensor(w_, w_, u_, ALU.mult))
            do(dve.reciprocal(r_, r_))
            do(dve.tensor_tensor(w_, w_, r_, ALU.mult))
            do(dve.scalar_tensor_tensor(dtv, dtv, 0.0, w_, ALU.max, ALU.add))
            dve.scalar_tensor_tensor(v_, dtv, -1.0, alog[:].unsqueeze(1).to_broadcast([P, NT, SSD_H]), ALU.mult,
                                     ALU.mult).then_inc(ad_done, 1)
            dve.wait_ge(tp_done, 17)
            dve.wait_ge(acs_done, 1)
            do(dve.memset(zer[:], 0.0))
            do(dve.tensor_scalar(wi[:], wi[:], IH ** -0.5, None, ALU.mult))

            for i in range(1, NT):
                nk = P * (i + 1)
                sco = score[:, i - 1, 0:nk]
                for h in range(IH):
                    n = IH * (i - 1) + h
                    dve.wait_ge(rl_full, n + 1)
                    if h == 0:
                        ins = dve.tensor_scalar(sco, rl[:, n % 4, 0:nk], wi[:, i, h:h + 1], None, ALU.mult)
                    else:
                        dve.wait_ge(rl_used, n)
                        ins = dve.scalar_tensor_tensor(sco, rl[:, n % 4, 0:nk], wi[:, i, h:h + 1], sco, ALU.mult, ALU.add)
                    ins.then_inc(rl_used, 1)
            do(dve.memset(mb[:, 0, 0:P], 0.0))
            do(dve.memset(mb[0:CHUNK, 0, CHUNK:P], NEG))
            dve.wait_ge(rl_used, IH * (NT - 1))
            for i in range(1, NT):
                nk = P * (i + 1)
                m = mb[:, i, 0:nk]
                sco = score[:, i - 1, 0:nk]
                do(dve.memset(score[0:CHUNK, i - 1, nk - CHUNK:nk], NEG))
                for r in range(TOPK // 8):
                    src = sco if r == 0 else work[:, 0:nk]
                    do(dve.max(tk8[:, 0:8], src))
                    if r < TOPK // 8 - 1:
                        do(dve.match_replace(work[:, 0:nk], tk8[:, 0:8], src, -3e38))
                do(dve.tensor_scalar(selm[:, 0:nk], sco, tk8[:, 7:8], 0.0, ALU.is_gt, ALU.add,
                                     accum_out=tk8[:, 8:9]))
                do(dve.tensor_scalar(eqm[:, 0:nk], sco, tk8[:, 7:8], None, ALU.is_equal))
                do(dve.tensor_tensor_scan(cum[:, 0:nk], eqm[:, 0:nk], zer[:, 0:nk], 0.0, ALU.add, ALU.add))
                do(dve.tensor_scalar(tk8[:, 9:10], tk8[:, 8:9], -1.0, float(TOPK), ALU.mult, ALU.add))
                do(dve.scalar_tensor_tensor(cum[:, 0:nk], cum[:, 0:nk], tk8[:, 9:10], eqm[:, 0:nk], ALU.is_le, ALU.mult))
                do(dve.tensor_tensor(selm[:, 0:nk], selm[:, 0:nk], cum[:, 0:nk], ALU.add))
                do(dve.tensor_scalar(m, selm[:, 0:nk], -1.0, -NEG, ALU.add, ALU.mult))

            for m in range(12):
                dve.wait_ge(qk_hi, m + 1)
                x, xh, xl = (a[:, m % 8] for a in ((qT, qTh, qTl) if m < 8 else (kT, kTh, kTl)))
                dve.tensor_tensor(xl, x, xh.bitcast(F), ALU.subtract).then_inc(qk_split, 1)

            def pt_copy(n):
                i = n // AH
                nk = P * (i + 1)
                dve.wait_ge(pt_done, n + 1)
                if n >= 2:
                    dve.wait_ge(pv_done, n - 1)
                dve.tensor_copy(pts[:, n % 2, 0:nk], bank[6][:, 0:nk]).then_inc(pt_evac, 1)

            for i in range(NT):
                nk = P * (i + 1)
                for h in range(AH):
                    n = AH * i + h
                    dve.wait_ge(s_done, n + 1)
                    if n >= 3:
                        dve.wait_ge(exp_done, n - 2)
                    do(dve.tensor_tensor_reduce(out=pm[:, n % 3, 0:nk], in0=bank[sb[n % 3]][:, 0:nk], in1=mb[:, i, 0:nk],
                                                scale=DH ** -0.5, scalar=-3e38, op0=ALU.add, op1=ALU.max,
                                                accum_out=asm[:, 2, h:h + 1]))
                    if h == 0 and i:
                        dve.wait_ge(exp_done, n)
                    dve.tensor_scalar(asm[:, 0, h:h + 1], asm[:, 2, h:h + 1], -1.0, None, ALU.mult).then_inc(neg_max, 1)
                    if h >= 2:
                        pt_copy(n - 2)
                pt_copy(AH * i + AH - 2)
                pt_copy(AH * i + AH - 1)
                dve.wait_ge(exp_done, AH * i + AH)
                do(dve.reciprocal(asm[:, 2], asm[:, 1]))
                dve.wait_ge(pv_done, AH * i + AH)
                if i:
                    dve.wait_ge(ot_done, 2 * i)
                for b in range(2):
                    dve.tensor_tensor(otok[:, 512 * b:512 * b + 512].rearrange("p (h d) -> p h d", d=DH),
                                      bank[7 if b == 0 else 3][:].rearrange("p (h d) -> p h d", d=DH),
                                      asm[:, 2, 8 * b:8 * b + 8].unsqueeze(2).to_broadcast([P, 8, DH]),
                                      ALU.mult).then_inc(o_ready, 1)
                dve.wait_ge(o_ready, 2 * i + 2)

            def conv(b, t, first):
                m = b * 4 + t
                cw = [convw[:].rearrange("p m k -> p (m k)")[:, bass.ds(m * CONV_K + k, 1)] for k in range(CONV_K)]
                dve.wait_ge(acc_free, 4 * (XBC.b0 - NMID) + 1 + m)
                if not first:
                    dve.wait_ge(silu_done, m - 3)
                do(dve.tensor_scalar(cacc[:, t], craw[:, t], cw[3], convb[:, bass.ds(m, 1)], ALU.mult, ALU.add))
                for k in range(1, CONV_K):
                    ins = dve.scalar_tensor_tensor(cacc[:, t, k:], craw[:, t, 0:T - k], cw[3 - k], cacc[:, t, k:],
                                                   ALU.mult, ALU.add)
                    if k < CONV_K - 1:
                        do(ins)
                    else:
                        ins.then_inc(conv_done, 1)

            def seg_head(i):
                if i is None:
                    return
                dve.wait_ge(seg_in[i % 2], 16 * (i // 2 + 1))
                do(dve.tensor_copy(ssm[:, 0], segs[i % 2][:, :, P - 1]))
                dve.tensor_tensor(ssm[:, 1], ssm[:, 0], acs[:, i], ALU.subtract).then_inc(alast_done, 1)

            def seg_min(i, g):
                if i is None:
                    return
                for h in range(8 * g, 8 * g + 8):
                    ins = dve.tensor_scalar(segs[i % 2][:, h], segs[i % 2][:, h], acs[:, i, h:h + 1], 0.0,
                                            ALU.subtract, ALU.min)
                    if h % 8 == 7:
                        ins.then_inc(segmin_done, 1)
                    else:
                        step(ins)

            seg_head(0)
            for g in range(SSD_G):
                seg_min(0, g)
            for t in range(4):
                conv(0, t, True)
            with dve.Fori(1, XBC.blocks) as b:
                step.enter(b - 1, 12)
                for t in range(4):
                    conv(b, t, False)
                step.leave(XBC.blocks - 1)

            dve.wait_ge(silu_done, NX)
            do(dve.memset(st[:], 0.0))

            def bc(x, n=SSD_P):
                return x.unsqueeze(2).to_broadcast([P, x.shape[1], n])

            for i in range(NT):
                nxt = i + 1 if i < NT - 1 else None
                for b in range(4):
                    dve.wait_ge(xp_done, 4 * i + b + 1)
                    pv_ = bank[b][:].rearrange("p (h d) -> p h d", d=SSD_P)
                    step(dve.tensor_tensor(xd[:, 512 * b:512 * b + 512].rearrange("p (h d) -> p h d", d=SSD_P), pv_,
                                           bc(dt[:, i, 8 * b:8 * b + 8]), ALU.mult))
                    step(dve.tensor_tensor(xsk[:, 512 * b:512 * b + 512].rearrange("p (h d) -> p h d", d=SSD_P), pv_,
                                           bc(dskip[:, 8 * b:8 * b + 8]), ALU.mult))
                step.wait()
                dve.sem_inc(xd_done, 1)
                dve.wait_ge(cb_done, i + 1)
                do(dve.tensor_tensor(cbm[:], bank[5][:].rearrange("p (g l) -> p g l", g=SSD_G),
                                     tri[:].unsqueeze(1).to_broadcast([P, SSD_G, P]), ALU.mult))
                for g in range(SSD_G):
                    dve.wait_ge(segexp_done, SSD_G * i + g + 1)
                    dve.tensor_tensor(segs[i % 2][:, 8 * g:8 * g + 8], segs[i % 2][:, 8 * g:8 * g + 8],
                                      cbm[:, g].unsqueeze(1).to_broadcast([P, 8, P]), ALU.mult).then_inc(m_ready, 1)
                dve.wait_ge(z_in, 16 * (i + 1))
                for g in range(SSD_G):
                    c = slice(512 * g, 512 * g + 512)
                    dve.wait_ge(yo_done, SSD_G * i + g + 1)
                    if i:
                        do(dve.tensor_tensor(ytmp[:].rearrange("p (h d) -> p h d", d=SSD_P),
                                             bank[yb[g % 2]][:].rearrange("p (h d) -> p h d", d=SSD_P),
                                             bc(eacs[:, i, 8 * g:8 * g + 8]), ALU.mult))
                        do(dve.tensor_tensor(xsk[:, c], xsk[:, c], ytmp[:], ALU.add))
                    do(dve.tensor_tensor(yt[:, c], bank[yb[g % 2] + 1][:], xsk[:, c], ALU.add))
                    dve.tensor_tensor(yt[:, c], yt[:, c], zc[:, c], ALU.mult).then_inc(y_used, 1)
                dve.wait_ge(yo_done, SSD_G * i + SSD_G)
                if i < NT - 1:
                    dve.wait_ge(st_decayed, i + 1)
                    for g in range(SSD_G):
                        c = slice(512 * g, 512 * g + 512)
                        dve.wait_ge(st_mm, SSD_G * i + g + 1)
                        dve.tensor_tensor(st[:, c], st[:, c], bank[4 + g % 2][:], ALU.add).then_inc(st_used, 1)
                seg_head(nxt)
                seg_min(nxt, 0)
                dve.wait_ge(ysq_done, i + 1)
                dve.tensor_scalar(ssm[:, 4, 0:4], ssm[:, 3, 0:4], 1.0 / 512, EPS, ALU.mult, ALU.add).then_inc(yn_done, 1)
                seg_min(nxt, 1)
                dve.wait_ge(yrt_done, i + 1)
                do(dve.reciprocal(ssm[:, 5, 0:4], ssm[:, 4, 0:4]))
                for g in range(SSD_G):
                    c = slice(512 * g, 512 * g + 512)
                    step(dve.tensor_scalar(yt[:, c], yt[:, c], ssm[:, 5, g:g + 1], None, ALU.mult))
                step.wait()
                dve.sem_inc(yn_done, 1)
                seg_min(nxt, 2)
                seg_min(nxt, 3)
                for b in range(2, 4):
                    dve.wait_ge(yt_done, 4 * i + b + 1)
                    for f in range(4):
                        m = 4 * b + f
                        ins = dve.tensor_scalar(xbc[:, m, i * P:(i + 1) * P], bank[b][:, f * P:(f + 1) * P],
                                                gssd[:, m:m + 1], None, ALU.mult)
                        if f % 2 == 1:
                            ins.then_inc(y_done, 1)
                        else:
                            step(ins)

            for k in range(NY):
                dve.wait_ge(y_hi, k + 1)
                if k == 0:
                    dve.wait_ge(y_done, 8 * NT)
                dve.tensor_tensor(yl[:, k], xbc[:, k], yh[:, k].bitcast(F), ALU.subtract).then_inc(y_split, 1)
            for k in range(NK):
                dve.wait_ge(a_split_hi, k + 1)
                dve.tensor_tensor(al[:, k], attnT[:, k], ah[:, k].bitcast(F), ALU.subtract).then_inc(a_split, 1)

            def evacuate(s, after):
                for m in range(4 * s.blocks):
                    dve.wait_ge(acc_done, 4 * s.b0 + m + 1)
                    after(m, m % 4)

            def ssd_gate(m, t):
                dve.wait_ge(gate_in[m % 2], 16 * (m // 2 + 1))
                dve.tensor_tensor(mg[:, m], bank[t][:], gring[:, m % 2], ALU.mult).then_inc(acc_free, 1)
                dve.wait_ge(acc_free, 4 * BR_S_free0 + m + 1)
                dve.sem_inc(gate_used, 1)

            def merged_lo(m):
                dve.wait_ge(m_hi, m + 1)
                dve.wait_ge(a_split, NK)
                dve.tensor_tensor(ml[:, m], mg[:, m], mh[:, m].bitcast(F), ALU.subtract).then_inc(m_split, 1)

            def attn_gate(m, t):
                dve.wait_ge(gate_in[m % 2], 16 * (NK // 2 + m // 2 + 1))
                if m:
                    dve.wait_ge(mg_done, m)
                dve.tensor_tensor(mtmp[:], bank[t][:], gring[:, m % 2], ALU.mult).then_inc(acc_free, 1)
                dve.wait_ge(acc_free, 4 * BR_S_free0 + NK + m + 1)
                dve.sem_inc(gate_used, 1)
                dve.tensor_tensor(mg[:, m], mg[:, m], mtmp[:], ALU.add).then_inc(mg_done, 1)
                if m:
                    merged_lo(m - 1)

            def residual(m, t):
                dve.scalar_tensor_tensor(xT[:, m], bank[t][:], mod[:, 16 + m:17 + m], xT[:, m], ALU.mult,
                                         ALU.add).then_inc(acc_free, 1)
                dve.wait_ge(acc_free, 4 * BR_S_free0 + 2 * NK + m + 1)
                dve.sem_inc(x1_done, 1)

            evacuate(BR_S, ssd_gate)
            evacuate(BR_A, attn_gate)
            merged_lo(NK - 1)
            dve.wait_ge(x_again, 16)
            evacuate(OUT, residual)
            def h2_lo(k):
                dve.wait_ge(h_hi, NK + k + 1)
                dve.scalar_tensor_tensor(hTl[:, k], hf2[:, k], mod[:, 24 + k:25 + k], hTh[:, k].bitcast(F), ALU.add,
                                         ALU.subtract).then_inc(h_ready, 1)

            dve.wait_ge(ssq_done, 2)
            dve.tensor_scalar(rms2[:, 0], bank[5][:], 1.0 / D, EPS, ALU.mult, ALU.add).then_inc(ms_done, 1)
            dve.wait_ge(rt_done, 2)
            do(dve.reciprocal(rms2[:, 0], rms2[:, 1]))
            for k in range(NK):
                dve.scalar_tensor_tensor(hf2[:, k], xT[:, k], a2[:, k:k + 1], rms2[:, 0], ALU.mult,
                                         ALU.mult).then_inc(h_made, 1)
                if k:
                    h2_lo(k - 1)
            h2_lo(NK - 1)
            for i in range(NT):
                dve.wait_ge(sc_full, 4 * i + 4)
                for h in range(PH):
                    for e in range(2):
                        row = sc[:, i, h, e]
                        do(dve.max(v8[:, h, e, 0:8], row))
                        step(dve.max_index(i8[:, h, e, 0:8], v8[:, h, e, 0:8], row))
                        step.wait()
                        do(dve.match_replace(row, v8[:, h, e, 0:8], row, -3e38))
                        do(dve.max(v8[:, h, e, 8:16], row))
                        step(dve.max_index(i8[:, h, e, 8:16], v8[:, h, e, 8:16], row))
                step.wait()
                step(dve.tensor_copy(if8[:], i8[:]))
                for h in range(PH):
                    step(dve.tensor_tensor(cand[:, h], v8[:, h, 0].unsqueeze(2).to_broadcast([P, PK, PK]),
                                           v8[:, h, 1].unsqueeze(1).to_broadcast([P, PK, PK]), ALU.add))
                step.wait()
                for h in range(PH):
                    row = cand[:, h].rearrange("p a b -> p (a b)")
                    do(dve.max(sv[:, h, 0:8], row))
                    step(dve.max_index(ci[:, h, 0:8], sv[:, h, 0:8], row))
                    step.wait()
                    do(dve.match_replace(row, sv[:, h, 0:8], row, -3e38))
                    do(dve.max(sv[:, h, 8:16], row))
                    step(dve.max_index(ci[:, h, 8:16], sv[:, h, 8:16], row))
                step.wait()
                do(dve.tensor_copy(gsm[:, 0], sv[:, :, 0]))
                dve.tensor_tensor(sv[:], sv[:], gsm[:, 0].unsqueeze(2).to_broadcast([P, PH, PK]),
                                  ALU.subtract).then_inc(sub_done, 1)
                step(dve.tensor_scalar(cab[:, 0], ci[:], 4, None, ALU.logical_shift_right))
                step(dve.tensor_scalar(cab[:, 1], ci[:], 15, None, ALU.bitwise_and))
                step.wait()
                do(dve.tensor_copy(cabf[:], cab[:]))
                if i:
                    dve.wait_ge(selT_tp, i)
                for e in range(2):
                    do(dve.tensor_tensor(eqa[:].rearrange("p h k j -> p (h k) j"),
                                         cabf[:, e].rearrange("p h k -> p (h k)").unsqueeze(2).to_broadcast([P, P, PK]),
                                         iota16[:].unsqueeze(1).to_broadcast([P, P, PK]), ALU.is_equal))
                    for h in range(PH):
                        step(dve.tensor_tensor(eqa[:, h], eqa[:, h], if8[:, h, e].unsqueeze(1).to_broadcast([P, PK, PK]), ALU.mult))
                    step.wait()
                    do(dve.tensor_reduce(sel[:, e], eqa[:].rearrange("p h k j -> p (h k) j"), AX.X, ALU.add))
                dve.wait_ge(gexp_done, i + 1)
                do(dve.tensor_reduce(gsm[:, 0], sv[:], AX.X, ALU.add))
                do(dve.reciprocal(gsm[:, 1], gsm[:, 0]))
                dve.tensor_tensor(sel[:, 2].rearrange("p (h k) -> p h k", k=PK), sv[:],
                                  gsm[:, 1].unsqueeze(2).to_broadcast([P, PH, PK]), ALU.mult).then_inc(sel_ready, 1)
                dve.wait_ge(sel_ready, i + 1)
            dve.wait_ge(ghl_hi, 1)
            do(dve.tensor_tensor(ghl[:, 1], selT[:, 2], ghl[:, 0].bitcast(F), ALU.subtract))

            def onehots(c, first):
                sT = selT[:].rearrange("p a t -> p (a t)")
                gT = ghl[:].rearrange("p a t -> p (a t)").bitcast(F)
                for n in range(2 * TC):
                    q = n % 16
                    if n % 4 == 0 and not (first and n < 16):
                        dve.wait_ge(w_done, c * 16 + (n // 4 - 3))
                    t = c * 64 + n
                    for e in range(2):
                        step(dve.tensor_scalar(oh1[:, q, e], iota[:], sT[:, bass.ds(t, 1)],
                                               gT[:, bass.ds(t + e * T, 1)], ALU.is_equal, ALU.mult))
                    ins = dve.tensor_scalar(oh2[:, q], iota[:], sT[:, bass.ds(t + T, 1)], None, ALU.is_equal)
                    if n % 4 == 3:
                        ins.then_inc(oh_made, 1)
                    else:
                        step(ins)
            onehots(0, True)
            with dve.Fori(1, NTC // 2) as c:
                onehots(c, False)
            step.n += (NTC // 2 - 2) * (2 * 2 * TC + 3 * TC // 2)

            dve.wait_ge(w_done, T // 4)
            do(dve.memset(acc[:], 0.0))

            def gate_tiles(g, ts, par):
                for t in ts:
                    dve.tensor_tensor(ain[:, t].rearrange("p (c t) -> p c t", t=TC),
                                      ain[:, t].rearrange("p (c t) -> p c t", t=TC), gg[:, :, t, :],
                                      ALU.mult).then_inc(gated, 1)
                for t in ts:
                    dve.wait_ge(act_hi, g * GT + (t + 1))
                    dve.tensor_tensor(acl[:, par, t], ain[:, t], ach[:, par, t].bitcast(F), ALU.subtract).then_inc(act_ready, 1)

            for t in range(0, GT, 2):
                if t == 0:
                    dve.wait_ge(ain_in, 16)
                    dve.wait_ge(gg_in, 16)
                gate_tiles(0, (t, t + 1), 0)

            def down_lo(n, r=0):
                dve.wait_ge(hi_done, r + (PU0 + NUP + n + 1))
                dve.tensor_tensor(wlo[:, n % 2], raw[:, n % 4], whi[:, n % 2].bitcast(F), ALU.subtract).then_inc(lo_done, 1)

            def down_group(g, par, first, is_last):
                for m in range(GT):
                    if not (is_last and m == GT - 1):
                        down_lo(par * GT + m + 1, (g - par) * GT)
                    if m >= 4 and not is_last:
                        if m == 4:
                            dve.wait_ge(ain_in, 16 * (2) + g * 16)
                            dve.wait_ge(gg_in, 16 * (2) + g * 16)
                            if not first:
                                dve.wait_ge(down_done, g * GT)
                        gate_tiles(g + 1, (2 * (m - 4), 2 * (m - 4) + 1), 1 - par)
                    dve.wait_ge(down_done, g * GT + (m + 1))
                    if not first:
                        dve.wait_ge(added, g * GT + (m - GT + 1))
                    dve.tensor_tensor(acc[:, m], acc[:, m], bank[2 + m % 2][:], ALU.add).then_inc(added, 1)

            down_lo(0)
            down_group(0, 0, True, False)
            down_group(1, 1, False, False)
            with dve.Fori(2, NG - 2, 2) as g:
                down_group(g, 0, False, False)
                down_group(g + 1, 1, False, False)
            down_group(NG - 2, 0, False, False)
            down_group(NG - 1, 1, False, True)
            for m in range(NK):
                dve.wait_ge(added, GT * (NG - 1) + m + 1)
                dve.scalar_tensor_tensor(xT[:, m], acc[:, m], mod[:, 40 + m:41 + m], xT[:, m], ALU.mult,
                                         ALU.add).then_inc(out_made, 1)

        @block.tensor
        def _(pe):
            step = Steps(pe, pe_step)
            pe.wait_ge(consts_made, 1)
            for k in range(NK):
                pe.wait_ge(sq_done, k + 1)
                ins = pe.matmul(bank[5][:], ones[:], sq[:, k], start=(k == 0), stop=(k == NK - 1))
            ins.then_inc(ssq_done, 1)
            pe.wait_ge(ada_v_used, NK)
            for m in range(16):
                ins = pe.matmul(bank[4][:, m:m + 1], ada[:, m * P:(m + 1) * P], ones[:, 0:1], start=True, stop=True)
            ins.then_inc(mod_done, 1)

            def free_wait(s, b, t):
                if s is Z or s is GATES:
                    if s is Z and b == 0:
                        pe.wait_ge(acc_free, 4 * (Z.b0 - 1) + t + 1)
                    else:
                        pe.wait_ge(stg_full, 4 * (s.b0 - Z.b0 + b - 1) + t + 1)
                elif s is XBC and isinstance(b, int):
                    pe.wait_ge(attn_ready, 2 * NT)
                else:
                    base = s.b0 if s.b0 < Z.b0 else s.b0 - NMID
                    n = 4 * (base - 1) + t + 1 + b * 4
                    if not (isinstance(n, int) and n <= 0):
                        pe.wait_ge(acc_free, n)

            def product(s, b, token_major, mov, ncols=CW, rhs_wait=None):
                mh_, ml_ = mov
                for j in range(s.units):
                    if s.u0 < S0:
                        pe.wait_ge(lo_done, s.u0 + j + 1 + b * s.units)
                    else:
                        pe.wait_ge(pool_split, s.u0 - S0 + j + 1 + b * s.units)
                    wh = whi[:, j % 2, 0:2 * ncols].rearrange("p (a c) -> p a c", a=2)
                    wl = wlo[:, j % 2, 0:2 * ncols].rearrange("p (a c) -> p a c", a=2)
                    for t in range(4):
                        if j == 0:
                            free_wait(s, b, t)
                        for a in range(2):
                            k = 2 * j + a
                            if rhs_wait and t == 0:
                                rhs_wait(k)
                            if token_major:
                                ht, lt = mh_[:, k, t * P:(t + 1) * P], ml_[:, k, t * P:(t + 1) * P]
                                three = ((ht, wh[:, a]), (ht, wl[:, a]), (lt, wh[:, a]))
                            else:
                                wht, wlt = wh[:, a, t * P:(t + 1) * P], wl[:, a, t * P:(t + 1) * P]
                                three = ((wht, mh_[:, k]), (wht, ml_[:, k]), (wlt, mh_[:, k]))
                            for q, (x, y) in enumerate(three):
                                ins = pe.matmul(bank[t][:, 0:ncols] if token_major else bank[t][:], x, y,
                                                start=(j == 0 and a == 0 and q == 0),
                                                stop=(j == s.units - 1 and a == 1 and q == 2))
                        if j == s.units - 1:
                            ins.then_inc(acc_done, 1)
                    if j < s.units - 1:
                        ins.then_inc(unit_used, 1)

            product(SMALL, 0, True, h_pair, NSMALL, rhs_wait=lambda k: pe.wait_ge(h_ready, k + 1))
            product(QI, 0, True, h_pair)
            product(KV, 0, True, h_pair)
            with pe.Fori(0, Q.blocks) as b:
                product(Q, b, True, h_pair)
            pe.wait_ge(ada_ready, 1)
            for m in range(16, 48):
                ins = pe.matmul(bank[4][:, m:m + 1], ada[:, m * P:(m + 1) * P], ones[:, 0:1], start=True, stop=True)
            ins.then_inc(mod_done, 1)

            def mid_product(n):
                if n < Z.blocks:
                    product(Z, n, True, h_pair)
                else:
                    product(GATES, n - Z.blocks, False, h_pair)

            mid_product(0)
            mid_product(1)

            pe.wait_ge(prep_done, 1)
            pe.wait_ge(mod_out, 1)
            for n in range(17):
                if n >= 4:
                    pe.wait_ge(tp_free, n - 3)
                for t in range(NT):
                    src = qk[:, t, n * P:(n + 1) * P] if n < 8 else \
                        kdup[:, t, n - 8].rearrange("p e d -> p (e d)") if n < 12 else \
                        qit[:, t, (n - 12) * P:(n - 11) * P] if n < 16 else kidup[:, t].rearrange("p e d -> p (e d)")
                    ins = pe.transpose(bank[4 + n % 4][:, t * P:(t + 1) * P], src, ident[:])
                ins.then_inc(tp_done, 1)
            pe.wait_ge(ad_done, 1)
            pe.wait_ge(tp_free, 17)
            pe.matmul(bank[4][:, 0:P], tri[:], ysq[:, 128:256], start=True, stop=True).then_inc(acs_done, 1)
            pe.wait_ge(acs_cp, 1)
            for t in range(NT):
                ins = pe.transpose(bank[5][0:SSD_H, t * P:(t + 1) * P], acs[:, t], ident[:])
            ins.then_inc(acsT_tp, 1)
            pe.wait_ge(acsT_ready, 1)
            for i in range(1, NT):
                nk = P * (i + 1)
                for h in range(IH):
                    n = IH * (i - 1) + h
                    if n >= 4:
                        pe.wait_ge(rl_full, n - 3)
                    o = 64 * (h % 2)
                    pe.matmul(bank[4 + n % 4][:, 0:nk], qiT[o:o + 64, h // 2, i * P:(i + 1) * P], kiT[o:o + 64, 0:nk],
                              start=True, stop=True).then_inc(ix_done, 1)
            for n in range(2, NMID):
                mid_product(n)

            def weights_t(n):
                i = n // AH
                pe.wait_ge(exp_done, n + 1)
                if n >= 1:
                    pe.wait_ge(pt_evac, n)
                for kt in range(i + 1):
                    ins = pe.transpose(bank[6][:, kt * P:(kt + 1) * P], pe_[:, n % 3, kt * P:(kt + 1) * P], ident[:])
                ins.then_inc(pt_done, 1)

            def values(n):
                i, h = n // AH, n % AH
                pe.wait_ge(pt_evac, n + 1)
                if h == 0 and i:
                    pe.wait_ge(o_ready, 2 * i)
                o = bank[7 if h < 8 else 3][:, (h % 8) * DH:(h % 8 + 1) * DH]
                g = h // (AH // KVH)
                for kt in range(i + 1):
                    ins = pe.matmul(o, pts[:, n % 2, kt * P:(kt + 1) * P], vt[:, kt, g * DH:(g + 1) * DH],
                                    start=(kt == 0), stop=(kt == i))
                ins.then_inc(pv_done, 1)

            pe.wait_ge(rl_full, IH * (NT - 1))
            pe.wait_ge(qk_split, 12)
            pe.wait_ge(stg_full, 4 * NMID)
            for i in range(NT):
                nk = P * (i + 1)
                for h in range(AH):
                    n = AH * i + h
                    if n >= 3:
                        pe.wait_ge(neg_max, n - 2)
                    o = 64 * (h % 2)
                    for e, (q_, k_) in enumerate(((qTh, kTh), (qTh, kTl), (qTl, kTh))):
                        ins = pe.matmul(bank[sb[n % 3]][:, 0:nk], q_[o:o + 64, h // 2, i * P:(i + 1) * P],
                                        k_[o:o + 64, h // (AH // KVH), 0:nk], start=(e == 0), stop=(e == 2))
                    ins.then_inc(s_done, 1)
                    if n >= 2 and not (h == 1 and i):
                        weights_t(n - 2)
                    if n >= 3 and not (h in (1, 2) and i):
                        values(n - 3)
                    if h == 0 and i:
                        weights_t(n - 1)
                        values(n - 2)
                        values(n - 1)
                    if h == 1 and i:
                        out_t(pe, i - 1)
            weights_t(AH * NT - 2)
            values(AH * NT - 3)
            weights_t(AH * NT - 1)
            values(AH * NT - 2)
            values(AH * NT - 1)
            out_t(pe, NT - 1)

            product(XBC, 0, False, h_pair)
            with pe.Fori(1, XBC.blocks) as b:
                product(XBC, b, False, h_pair)

            for i in range(NT):
                cols = slice(i * P, (i + 1) * P)
                if i == 0:
                    pe.wait_ge(silu_done, NX)
                for b in range(4):
                    if i:
                        pe.wait_ge(y_done, 8 * i)
                    for f in range(4):
                        ins = pe.transpose(bank[b][:, f * P:(f + 1) * P], xbc[:, 4 * b + f, cols], ident[:])
                    ins.then_inc(xp_done, 1)
                if i:
                    pe.wait_ge(st_used, SSD_G * i)
                for g in range(SSD_G):
                    ins = pe.transpose(bank[4][:, g * P:(g + 1) * P], xbc[:, NY + g, cols], ident[:])
                ins.then_inc(b_done, 1)
                for g in range(SSD_G):
                    ins = pe.matmul(bank[5][:, g * P:(g + 1) * P], xbc[:, NY + g, cols], xbc[:, NY + SSD_G + g, cols],
                                    start=True, stop=True)
                ins.then_inc(cb_done, 1)
                for g in range(SSD_G):
                    c = slice(512 * g, 512 * g + 512)
                    if g == 0:
                        pe.wait_ge(xd_done, i + 1)
                    if i or g >= 2:
                        pe.wait_ge(y_used, SSD_G * i + g - 1)
                    if i:
                        pe.matmul(bank[yb[g % 2]][:], xbc[:, NY + SSD_G + g, cols], st[:, c], start=True, stop=True)
                    pe.wait_ge(m_ready, SSD_G * i + g + 1)
                    for q in range(8):
                        hh = 8 * g + q
                        ins = pe.matmul(bank[yb[g % 2] + 1][:, q * SSD_P:(q + 1) * SSD_P], segs[i % 2][:, hh],
                                        xd[:, hh * SSD_P:(hh + 1) * SSD_P], start=True, stop=True)
                    ins.then_inc(yo_done, 1)
                if i < NT - 1:
                    pe.wait_ge(b_copied, i + 1)
                    pe.wait_ge(xdd_done, i + 1)
                    for g in range(SSD_G):
                        if g >= 2:
                            pe.wait_ge(st_used, SSD_G * i + g - 1)
                        pe.matmul(bank[4 + g % 2][:], btok[:, g], xdd[:, 512 * g:512 * g + 512], start=True,
                                  stop=True).then_inc(st_mm, 1)
                pe.wait_ge(yn_done, 2 * i + 2)
                for b in range(4):
                    for f in range(4):
                        ins = pe.transpose(bank[b][:, f * P:(f + 1) * P], yt[:, (4 * b + f) * P:(4 * b + f + 1) * P], ident[:])
                    ins.then_inc(yt_done, 1)

            pe.wait_ge(y_done, 8 * NT)
            with_wait = lambda sem_, n0: (lambda k: pe.wait_ge(sem_, n0 + k + 1))
            for b in range(2):
                product(BR_S, b, False, (yh, yl), rhs_wait=with_wait(y_split, 0) if b == 0 else None)
            for b in range(2):
                product(BR_A, b, False, (ah, al), rhs_wait=with_wait(a_split, 0) if b == 0 else None)
            for b in range(2):
                product(OUT, b, False, (mh, ml), rhs_wait=with_wait(m_split, 0) if b == 0 else None)
            for k in range(NK):
                pe.wait_ge(sq_done, NK + k + 1)
                ins = pe.matmul(bank[5][:], ones[:], sq2[:, k], start=(k == 0), stop=(k == NK - 1))
            ins.then_inc(ssq_done, 1)
            for b in range(2):
                product(PQ, b, False, h_pair, rhs_wait=with_wait(h_ready, NK) if b == 0 else None)

            pe.wait_ge(sk_in, 32)
            pe.wait_ge(acc_free, 4 * (PQ.b1 - 8))
            for n in range(4 * NT):
                i = n // 4
                if n >= 2:
                    pe.wait_ge(sc_full, n - 1)
                for h in range(2):
                    hh = 2 * (n % 4) + h
                    ins = pe.matmul(bank[2 + n % 2][:, 256 * h:256 * h + 256], pqT[:, hh, i * P:(i + 1) * P],
                                    skbd[:, hh].rearrange("p a n -> p (a n)"), start=True, stop=True)
                ins.then_inc(sc_done, 1)

            def three_pass(o, slot, xh, xl, wait=None):
                for k in range(NK):
                    if wait:
                        wait(k)
                    wh, wl = whi[:, slot, k * P:(k + 1) * P], wlo[:, slot, k * P:(k + 1) * P]
                    for q, (x, y) in enumerate(((wh, xh(k)), (wh, xl(k)), (wl, xh(k)))):
                        ins = pe.matmul(o[:], x, y, start=(k == 0 and q == 0), stop=(k == NK - 1 and q == 2))
                return ins

            def up_unit(n, r=0, first=False):
                pe.wait_ge(pool_split, r + (PU0 - S0 + n + 1))
                if not first:
                    pe.wait_ge(gelu_done, r + (n - 1))
                three_pass(bank[n % 2], n % 2, lambda k: hTh[:, k], lambda k: hTl[:, k]).then_inc(up_done, 1)

            def gate_banks(c, n, first):
                for q in range(2):
                    i = 2 * n + q
                    pe.wait_ge(oh_made, c * 16 + (i + 1))
                    if not (first and i < 4):
                        pe.wait_ge(w_evac, c * 16 + (i - 3))
                    for k in range(4):
                        s = (4 * i + k) % 16
                        for e in range(2):
                            ins = pe.matmul(bank[4 + i % 4][:, k * P:(k + 1) * P], oh2[:, s], oh1[:, s, e],
                                            start=(e == 0), stop=(e == 1))
                    ins.then_inc(w_done, 1)

            for i in range(NT):
                if i == 0:
                    for n in range(4):
                        up_unit(n, first=n < 2)
                with pe.Fori(ROUTE * i + (4 if i == 0 else 0), ROUTE * (i + 1), 4) as r:
                    for n in range(4):
                        up_unit(n, r)
                if i:
                    picks_t(pe, i - 1)
            for n in range(4):
                up_unit(GATE0 + n)
            picks_t(pe, NT - 1)
            pe.wait_ge(selT_done, NT)
            for n in range(8):
                up_unit(GATE1 + n)
                gate_banks(0, n, True)
            with pe.Fori(1, (TAIL0 - GATE1) // 8) as c:
                for n in range(8):
                    up_unit(n, c * 8 + GATE1)
                    gate_banks(c, n, False)
            with pe.Fori(TAIL0, NUP, 4) as r:
                for n in range(4):
                    up_unit(n, r)

            def down_group(g, par, first):
                for m in range(GT):
                    pe.wait_ge(lo_done, g * GT + (S0 + m + 1))
                    if first and m < 2:
                        pe.wait_ge(sc_full, 4 * NT)
                    else:
                        pe.wait_ge(added, g * GT + (m - 1))
                    three_pass(bank[2 + m % 2], m % 2, lambda k: ach[:, par, k], lambda k: acl[:, par, k],
                               (lambda k: pe.wait_ge(act_ready, g * GT + (k + 1))) if m == 0 else None
                               ).then_inc(down_done, 1)

            down_group(0, 0, True)
            down_group(1, 1, False)
            with pe.Fori(2, NG, 2) as g:
                down_group(g, 0, False)
                down_group(g + 1, 1, False)


IN_NAMES = ("xT", "cT", "pos", "w_ada", "b_ada", "g1", "g2", "w_in", "w_small", "conv_w", "conv_b", "dt_bias",
            "a_log", "d_skip", "g_ssd", "q_g", "k_g", "w_ssd_br", "w_attn_br", "w_out", "w_peer_q", "subkeys", "U", "V")


def lay_out(inp):
    a = {k: np.asarray(v) for k, v in inp.items()}
    col = lambda v: np.ascontiguousarray(v.reshape(-1, P).T)
    w_in = a["w_in"][0]
    o = {
        "xT": a["x"][0].T, "cT": col(a["c"][0]), "pos": col(a["positions"][0]),
        "w_ada": a["w_ada"][0], "b_ada": col(a["b_ada"][0]), "g1": col(a["g_norm1"][0]), "g2": col(a["g_norm2"][0]),
        "w_in": w_in, "w_small": np.concatenate([w_in[:, C_DT:C_DT + SSD_H], w_in[:, C_KI:C_G]], axis=1),
        "conv_w": a["conv_w"][0].reshape(CONV_K, NX, P).transpose(2, 1, 0).reshape(P, NX * CONV_K),
        "conv_b": col(a["conv_b"][0]), "dt_bias": a["dt_bias"], "a_log": a["a_log"], "d_skip": a["d_skip"],
        "g_ssd": col(a["g_ssd"][0]), "q_g": a["q_norm_g"], "k_g": a["k_norm_g"],
        "w_ssd_br": a["w_ssd_br"][0], "w_attn_br": a["w_attn_br"][0], "w_out": a["w_out"][0],
        "w_peer_q": a["w_peer_q"][0],
        "subkeys": a["peer_subkeys"][0].transpose(1, 3, 0, 2).reshape(P, PH * NKEYS),
        "U": a["peer_u"][0].reshape(NKEYS, P, NK, P).transpose(0, 3, 2, 1).reshape(NKEYS, P, NK * P),
        "V": a["peer_v"][0].reshape(NG, GT, P, NK, P).transpose(0, 3, 2, 1, 4).reshape(NG * NK, P, GT * P),
    }
    return {k: np.ascontiguousarray(v) for k, v in o.items()}


def kernel(**inputs):
    import concourse.bacc as bacc
    from concourse.bass_utils import run_bass_kernel_spmd

    arrays = lay_out(inputs)
    nc = bacc.Bacc("TRN2", target_bir_lowering=False, num_devices=1)
    aps = {n: nc.dram_tensor(n, arrays[n].shape, mybir.dt.from_np(arrays[n].dtype), kind="ExternalInput").ap()
           for n in IN_NAMES}
    aps["out"] = nc.dram_tensor("out", (D, T), mybir.dt.float32, kind="ExternalOutput").ap()
    build(nc, aps)
    r = run_bass_kernel_spmd(nc, [arrays], core_ids=[0])
    return np.ascontiguousarray(r.results[0]["out"].T)[None]
```
